# Optimizing a Trainium2 kernel written in Bass

```python
import jax
import jax.numpy as jnp
from jax import lax
import numpy as np

D_MODEL = 1024
BATCH = 1
SEQ = 512
DEPTH = 1
DEC_BATCH = 8
DEC_SEQ = 4
PAST_LEN = 4096
PAGE_SIZE = 128

HEAD_DIM = 64
Q_BLOCK = 128
NSA_HEADS = 8
NSA_KV_GROUPS = 2
NSA_HPG = NSA_HEADS // NSA_KV_GROUPS
CMP_LEN = 32
CMP_STRIDE = 16
CMP_HIDDEN = 2 * HEAD_DIM
SLC_LEN = 64
SLC_TOPN = 16
SLC_Q_BLOCK = 64
NSA_WIN = 512
FORCE_BONUS = 1.0e4
RWKV_HEADS = 8
RWKV_W = RWKV_HEADS * HEAD_DIM
R_DECAY = 64
R_ICLR = 64
R_GATE = 128
SHIFT_W = 3 * RWKV_W + R_DECAY + R_ICLR + R_GATE
GN_EPS = 64e-5
DIL_CONFIGS = ((128, 1), (512, 4), (2048, 16))
DIL_HPG = 4
DIL_HEADS = DIL_HPG * len(DIL_CONFIGS)
DIL_W = DIL_HEADS * HEAD_DIM
FF_HIDDEN = -(-8 * D_MODEL // (3 * 256)) * 256
NSA_Q = NSA_HEADS * HEAD_DIM
NSA_KV = 2 * NSA_KV_GROUPS * HEAD_DIM
NSA_GATE = 3 * NSA_HEADS
IN_SPLITS = (NSA_Q, NSA_KV, NSA_KV, NSA_KV, NSA_GATE, SHIFT_W, DIL_W, DIL_W, DIL_W, 3 * D_MODEL)
IN_W = sum(IN_SPLITS)
DEEPNORM_ALPHA = (2 * DEPTH) ** 0.25
DEEPNORM_BETA = (8 * DEPTH) ** -0.25

kernel_name = 'hybrid_nsa_rwkv7_dilated_decoder_step'

def alibi_slopes(n):
    return jnp.asarray([2.0 ** (-8.0 * (i + 1) / n) for i in range(n)], dtype=jnp.float32)

def _split(z, sizes):
    return jnp.split(z, [int(i) for i in np.cumsum(sizes)[:-1]], axis=-1)

def _stack(states, name):
    return jnp.stack([s[name] for s in states], axis=0)

def pick_block(T, qb):
    return qb if T % qb == 0 else T

def layer_norm(x, g, b, eps=1e-5):
    xf = x.astype(jnp.float32)
    mu = xf.mean(-1, keepdims=True)
    var = jnp.square(xf - mu).mean(-1, keepdims=True)
    return ((xf - mu) * lax.rsqrt(var + eps) * g + b).astype(x.dtype)

def masked_softmax(s, mask):
    s = jnp.where(mask, s.astype(jnp.float32), -jnp.inf)
    m = jnp.max(s, axis=-1, keepdims=True)
    m = jnp.where(jnp.isfinite(m), m, 0.0)
    e = jnp.exp(s - m)
    den = jnp.sum(e, axis=-1, keepdims=True)
    p = e / jnp.where(den > 0.0, den, 1.0)
    lse = (m + jnp.log(den))[..., 0]
    return p, lse

def sweep_query_blocks(fn, T, qb):
    outs = lax.map(fn, jnp.arange(T // qb) * qb)
    def unblock(o):
        o = jnp.moveaxis(o, 0, 1)
        return o.reshape((o.shape[0], T) + o.shape[3:])
    return jax.tree_util.tree_map(unblock, outs)

def banded_attend(q, kv, n_prefix, window, slopes):
    B, T, G, n, dk = q.shape
    qb = pick_block(T, Q_BLOCK)
    span = qb + window
    kvp = jnp.pad(kv, ((0, 0), (0, 0), (0, 0), (window, 0), (0, 0)))
    rel = jnp.arange(qb)[:, None] - jnp.arange(span)[None, :] + window
    bias = slopes[None, :, :, None, None] * rel
    def block(q0):
        qblk = lax.dynamic_slice_in_dim(q, q0, qb, axis=1)
        slab = lax.dynamic_slice_in_dim(kvp, n_prefix + q0, span, axis=3)
        krow = n_prefix + q0 - window + jnp.arange(span)
        mask = (rel >= 0) & (rel <= window) & (krow >= 0)[None, :]
        s = jnp.einsum('bqgnd,bgkd->bgnqk', qblk, slab[:, 0]) * (dk ** -0.5) - bias
        p, _ = masked_softmax(s, mask)
        return jnp.einsum('bgnqk,bgkd->bqgnd', p.astype(kv.dtype), slab[:, 1])
    return sweep_query_blocks(block, T, qb)

def dilated_attend(q, kv, n_prefix, window, dil, slopes):
    B, T, H, dk = q.shape
    qb = pick_block(T, Q_BLOCK)
    offs = dil * jnp.arange(window // dil + 1)
    bias = slopes[None, :, None, None] * offs
    def block(q0):
        qblk = lax.dynamic_slice_in_dim(q, q0, qb, axis=1)
        krow = n_prefix + q0 + jnp.arange(qb)[:, None] - offs[None, :]
        kvg = jnp.take(kv, jnp.maximum(krow, 0), axis=3)
        s = jnp.einsum('bqhd,bhqkd->bhqk', qblk, kvg[:, 0]) * (dk ** -0.5) - bias
        p, lse = masked_softmax(s, krow >= 0)
        o = jnp.einsum('bhqk,bhqkd->bqhd', p.astype(kv.dtype), kvg[:, 1])
        return o, jnp.moveaxis(lse, 1, 2)
    return sweep_query_blocks(block, T, qb)

def compress_rows(rows, w1, pe, w2):
    B, G, L, dk = rows.shape
    hid = lax.conv_general_dilated(rows.reshape(B * G, L, dk), w1, (CMP_STRIDE,), 'VALID',
                                   dimension_numbers=('NWC', 'WIO', 'NWC'))
    hid = jax.nn.gelu(hid + jnp.einsum('ld,ldh->h', pe, w1))
    return (hid @ w2).reshape(B, G, -1, dk)

def nsa_cmp_slc(q, pos0, kc, vc, n_slc, gather_fn, slopes):
    B, T, G, n, dk = q.shape
    NC = kc.shape[2]
    qb = pick_block(T, SLC_Q_BLOCK)
    topn = min(SLC_TOPN, n_slc)
    scale = dk ** -0.5
    c_end = jnp.arange(NC) * CMP_STRIDE + (CMP_LEN - 1)
    j_idx = jnp.arange(n_slc)
    j_start = j_idx * SLC_LEN
    overlap = ((c_end[:, None] - (CMP_LEN - 1) < j_start[None, :] + SLC_LEN)
               & (c_end[:, None] >= j_start[None, :])).astype(jnp.float32)
    sl = slopes[None, :, :, None, None]
    def block(q0):
        qblk = lax.dynamic_slice_in_dim(q, q0, qb, axis=1)
        t = pos0 + q0 + jnp.arange(qb)
        dist_c = t[:, None] - c_end[None, :]
        s_c = jnp.einsum('bqgnd,bgcd->bgnqc', qblk, kc) * scale - sl * dist_c
        p_c, _ = masked_softmax(s_c, dist_c >= 0)
        o_c = jnp.einsum('bgnqc,bgcd->bqgnd', p_c.astype(vc.dtype), vc)
        imp = jnp.einsum('bgnqc,cj->bgqj', p_c, overlap)
        jt = (t // SLC_LEN)[:, None]
        forced = (j_idx == 0) | (j_idx == jt) | (j_idx == jt - 1)
        score = jnp.where(j_idx <= jt, imp + FORCE_BONUS * forced, -jnp.inf)
        top, idx = lax.top_k(score, topn)
        kv_sel = gather_fn(idx)
        dist_s = t[None, None, :, None, None] - (idx[..., None] * SLC_LEN + jnp.arange(SLC_LEN))
        mask = ((dist_s >= 0) & jnp.isfinite(top)[..., None]).reshape(B, G, 1, qb, topn * SLC_LEN)
        s_s = (jnp.einsum('bqgnd,bgqkld->bgnqkl', qblk, kv_sel[:, :, :, :, 0]) * scale
               - slopes[None, :, :, None, None, None] * dist_s[:, :, None])
        p_s, _ = masked_softmax(s_s.reshape(B, G, n, qb, topn * SLC_LEN), mask)
        v_sel = kv_sel[:, :, :, :, 1].reshape(B, G, qb, topn * SLC_LEN, dk)
        o_s = jnp.einsum('bgnqm,bgqmd->bqgnd', p_s.astype(v_sel.dtype), v_sel)
        return o_c, o_s
    return sweep_query_blocks(block, T, qb)

def paged_rows(pool, page_table):
    pages = pool[page_table]
    B, NP, two, G, PS, dk = pages.shape
    return pages.transpose(0, 2, 3, 1, 4, 5).reshape(B, two, G, NP * PS, dk)

def sample_block_gather(pool, page_table, kv_new):
    n_phys, _, G, PS, dk = pool.shape
    subs = PS // SLC_LEN
    n_past_blocks = page_table.shape[1] * subs
    poolb = pool.reshape(n_phys, 2, G, subs, SLC_LEN, dk).transpose(0, 2, 3, 1, 4, 5)
    B, T = kv_new.shape[0], kv_new.shape[3]
    nnb = -(-T // SLC_LEN)
    newb = jnp.pad(kv_new, ((0, 0), (0, 0), (0, 0), (0, nnb * SLC_LEN - T), (0, 0)))
    newb = newb.reshape(B, 2, G, nnb, SLC_LEN, dk).transpose(0, 2, 3, 1, 4, 5)
    bi = jnp.arange(B)[:, None, None, None]
    gi = jnp.arange(G)[None, :, None, None]
    def gather(idx):
        is_past = idx < n_past_blocks
        jp = jnp.minimum(idx, n_past_blocks - 1)
        phys = page_table[bi, jp // subs]
        from_past = poolb[phys, gi, jp % subs]
        from_new = newb[bi, gi, jnp.clip(idx - n_past_blocks, 0, nnb - 1)]
        return jnp.where(is_past[..., None, None, None], from_past, from_new)
    return gather, n_past_blocks + nnb

def rwkv7_mix(p, shift_prev, S0, lp):
    B, T, _ = p.shape
    prev = jnp.concatenate([shift_prev, p[:, :-1]], axis=1)
    xm = p + (prev - p) * lp['rw_mu']
    r, k, v, xw, xa, xg = _split(xm, (RWKV_W, RWKV_W, RWKV_W, R_DECAY, R_ICLR, R_GATE))
    w = -jax.nn.softplus(-(lp['rw_w0'] + jnp.tanh(xw) @ lp['rw_w2'])) - 0.5
    decay = jnp.exp(-jnp.exp(w.astype(jnp.float32)))
    a = jax.nn.sigmoid(lp['rw_a0'] + xa @ lp['rw_a2'])
    g = jax.nn.sigmoid(xg) @ lp['rw_g2']
    def heads(z):
        return z.astype(jnp.float32).reshape(B, T, RWKV_HEADS, HEAD_DIM)
    kk = heads(k * lp['rw_kk'])
    kk = kk / jnp.maximum(jnp.linalg.norm(kk, axis=-1, keepdims=True), 1e-12)
    k = k * (1.0 + (a - 1.0) * lp['rw_ka'])
    rh, kh, vh, ah, dh = heads(r), heads(k), heads(v), heads(a), heads(decay)
    def step(S, inp):
        r_t, d_t, k_t, v_t, kk_t, b_t = inp
        sa = jnp.einsum('bhij,bhj->bhi', S, -kk_t)
        S = S * d_t[:, :, None, :] + sa[..., None] * b_t[:, :, None, :] + v_t[..., None] * k_t[:, :, None, :]
        return S, jnp.einsum('bhij,bhj->bhi', S, r_t)
    xs = tuple(jnp.moveaxis(z, 1, 0) for z in (rh, dh, kh, vh, kk, kk * ah))
    S1, out = lax.scan(step, S0.astype(jnp.float32), xs)
    out = jnp.moveaxis(out, 0, 1)
    mu = out.mean(-1, keepdims=True)
    var = jnp.square(out - mu).mean(-1, keepdims=True)
    out = ((out - mu) * lax.rsqrt(var + GN_EPS)).reshape(B, T, RWKV_W) * lp['rw_gn_g'] + lp['rw_gn_b']
    bonus = (rh * kh * lp['rw_rk']).sum(-1, keepdims=True) * vh
    out = (out + bonus.reshape(B, T, RWKV_W)) * g
    return out.astype(p.dtype), S1.astype(S0.dtype), p[:, -1:]

def trunk_layer(x, c, lp, past):
    B, T, _ = x.shape
    G, HD = NSA_KV_GROUPS, HEAD_DIM
    mod = jax.nn.silu(c) @ lp['w_ada'] + lp['b_ada']
    sh_m, sc_m, g_m, sh_f, sc_f, g_f = jnp.split(mod[:, None, :], 6, axis=-1)
    h = x * (1.0 + sc_m) + sh_m
    q_a, kvc, kvs, kvw, g_a, p_b, q_c, k_c, v_c, g_mrg = _split(h @ lp['w_in'], IN_SPLITS)
    def as_kv(z, nh):
        return z.reshape(B, T, 2, nh, HD).transpose(0, 2, 3, 1, 4)
    kvc, kvs, kvw = as_kv(kvc, G), as_kv(kvs, G), as_kv(kvw, G)
    q_a = q_a.reshape(B, T, G, NSA_HPG, HD)
    slopes_a = alibi_slopes(NSA_HEADS).reshape(G, NSA_HPG)
    slopes_c = alibi_slopes(DIL_HEADS).reshape(len(DIL_CONFIGS), DIL_HPG)
    new = {'nsa_cmp': kvc, 'nsa_slc': kvs}
    if past is None:
        pos0, kvc_full, kvw_full, n_pref_w = 0, kvc, kvw, 0
        src = kvs.reshape(B, 2, G, T // SLC_LEN, SLC_LEN, HD).transpose(0, 2, 3, 1, 4, 5)
        bi = jnp.arange(B)[:, None, None, None]
        gi = jnp.arange(G)[None, :, None, None]
        def gather_fn(idx):
            return src[bi, gi, idx]
        n_slc = T // SLC_LEN
        new['nsa_win'] = kvw[:, :, :, -min(NSA_WIN, T):]
        shift0 = jnp.zeros((B, 1, SHIFT_W), p_b.dtype)
        S0 = jnp.zeros((B, RWKV_HEADS, HD, HD), jnp.float32)
    else:
        pos0 = PAST_LEN
        kvc_full = jnp.concatenate([paged_rows(past['nsa_cmp'], past['page_table']), kvc], axis=3)
        gather_fn, n_slc = sample_block_gather(past['nsa_slc'], past['page_table'], kvs)
        n_pref_w = past['nsa_win'].shape[3]
        kvw_full = jnp.concatenate([past['nsa_win'], kvw], axis=3)
        new['nsa_win'] = kvw_full[:, :, :, -n_pref_w:]
        shift0, S0 = past['rwkv_shift'], past['rwkv']
    kc = compress_rows(kvc_full[:, 0], lp['phi_w1'][0], lp['phi_pe'][0], lp['phi_w2'][0])
    vc = compress_rows(kvc_full[:, 1], lp['phi_w1'][1], lp['phi_pe'][1], lp['phi_w2'][1])
    o_cmp, o_slc = nsa_cmp_slc(q_a, pos0, kc, vc, n_slc, gather_fn, slopes_a)
    o_win = banded_attend(q_a, kvw_full, n_pref_w, NSA_WIN, slopes_a)
    gb = jax.nn.sigmoid(g_a.astype(jnp.float32)).reshape(B, T, G, NSA_HPG, 3)
    o_a = (gb[..., 0:1] * o_cmp + gb[..., 1:2] * o_slc + gb[..., 2:3] * o_win).reshape(B, T, NSA_Q)
    o_b, new['rwkv'], new['rwkv_shift'] = rwkv7_mix(p_b, shift0, S0, lp)
    q_c = q_c.reshape(B, T, DIL_HEADS, HD)
    k_c = k_c.reshape(B, T, DIL_HEADS, HD)
    v_c = v_c.reshape(B, T, DIL_HEADS, HD)
    outs, lses = [], []
    for gidx, (win, dil) in enumerate(DIL_CONFIGS):
        hs = slice(gidx * DIL_HPG, (gidx + 1) * DIL_HPG)
        kv_g = jnp.stack([k_c[:, :, hs], v_c[:, :, hs]], axis=1).transpose(0, 1, 3, 2, 4)
        if past is None:
            kv_full, n_pref = kv_g, 0
            new['dil%d' % gidx] = kv_g[:, :, :, -min(win, T):]
        else:
            buf = past['dil'][gidx]
            n_pref = buf.shape[3]
            kv_full = jnp.concatenate([buf, kv_g], axis=3)
            new['dil%d' % gidx] = kv_full[:, :, :, -n_pref:]
        o_g, lse_g = dilated_attend(q_c[:, :, hs], kv_full, n_pref, win, dil, slopes_c[gidx])
        outs.append(o_g)
        lses.append(lse_g)
    wd = jax.nn.softmax(jnp.stack(lses, axis=0), axis=0)
    o_c = jnp.einsum('gbth,gbthd->bthd', wd, jnp.stack(outs, axis=0)).reshape(B, T, DIL_HPG * HD)
    gm = jax.nn.sigmoid(g_mrg.astype(jnp.float32)).reshape(B, T, 3, D_MODEL)
    m = (gm[:, :, 0] * (o_a.astype(x.dtype) @ lp['w_br_a'])
         + gm[:, :, 1] * (o_b @ lp['w_br_b'])
         + gm[:, :, 2] * (o_c.astype(x.dtype) @ lp['w_br_c']))
    mix = m.astype(x.dtype) @ lp['w_o']
    x = layer_norm(DEEPNORM_ALPHA * x + g_m * mix, lp['ln1_g'], lp['ln1_b'])
    hf = x * (1.0 + sc_f) + sh_f
    f_gate, f_up = jnp.split(hf @ lp['w_ffn1'], 2, axis=-1)
    f = (jax.nn.silu(f_gate) * f_up) @ lp['w_ffn2']
    x = layer_norm(DEEPNORM_ALPHA * x + g_f * f, lp['ln2_g'], lp['ln2_b'])
    return x, new

def setup_inputs(seed: int = 0) -> dict:
    key = jax.random.key(seed)
    keys = iter(jax.random.split(key, 64))
    def nrm(shape, scale=1.0):
        return jax.random.normal(next(keys), shape, jnp.float32) * scale
    def unif(shape, lo, hi):
        return jax.random.uniform(next(keys), shape, jnp.float32, lo, hi)
    n_pages = PAST_LEN // PAGE_SIZE
    n_phys = (5 * DEC_BATCH * n_pages + 3) // 4
    perm = jax.random.permutation(next(keys), n_phys)
    page_table = perm[: DEC_BATCH * n_pages].reshape(DEC_BATCH, n_pages).astype(jnp.int32)
    L, G, HD, d = DEPTH, NSA_KV_GROUPS, HEAD_DIM, D_MODEL
    la = min(NSA_WIN, PAST_LEN)
    beta = DEEPNORM_BETA
    return {
        'x_prompt': nrm((BATCH, SEQ, d)),
        'x_sample': nrm((DEC_BATCH, DEC_SEQ, d)),
        'cache_nsa_cmp': nrm((L, n_phys, 2, G, PAGE_SIZE, HD)),
        'cache_nsa_slc': nrm((L, n_phys, 2, G, PAGE_SIZE, HD)),
        'cache_nsa_win': nrm((L, DEC_BATCH, 2, G, la, HD)),
        'state_rwkv': nrm((L, DEC_BATCH, RWKV_HEADS, HD, HD), 0.3),
        'state_rwkv_shift': nrm((L, DEC_BATCH, 1, SHIFT_W)),
        'cache_dil0': nrm((L, DEC_BATCH, 2, DIL_HPG, min(DIL_CONFIGS[0][0], PAST_LEN), HD)),
        'cache_dil1': nrm((L, DEC_BATCH, 2, DIL_HPG, min(DIL_CONFIGS[1][0], PAST_LEN), HD)),
        'cache_dil2': nrm((L, DEC_BATCH, 2, DIL_HPG, min(DIL_CONFIGS[2][0], PAST_LEN), HD)),
        'page_table': page_table,
        'c_prompt': nrm((BATCH, d)),
        'c_sample': nrm((DEC_BATCH, d)),
        'w_ada': nrm((L, d, 6 * d), 0.5 * d ** -0.5),
        'b_ada': nrm((L, 6 * d), 0.1),
        'w_in': nrm((L, d, IN_W), d ** -0.5),
        'phi_w1': nrm((L, 2, CMP_LEN, HD, CMP_HIDDEN), (CMP_LEN * HD) ** -0.5),
        'phi_pe': nrm((L, 2, CMP_LEN, HD), 0.5),
        'phi_w2': nrm((L, 2, CMP_HIDDEN, HD), CMP_HIDDEN ** -0.5),
        'rw_mu': unif((L, SHIFT_W), 0.0, 1.0),
        'rw_w0': unif((L, RWKV_W), -5.0, 0.5),
        'rw_w2': nrm((L, R_DECAY, RWKV_W), 0.1 * R_DECAY ** -0.5),
        'rw_a0': nrm((L, RWKV_W), 0.5),
        'rw_a2': nrm((L, R_ICLR, RWKV_W), 0.5 * R_ICLR ** -0.5),
        'rw_g2': nrm((L, R_GATE, RWKV_W), R_GATE ** -0.5),
        'rw_kk': 0.85 + nrm((L, RWKV_W), 0.05),
        'rw_ka': 1.0 + nrm((L, RWKV_W), 0.05),
        'rw_rk': nrm((L, RWKV_HEADS, HD), 0.1),
        'rw_gn_g': 1.0 + nrm((L, RWKV_W), 0.05),
        'rw_gn_b': nrm((L, RWKV_W), 0.05),
        'w_br_a': nrm((L, NSA_Q, d), beta * NSA_Q ** -0.5),
        'w_br_b': nrm((L, RWKV_W, d), beta * RWKV_W ** -0.5),
        'w_br_c': nrm((L, DIL_HPG * HD, d), beta * (DIL_HPG * HD) ** -0.5),
        'w_o': nrm((L, d, d), beta * d ** -0.5),
        'ln1_g': 1.0 + nrm((L, d), 0.05),
        'ln1_b': nrm((L, d), 0.05),
        'ln2_g': 1.0 + nrm((L, d), 0.05),
        'ln2_b': nrm((L, d), 0.05),
        'w_ffn1': nrm((L, d, 2 * FF_HIDDEN), d ** -0.5),
        'w_ffn2': nrm((L, FF_HIDDEN, d), beta * FF_HIDDEN ** -0.5),
    }

def reference(x_prompt, x_sample, cache_nsa_cmp, cache_nsa_slc, cache_nsa_win, state_rwkv, state_rwkv_shift,
              cache_dil0, cache_dil1, cache_dil2, page_table, c_prompt, c_sample, w_ada, b_ada, w_in,
              phi_w1, phi_pe, phi_w2, rw_mu, rw_w0, rw_w2, rw_a0, rw_a2, rw_g2, rw_kk, rw_ka, rw_rk,
              rw_gn_g, rw_gn_b, w_br_a, w_br_b, w_br_c, w_o, ln1_g, ln1_b, ln2_g, ln2_b, w_ffn1, w_ffn2):
    yp, ys = x_prompt, x_sample
    new_p, new_s = [], []
    for l in range(DEPTH):
        lp = {'w_ada': w_ada[l], 'b_ada': b_ada[l], 'w_in': w_in[l], 'phi_w1': phi_w1[l],
              'phi_pe': phi_pe[l], 'phi_w2': phi_w2[l], 'rw_mu': rw_mu[l], 'rw_w0': rw_w0[l],
              'rw_w2': rw_w2[l], 'rw_a0': rw_a0[l], 'rw_a2': rw_a2[l], 'rw_g2': rw_g2[l],
              'rw_kk': rw_kk[l], 'rw_ka': rw_ka[l], 'rw_rk': rw_rk[l], 'rw_gn_g': rw_gn_g[l],
              'rw_gn_b': rw_gn_b[l], 'w_br_a': w_br_a[l], 'w_br_b': w_br_b[l], 'w_br_c': w_br_c[l],
              'w_o': w_o[l], 'ln1_g': ln1_g[l], 'ln1_b': ln1_b[l], 'ln2_g': ln2_g[l], 'ln2_b': ln2_b[l],
              'w_ffn1': w_ffn1[l], 'w_ffn2': w_ffn2[l]}
        past = {'nsa_cmp': cache_nsa_cmp[l], 'nsa_slc': cache_nsa_slc[l], 'page_table': page_table,
                'nsa_win': cache_nsa_win[l], 'rwkv': state_rwkv[l], 'rwkv_shift': state_rwkv_shift[l],
                'dil': (cache_dil0[l], cache_dil1[l], cache_dil2[l])}
        yp, sp = trunk_layer(yp, c_prompt, lp, None)
        ys, ss = trunk_layer(ys, c_sample, lp, past)
        new_p.append(sp)
        new_s.append(ss)
    return (yp, ys,
            _stack(new_p, 'nsa_cmp'), _stack(new_s, 'nsa_cmp'),
            _stack(new_p, 'nsa_slc'), _stack(new_s, 'nsa_slc'),
            _stack(new_p, 'nsa_win'), _stack(new_s, 'nsa_win'),
            _stack(new_p, 'rwkv'), _stack(new_s, 'rwkv'),
            _stack(new_p, 'rwkv_shift'), _stack(new_s, 'rwkv_shift'),
            _stack(new_p, 'dil0'), _stack(new_s, 'dil0'),
            _stack(new_p, 'dil1'), _stack(new_s, 'dil1'),
            _stack(new_p, 'dil2'), _stack(new_s, 'dil2'))


_drawn_inputs = setup_inputs


def setup_inputs(seed=0):
    import zlib

    import numpy as np

    out = dict(_drawn_inputs(seed))
    spreads = {}
    factors = {'cache_nsa_cmp': 4.81,
     'cache_nsa_slc': 8.0,
     'phi_w1': 3.705,
     'phi_pe': 6.852,
     'phi_w2': 3.243,
     'rw_w2': 5.078,
     'rw_rk': 6.875,
     'rw_gn_g': 57.19,
     'rw_gn_b': 64.0,
     'w_br_c': 2.745}
    for name, (base, spread) in spreads.items():
        noise = np.random.default_rng([zlib.crc32(name.encode()), seed]).standard_normal(out[name].shape)
        drawn = base * np.exp(spread * noise) if base else spread * noise
        out[name] = jnp.asarray(drawn.astype(out[name].dtype))
    for name, factor in factors.items():
        out[name] = (out[name] * factor).astype(out[name].dtype)
    return out
```

```python
import math
from contextlib import ExitStack

import numpy as np

import concourse.bass as bass
from concourse import mybir

P = 128
D = 1024
KD = D // P
SEQ = 512
DB, DT = 8, 4
NS = DB * DT
NT = SEQ + NS
HN = NT // 2
HD = 64
PAST = 4096
PAGE = 128
NPAGE = PAST // PAGE
GRP = 2
HPG = 4
SHIFT_W = 1792
FF = 2816
ALPHA = 2.0 ** 0.25
GN_EPS = 64e-5
LN_EPS = 1e-5
BIG = 1e30
DIL = ((128, 1), (512, 4), (2048, 16))
NC_P = (SEQ - 32) // 16 + 1
NC_S = (PAST + DT - 32) // 16 + 1
NBLK = PAST // 64 + 1
TOPN = 16
MODT = 6 * KD

F32 = mybir.dt.float32
I32 = mybir.dt.int32
ALU = mybir.AluOpType
ACT = mybir.ActivationFunctionType
AX = mybir.AxisListType.X

SEGMENTS = [
    ("qa", 0, 512), ("kvc", 512, 256), ("kvs", 768, 256), ("kvw", 1024, 256), ("ga", 1280, 24),
    ("pb", 1304, 1792), ("qc", 3096, 768), ("kc", 3864, 768), ("vc", 4632, 768), ("gm", 5400, 3072),
]
TILE0 = {}
GROUPS = []
_t = 0
for _n, _c, _w in SEGMENTS:
    TILE0[_n] = _t
    for _o in range(0, _w, 512):
        GROUPS.append((_c + _o, min(512, _w - _o), _t + _o // P))
    _t += -(-_w // P)
NTILE = _t

TM_TILES = [TILE0["kvc"] + i for i in range(6)] + [TILE0["kc"] + i for i in range(12)]
TM_W = len(TM_TILES) * P
TM_COL = {"cmp": 0, "slc": 256, "win": 512, "kc": 768, "vc": 1536}

PROWS = [("rw_mu", 14), ("rw_w0", 4), ("rw_a0", 4), ("rw_kk", 4), ("rw_ka", 4), ("rw_rk", 4),
         ("rw_gn_g", 4), ("rw_gn_b", 4), ("ln1_g", 8), ("ln1_b", 8), ("ln2_g", 8), ("ln2_b", 8),
         ("b_ada", 48)]
PROW = {}
_r = 0
for _n, _c in PROWS:
    PROW[_n] = _r
    _r += _c
NPROW = _r


def slopes(n):
    return [2.0 ** (-8.0 * (i + 1) / n) for i in range(n)]


class Chain:

    def __init__(self, eng, sem):
        self.eng, self.sem, self.n = eng, sem, 0

    def __call__(self, ins):
        ins.then_inc(self.sem, 1)
        self.n += 1
        self.eng.wait_ge(self.sem, self.n)


def sem_maker(nc, ctx, phase):
    held = []

    def clear():
        nc.clear_and_free_semaphores(held)
        nc.all_engine_barrier()

    def make(name):
        held.append(nc.alloc_semaphore(f"{phase}_{name}"))
        return held[-1]

    ctx.callback(clear)
    return make


def sb_maker(nc, ctx, phase):
    return lambda name, shape, dt=F32: ctx.enter_context(nc.sbuf_tensor(f"{phase}_{name}", shape, dt))


def ps_maker(nc, ctx, phase):
    return lambda name, shape: ctx.enter_context(nc.psum_tensor(f"{phase}_{name}", shape, F32))


def conditioning(nc, a, m):
    NG = MODT * P // 512
    with ExitStack() as ctx:
        sem, sb, ps = (f(nc, ctx, "ada") for f in (sem_maker, sb_maker, ps_maker))
        xtok = sb("xtok", [P, 5, D])
        c9 = sb("c9", [1 + DB, D])
        prow = sb("prow", [NPROW, P])
        wada = sb("wada", [P, 3, KD, 512])
        cT = sb("cT", [P, KD, 1 + DB])
        psx = ps("psx", [P, 2, 512])
        psd = ps("psd", [P, KD, NS])
        psc = ps("psc", [P, 512])
        psm = ps("psm", [P, 2, 512])
        loaded = sem("loaded")
        w_in = [sem(f"w{i}") for i in range(3)]
        silu = sem("silu")
        xps, xev, cps, cev, mps, mev = (sem(s) for s in ("xps", "xev", "cps", "cev", "mps", "mev"))
        vch = sem("vch")
        w_r = a["w_ada"][0].rearrange("(k p) n -> p k n", p=P)
        with nc.Block() as block:

            @block.sync
            def _(sp):
                sp.dma_start(m["ident"][:, :], a["c_ident"]).then_inc(loaded, 16)
                sp.dma_start(m["headones"][:, :], a["c_headones"]).then_inc(loaded, 16)
                sp.dma_start(m["reset"][:, :], a["c_reset"]).then_inc(loaded, 16)
                sp.dma_start(c9[0:1, :], a["c_prompt"]).then_inc(loaded, 16)
                sp.dma_start(c9[1:1 + DB, :], a["c_sample"]).then_inc(loaded, 16)
                sp.dma_start(xtok[:, 0:4, :], a["x_prompt"][0].rearrange("(t p) d -> p t d", p=P)).then_inc(loaded, 16)
                sp.dma_start(xtok[0:NS, 4, :], a["x_sample"].rearrange("b t d -> (b t) d")).then_inc(loaded, 16)
                for name, rows in PROWS:
                    v = a[name][0]
                    if name == "rw_rk":
                        v = v.rearrange("h d -> (h d)")
                    sp.dma_start(prow[PROW[name]:PROW[name] + rows, :],
                                 v.rearrange("(r c) -> r c", c=P)).then_inc(loaded, 16)
                for g in range(NG):
                    if g >= 3:
                        sp.wait_ge(mps, g - 2)
                    sp.dma_start(wada[:, g % 3, :, :], w_r[:, :, g * 512:(g + 1) * 512]).then_inc(w_in[g % 3], 16)

            NLOAD = 16 * (7 + len(PROWS))

            @block.scalar
            def _(act):
                act.wait_ge(loaded, NLOAD)
                nc.scalar.activation(c9[:, :], c9[:, :], ACT.Silu).then_inc(silu, 1)

            @block.tensor
            def _(pe):
                pe.wait_ge(loaded, NLOAD)
                pe.wait_ge(silu, 1)
                pe.transpose(psc[:, 0:NPROW], prow[:, :], m["ident"][0:NPROW, 0:NPROW])
                for k in range(KD):
                    i = pe.transpose(psc[:, P + k * 9:P + k * 9 + 9], c9[:, k * P:(k + 1) * P], m["ident"][0:9, 0:9])
                i.then_inc(cps, 1)
                for k in range(KD):
                    i = pe.transpose(psd[:, k, :], xtok[0:NS, 4, k * P:(k + 1) * P], m["ident"][0:NS, 0:NS])
                i.then_inc(cps, 1)
                for k in range(KD):
                    if k >= 2:
                        pe.wait_ge(xev, k - 1)
                    for t in range(4):
                        i = pe.transpose(psx[:, k % 2, t * P:(t + 1) * P], xtok[:, t, k * P:(k + 1) * P], m["ident"][:, :])
                    i.then_inc(xps, 1)
                pe.wait_ge(cev, 2)
                for g in range(NG):
                    pe.wait_ge(w_in[g % 3], 16 * (g // 3 + 1))
                    if g >= 2:
                        pe.wait_ge(mev, g - 1)
                    for j in range(4):
                        for k in range(KD):
                            i = pe.matmul(psm[:, g % 2, j * 9:j * 9 + 9], wada[:, g % 3, k, j * P:(j + 1) * P],
                                          cT[:, k, :], start=(k == 0), stop=(k == KD - 1))
                    i.then_inc(mps, 1)

            @block.vector
            def _(dve):
                chain = Chain(dve, vch)
                dve.wait_ge(cps, 1)
                dve.tensor_copy(m["prm"][:, :], psc[:, 0:NPROW]).then_inc(cev, 1)
                dve.tensor_copy(cT[:, :, :], psc[:, P:P + 72].rearrange("p (k c) -> p k c", k=KD)).then_inc(cev, 1)
                dve.wait_ge(cps, 2)
                chain(dve.tensor_copy(m["xT"][:, :, SEQ:NT], psd[:, :, :]))
                for k in range(KD):
                    dve.wait_ge(xps, k + 1)
                    dve.tensor_copy(m["xT"][:, k, 0:SEQ], psx[:, k % 2, :]).then_inc(xev, 1)
                dve.wait_ge(cev, 2)
                for g in range(NG):
                    dve.wait_ge(mps, g + 1)
                    dve.tensor_tensor(m["modT"][:, 4 * g:4 * g + 4, :],
                                      psm[:, g % 2, 0:36].rearrange("p (j c) -> p j c", j=4),
                                      m["prm"][:, PROW["b_ada"] + 4 * g:PROW["b_ada"] + 4 * g + 4]
                                      .unsqueeze(2).to_broadcast([P, 4, 9]), ALU.add).then_inc(mev, 1)
                dve.wait_ge(mev, NG)
                for s in (KD, 4 * KD):
                    chain(dve.tensor_scalar(m["modT"][:, s:s + KD, :], m["modT"][:, s:s + KD, :], 1.0, None, ALU.add))
                dve.wait_ge(xev, KD)
                modulate(dve, chain, m["hT"], m["xT"], m["modT"], 0, KD)


def modulate(dve, chain, out, x, modT, shift, scale):
    for k in range(KD):
        dve.tensor_scalar(out[:, k, 0:SEQ], x[:, k, 0:SEQ], modT[:, scale + k, 0:1], modT[:, shift + k, 0:1],
                          ALU.mult, ALU.add).then_inc(chain.sem, 1)
        chain.n += 1
    xs = x[:, :, SEQ:NT].rearrange("p k (b t) -> p k b t", t=DT)
    os = out[:, :, SEQ:NT].rearrange("p k (b t) -> p k b t", t=DT)
    chain(dve.tensor_tensor(os, xs, modT[:, scale:scale + KD, 1:9].unsqueeze(3).to_broadcast([P, KD, DB, DT]), ALU.mult))
    chain(dve.tensor_tensor(os, os, modT[:, shift:shift + KD, 1:9].unsqueeze(3).to_broadcast([P, KD, DB, DT]), ALU.add))


def in_projection(nc, a, m):
    NW = 3
    tiles = [(g, j, t0 + j, min(P, w - j * P)) for g, (_, w, t0) in enumerate(GROUPS) for j in range(-(-w // P))]
    with ExitStack() as ctx:
        sem, sb, ps = (f(nc, ctx, "inp") for f in (sem_maker, sb_maker, ps_maker))
        w = sb("w", [P, NW, KD, 512])
        o = sb("o", [P, 4, NT])
        acc = ps("acc", [P, 4, 2, 512])
        wl = [sem(f"w{i}") for i in range(NW)]
        done, evac, stored = sem("done"), sem("evac"), [sem(f"st{i}") for i in range(4)]
        groups_done = sem("gdone")
        last = {g: n for n, (g, *_) in enumerate(tiles)}
        w_r = a["w_in"][0].rearrange("(k p) n -> p k n", p=P)
        with nc.Block() as block:

            @block.sync
            def _(sp):
                for g, (c, n, _) in enumerate(GROUPS):
                    if g >= NW:
                        sp.wait_ge(done, last[g - NW] + 1)
                    sp.dma_start(w[:, g % NW, :, 0:n], w_r[:, :, c:c + n]).then_inc(wl[g % NW], 16)

            @block.tensor
            def _(pe):
                for n, (g, j, t, rows) in enumerate(tiles):
                    if j == 0:
                        pe.wait_ge(wl[g % NW], 16 * (g // NW + 1))
                    if n >= 4:
                        pe.wait_ge(evac, n - 3)
                    for k in range(KD):
                        for h in range(2):
                            i = pe.matmul(acc[0:rows, n % 4, h, 0:HN], w[:, g % NW, k, j * P:j * P + rows],
                                          m["hT"][:, k, h * HN:(h + 1) * HN], start=(k == 0), stop=(k == KD - 1))
                    i.then_inc(done, 1)

            @block.vector
            def _(dve):
                for n, (g, j, t, rows) in enumerate(tiles):
                    dve.wait_ge(done, n + 1)
                    if n >= 4:
                        dve.wait_ge(stored[n % 4], 16 * (n // 4))
                    dve.tensor_copy(o[0:rows, n % 4, :].rearrange("p (h c) -> p h c", h=2),
                                    acc[0:rows, n % 4, :, 0:HN]).then_inc(evac, 1)

            @block.gpsimd
            def _(pool):
                shift_caches(pool, a, m["copied"])

            @block.scalar
            def _(act):
                for n, (g, j, t, rows) in enumerate(tiles):
                    act.wait_ge(evac, n + 1)
                    act.dma_start(a["PT"][t * P:t * P + rows, :], o[0:rows, n % 4, :]).then_inc(stored[n % 4], 16)
                for s in range(4):
                    act.wait_ge(stored[s], 16 * len(range(s, len(tiles), 4)))


def token_major(nc, a, m):
    fgroups = [(i, min(4, len(TM_TILES) - i)) for i in range(0, len(TM_TILES), 4)]
    work = [(t, i, n) for t in range(5) for i, n in fgroups]
    with ExitStack() as ctx:
        sem, sb, ps = (f(nc, ctx, "tok") for f in (sem_maker, sb_maker, ps_maker))
        ft = sb("ft", [P, len(TM_TILES), NT])
        pt = sb("pt", [P, 14, NS + 1])
        gt = sb("gt", [24, NT])
        tok = sb("tok", [P, 5, TM_W])
        pbs = sb("pbs", [NS + 1, SHIFT_W])
        gate = sb("gate", [P, 5, 24])
        tp = ps("tp", [P, 4, 512])
        pp = ps("pp", [P, 4, 512])
        loaded, turned, kept, pturned, pkept, sig = (
            sem(s) for s in ("loaded", "turned", "kept", "pturned", "pkept", "sig"))
        out = m["token_rows_out"]
        rows = lambda t: P if t < 4 else NS
        with nc.Block() as block:

            @block.sync
            def _(sp):
                for i, t in enumerate(TM_TILES):
                    sp.dma_start(ft[:, i, :], a["PT"][t * P:(t + 1) * P, :]).then_inc(loaded, 16)
                t = TILE0["pb"] * P
                sp.dma_start(pt[:, :, :], a["PT"][t:t + SHIFT_W, SEQ - 1:NT].rearrange("(n p) t -> p n t", p=P)).then_inc(loaded, 16)
                t = TILE0["ga"] * P
                sp.dma_start(gt[:, :], a["PT"][t:t + 24, :]).then_inc(loaded, 16)

            @block.tensor
            def _(pe):
                pe.wait_ge(loaded, 16 * (len(TM_TILES) + 2))
                for t in range(5):
                    i = pe.transpose(pp[0:rows(t), 0, t * 32:t * 32 + 24], gt[:, t * P:t * P + rows(t)], m["ident"][0:24, 0:24])
                i.then_inc(pturned, 1)
                for n in range(14):
                    if n % 4 == 0 and n == 12:
                        pe.wait_ge(pkept, 1)
                    i = pe.transpose(pp[0:NS + 1, (n // 4 + 1) % 4, (n % 4) * P:(n % 4 + 1) * P], pt[:, n, :], m["ident"][:, :])
                    if n % 4 == 3 or n == 13:
                        i.then_inc(pturned, 1)
                for w, (t, i0, n) in enumerate(work):
                    if w >= 4:
                        pe.wait_ge(kept, w - 3)
                    for j in range(n):
                        i = pe.transpose(tp[0:rows(t), w % 4, j * P:(j + 1) * P], ft[:, i0 + j, t * P:t * P + rows(t)], m["ident"][:, :])
                    i.then_inc(turned, 1)

            @block.vector
            def _(dve):
                dve.wait_ge(pturned, 1)
                dve.tensor_copy(gate[:, 0:4, :], pp[:, 0, 0:P].rearrange("p (t c) -> p t c", t=4)[:, :, 0:24])
                dve.tensor_copy(gate[0:NS, 4, :], pp[0:NS, 0, P:P + 24]).then_inc(pkept, 1)
                for g in range(4):
                    n = min(512, SHIFT_W - g * 512)
                    dve.wait_ge(pturned, g + 2)
                    dve.tensor_copy(pbs[:, g * 512:g * 512 + n], pp[0:NS + 1, (g + 1) % 4, 0:n]).then_inc(pkept, 1)
                for w, (t, i0, n) in enumerate(work):
                    dve.wait_ge(turned, w + 1)
                    dve.tensor_copy(tok[0:rows(t), t, i0 * P:(i0 + n) * P], tp[0:rows(t), w % 4, 0:n * P]).then_inc(kept, 1)

            @block.scalar
            def _(act):
                act.wait_ge(pkept, 1)
                nc.scalar.activation(m["gateP"][:, :, :], gate[:, 0:4, :], ACT.Sigmoid).then_inc(sig, 1)
                nc.scalar.activation(gate[0:NS, 4, :], gate[0:NS, 4, :], ACT.Sigmoid).then_inc(sig, 1)
                act.wait_ge(sig, 2)
                act.dma_start(a["GA"][SEQ:NT, :], gate[0:NS, 4, :]).then_inc(out, 16)
                act.wait_ge(pkept, 5)
                act.dma_start(a["PBS"], pbs[:, :]).then_inc(out, 16)
                act.dma_start(a["o_shift_p"][0, 0], pbs[0:1, :]).then_inc(out, 16)
                for b in range(DB):
                    r = 1 + b * DT + DT - 1
                    act.dma_start(a["o_shift_s"][0, b], pbs[r:r + 1, :]).then_inc(out, 16)
                n_out = 3 + DB
                act.wait_ge(kept, len(work))
                for t in range(5):
                    act.dma_start(a["TM"][t * P:t * P + rows(t), :], tok[0:rows(t), t, :]).then_inc(out, 16)
                n_out += 5
                for name, col in (("cmp", 0), ("slc", 256), ("win", 512)):
                    for t in range(4):
                        act.dma_start(a[f"o_{name}_p"][0, 0].rearrange("v g t d -> t (v g) d")[t * P:(t + 1) * P],
                                      tok[:, t, col:col + 256].rearrange("p (c d) -> p c d", d=HD)).then_inc(out, 16)
                n_out += 12
                for g, (win, _) in enumerate(DIL):
                    first = 4 - min(win, SEQ) // P
                    for v in range(2):
                        col = TM_COL["kc" if v == 0 else "vc"] + g * 256
                        for t in range(first, 4):
                            act.dma_start(a[f"o_dil{g}_p"][0, 0, v].rearrange("h t d -> t h d")[(t - first) * P:(t - first + 1) * P],
                                          tok[:, t, col:col + 256].rearrange("p (c d) -> p c d", d=HD)).then_inc(out, 16)
                            n_out += 1
                for b in range(DB):
                    s = slice(b * DT, (b + 1) * DT)
                    for name, col in (("cmp", 0), ("slc", 256), ("win", 512)):
                        o = a[f"o_{name}_s"][0, b]
                        w = o.shape[2]
                        act.dma_start(o.rearrange("v g t d -> t (v g) d")[w - DT:w],
                                      tok[s, 4, col:col + 256].rearrange("p (c d) -> p c d", d=HD)).then_inc(out, 16)
                        n_out += 1
                    for g, (win, _) in enumerate(DIL):
                        for v in range(2):
                            col = TM_COL["kc" if v == 0 else "vc"] + g * 256
                            act.dma_start(a[f"o_dil{g}_s"][0, b, v].rearrange("h t d -> t h d")[win - DT:win],
                                          tok[s, 4, col:col + 256].rearrange("p (c d) -> p c d", d=HD)).then_inc(out, 16)
                            n_out += 1
                act.wait_ge(out, 16 * n_out)


def shift_caches(pool, a, copied):
    n = 0
    for name, w, heads, cut in (("win", 512, 4, 4), ("dil0", 128, 8, 1), ("dil1", 512, 8, 4), ("dil2", 2048, 8, 28)):
        src = a["cache_nsa_win" if name == "win" else f"cache_{name}"][0].rearrange("b v h t d -> (b v h) (t d)")
        dst = a[f"o_{name}_s"][0].rearrange("b v h t d -> (b v h) (t d)")
        src, dst = src[:, DT * HD:], dst[:, 0:(w - DT) * HD]
        pool.dma_start(dst.rearrange("r (c n) -> r c n", c=cut), src.rearrange("r (c n) -> r c n", c=cut)).then_inc(copied, 16)
        n += 1
    return n


def head_sums(pe, out, ones, x, ready=None):
    for h in range(2):
        i = pe.matmul(out[:, h, 0:HN], ones, x[:, h * HN:(h + 1) * HN], start=True, stop=True)
    return i


def halves(ap):
    return ap.rearrange("p (h c) -> p h c", h=2)


CH = 64
NCH = SEQ // CH
HALF_LIFE = math.exp(-0.5)


def rwkv(nc, a, m):
    with ExitStack() as ctx:
        sem, sb, ps = (f(nc, ctx, "rw") for f in (sem_maker, sb_maker, ps_maker))
        pb = sb("pb", [P, 14, NT])
        xm = sb("xm", [P, 14, NT])
        cum = sb("cum", [P, 4, SEQ])
        masks = sb("masks", [P, 9, P])
        gam = sb("gam", [P, 4, NCH])
        kk, kp, bb = pb[:, 0:4], pb[:, 4:8], pb[:, 8:12]
        r, k, v = xm[:, 0:4], xm[:, 4:8], xm[:, 8:12]
        gate, bonus = m["hT"][:, 0:4], m["hT"][:, 4:8]
        rwkv_elementwise(nc, a, m, pb, xm, cum, masks, gam, kk, kp, bb, r, k, v, gate, bonus)
        rwkv_sample(nc, a, m)
        rwkv_chunks(nc, a, m, kk, kp, bb, r, k, v, cum, masks, gam)
        rwkv_norm(nc, a, m, gate, bonus)


def rwkv_elementwise(nc, a, m, pb, xm, cum, masks, gam, kk, kp, bb, r, k, v, gate, bonus):
    prm = m["prm"]
    with ExitStack() as ctx:
        sem, sb, ps = (f(nc, ctx, "rwe") for f in (sem_maker, sb_maker, ps_maker))
        ld = sb("ld", [P, 4, NT])
        av = sb("av", [P, 4, NT])
        tmp = sb("tmp", [P, 4, NT])
        shs = sb("shs", [DB, SHIFT_W])
        shT = sb("shT", [P, 14, DB])
        w2 = sb("w2", [P, 512])
        g2 = sb("g2", [P, 512])
        omka = sb("omka", [P, 4])
        dq = sb("dq", [NS, 6, 512])
        acc = ps("acc", [P, 4, 2, 512])
        loaded, sht, ch, ach, z_in, z, zout, sqr, kkn, kkn2, bin_, bsum, exps, dqt, dqc, stored, cums, cumd, vdone, xmd = (sem(s) for s in (
            "loaded", "sht", "ch", "ach", "z_in", "z", "zout", "sqr", "kkn", "kkn2", "bin", "bsum", "exps", "dqt", "dqc", "stored", "cums", "cumd", "vdone", "xmd"))
        with nc.Block() as block:

            @block.sync
            def _(sp):
                t = TILE0["pb"] * P
                sp.dma_start(pb[:, :, :], a["PT"][t:t + SHIFT_W, :].rearrange("(n p) t -> p n t", p=P)).then_inc(loaded, 16)
                sp.dma_start(shs[:, :], a["state_rwkv_shift"][0].rearrange("b o w -> (b o) w")).then_inc(loaded, 16)
                sp.dma_start(w2[0:64, :], a["rw_w2"][0]).then_inc(loaded, 16)
                sp.dma_start(w2[64:128, :], a["rw_a2"][0]).then_inc(loaded, 16)
                sp.dma_start(g2[:, :], a["rw_g2"][0]).then_inc(loaded, 16)
                sp.dma_start(masks[:, :, :], a["c_masks"].rearrange("l p q -> p l q")).then_inc(loaded, 16)
                sp.wait_ge(dqc, 6)
                sp.dma_start(a["DQ"], dq[:, :, :]).then_inc(stored, 16)
                sp.wait_ge(stored, 16)

            @block.tensor
            def _(pe):
                pe.wait_ge(loaded, 96)
                for n in range(14):
                    i = pe.transpose(acc[:, 3, 1, n * DB:(n + 1) * DB], shs[:, n * P:(n + 1) * P], m["ident"][0:DB, 0:DB])
                i.then_inc(sht, 1)
                pe.wait_ge(z_in, 2)
                for n in range(12):
                    which, t = n // 4, n % 4
                    lhs = (w2[0:64], w2[64:128], g2)[which][:, t * P:(t + 1) * P]
                    rhs = (xm[0:64, 12], xm[64:128, 12], xm[:, 13])[which]
                    if n >= 4:
                        pe.wait_ge(zout, n - 3)
                    for h in range(2):
                        i = pe.matmul(acc[:, n % 4, h, 0:HN], lhs, rhs[:, h * HN:(h + 1) * HN], start=True, stop=True)
                    i.then_inc(z, 1)
                pe.wait_ge(zout, 12)
                for t in range(4):
                    pe.wait_ge(kkn, t + 1)
                    head_sums(pe, acc[:, t], m["headones"][:, :], tmp[:, t]).then_inc(sqr, 1)
                for t in range(4):
                    pe.wait_ge(bin_, t + 1)
                    head_sums(pe, acc[:, t], m["headones"][:, :], tmp[:, t]).then_inc(bsum, 1)
                pe.wait_ge(vdone, 1)
                for q, src in enumerate((r, ld, kp, v, kk, bb)):
                    if q >= 2:
                        pe.wait_ge(dqc, q - 1)
                    for t in range(4):
                        i = pe.transpose(acc[0:NS, q % 2, 0, t * P:(t + 1) * P], src[:, t, SEQ:NT], m["ident"][:, :])
                    i.then_inc(dqt, 1)

            @block.scalar
            def _(act):
                act.wait_ge(xmd, 1)
                nc.scalar.activation(xm[0:64, 12, :], xm[0:64, 12, :], ACT.Tanh).then_inc(z_in, 1)
                nc.scalar.activation(xm[:, 13, :], xm[:, 13, :], ACT.Sigmoid).then_inc(z_in, 1)
                for n in range(12):
                    which, t = n // 4, n % 4
                    act.wait_ge(z, n + 1)
                    src = acc[:, n % 4, :, 0:HN]
                    if which == 0:
                        i = nc.scalar.activation(halves(ld[:, t]), src, ACT.Sigmoid, bias=prm[:, PROW["rw_w0"] + t:PROW["rw_w0"] + t + 1])
                    elif which == 1:
                        i = nc.scalar.activation(halves(av[:, t]), src, ACT.Sigmoid, bias=prm[:, PROW["rw_a0"] + t:PROW["rw_a0"] + t + 1])
                    else:
                        i = nc.scalar.activation(halves(gate[:, t]), src, ACT.Copy)
                    i.then_inc(zout, 1)
                for t in range(4):
                    act.wait_ge(sqr, t + 1)
                    nc.scalar.activation(halves(tmp[:, t]), acc[:, t, :, 0:HN], ACT.Sqrt).then_inc(kkn2, 1)
                act.wait_ge(cumd, 1)
                nc.scalar.activation(av[:, :, 0:SEQ], cum[:, :, :], ACT.Exp).then_inc(exps, 1)
                nc.scalar.activation(gam[:, :, :], cum[:, :, CH - 1:SEQ:CH], ACT.Exp).then_inc(exps, 1)
                nc.scalar.activation(tmp[:, :, 0:SEQ], tmp[:, :, 0:SEQ], ACT.Exp).then_inc(exps, 1)
                act.wait_ge(exps, 3)
                nc.scalar.activation(cum[:, :, :], cum[:, :, :], ACT.Exp, scale=-1.0).then_inc(exps, 1)
                nc.scalar.activation(ld[:, :, SEQ:NT], ld[:, :, SEQ:NT], ACT.Exp).then_inc(exps, 1)

            @block.vector
            def _(dve):
                c = Chain(dve, ch)
                dve.wait_ge(loaded, 96)
                dve.wait_ge(sht, 1)
                c(dve.tensor_copy(shT[:, :, :], acc[:, 3, 1, 0:14 * DB].rearrange("p (n b) -> p n b", b=DB)))
                c(dve.tensor_scalar(omka[:, :], prm[:, PROW["rw_ka"]:PROW["rw_ka"] + 4], -1.0, 1.0, ALU.mult, ALU.add))
                pbs = pb[:, :, SEQ:NT].rearrange("p n (b t) -> p n b t", t=DT)
                xms = xm[:, :, SEQ:NT].rearrange("p n (b t) -> p n b t", t=DT)
                c(dve.tensor_tensor(xm[:, :, 1:SEQ], pb[:, :, 0:SEQ - 1], pb[:, :, 1:SEQ], ALU.subtract))
                c(dve.tensor_scalar(xm[:, :, 0:1], pb[:, :, 0:1], -1.0, None, ALU.mult))
                c(dve.tensor_tensor(xms[:, :, :, 1:DT], pbs[:, :, :, 0:DT - 1], pbs[:, :, :, 1:DT], ALU.subtract))
                c(dve.tensor_tensor(xms[:, :, :, 0], shT[:, :, :], pbs[:, :, :, 0], ALU.subtract))
                for n in range(14):
                    i = dve.scalar_tensor_tensor(xm[:, n], xm[:, n], prm[:, PROW["rw_mu"] + n:PROW["rw_mu"] + n + 1],
                                                 pb[:, n], ALU.mult, ALU.add)
                    c(i)
                c(dve.memset(gam[:, 0, 0:1], 0.0))
                dve.tensor_copy(omka[:, :], omka[:, :]).then_inc(xmd, 1)
                for t in range(4):
                    c(dve.tensor_scalar(kk[:, t], k[:, t], prm[:, PROW["rw_kk"] + t:PROW["rw_kk"] + t + 1], None, ALU.mult))
                    dve.tensor_tensor(tmp[:, t], kk[:, t], kk[:, t], ALU.mult).then_inc(kkn, 1)
                dve.wait_ge(kkn2, 4)
                c(dve.tensor_scalar(tmp[:, :, :], tmp[:, :, :], 1e-12, None, ALU.max))
                c(dve.reciprocal(tmp[:, :, :], tmp[:, :, :]))
                c(dve.tensor_tensor(kk, kk, tmp[:, :, :], ALU.mult))
                dve.wait_ge(zout, 12)
                for t in range(4):
                    c(dve.tensor_scalar(kp[:, t], av[:, t], prm[:, PROW["rw_ka"] + t:PROW["rw_ka"] + t + 1], omka[:, t:t + 1], ALU.mult, ALU.add))
                c(dve.tensor_tensor(kp, kp, k, ALU.mult))
                c(dve.tensor_tensor(bb, kk, av[:, :, :], ALU.mult))
                for t in range(4):
                    dve.scalar_tensor_tensor(tmp[:, t], r[:, t], prm[:, PROW["rw_rk"] + t:PROW["rw_rk"] + t + 1], kp[:, t],
                                             ALU.mult, ALU.mult).then_inc(bin_, 1)
                for t in range(4):
                    dve.wait_ge(bsum, t + 1)
                    c(dve.tensor_tensor(halves(bonus[:, t]), acc[:, t, :, 0:HN], halves(v[:, t]), ALU.mult))
                c(dve.tensor_scalar(ld[:, :, :], ld[:, :, :], -HALF_LIFE, None, ALU.mult))
                for t in range(4):
                    c(dve.tensor_tensor_scan(cum[:, t, :], m["reset"][:, :], ld[:, t, 0:SEQ], 0.0, ALU.mult, ALU.add))
                c(dve.tensor_tensor(tmp[:, :, 0:SEQ], cum[:, :, :], ld[:, :, 0:SEQ], ALU.subtract))
                dve.tensor_copy(omka[:, :], omka[:, :]).then_inc(cumd, 1)
                dve.wait_ge(exps, 5)
                c(dve.tensor_tensor(r[:, :, 0:SEQ], r[:, :, 0:SEQ], av[:, :, 0:SEQ], ALU.mult))
                c(dve.tensor_tensor(kk[:, :, 0:SEQ], kk[:, :, 0:SEQ], tmp[:, :, 0:SEQ], ALU.mult))
                c(dve.tensor_tensor(bb[:, :, 0:SEQ], bb[:, :, 0:SEQ], cum[:, :, :], ALU.mult))
                c(dve.tensor_tensor(kp[:, :, 0:SEQ], kp[:, :, 0:SEQ], cum[:, :, :], ALU.mult))
                dve.tensor_copy(omka[:, :], omka[:, :]).then_inc(vdone, 1)
                for q in range(6):
                    dve.wait_ge(dqt, q + 1)
                    dve.tensor_copy(dq[:, q, :], acc[0:NS, q % 2, 0, :]).then_inc(dqc, 1)


def rwkv_sample(nc, a, m):
    HR = HD // 2
    with ExitStack() as ctx:
        sem, sb, ps = (f(nc, ctx, "rws") for f in (sem_maker, sb_maker, ps_maker))
        S = sb("S", [P, HR, HD])
        tmp = sb("tmp", [P, HR, HD])
        q = sb("q", [P, DT * 6, HD])
        vs = sb("vs", [P, DT, HR])
        sa = sb("sa", [P, HR])
        o = sb("o", [P, DT, HR])
        ot = sb("ot", [NS, 512])
        pt = ps("pt", [P, 4, NS])
        loaded, ch, done, back, turned = (sem(s) for s in ("loaded", "ch", "done", "back", "turned"))
        out = m["sample_state_out"]
        DQ = a["DQ"]
        with nc.Block() as block:

            @block.sync
            def _(sp):
                st = a["state_rwkv"][0].rearrange("b h i j -> (b h) i j")
                n = 0
                for ih in range(2):
                    sp.dma_start(S[ih * 64:ih * 64 + 64], st[:, ih * HR:(ih + 1) * HR, :]).then_inc(loaded, 16)
                    n += 1
                    for b in range(DB):
                        p0 = ih * 64 + b * 8
                        rows = DQ[b * DT:(b + 1) * DT]
                        sp.dma_start(q[p0:p0 + 8], rows.rearrange("t q (h d) -> h (t q) d", h=8)).then_inc(loaded, 16)
                        sp.dma_start(vs[p0:p0 + 8], rows[:, 3, :].rearrange("t (h d) -> h t d", h=8)[:, :, ih * HR:(ih + 1) * HR]).then_inc(loaded, 16)
                        n += 2
                sp.wait_ge(done, 1)
                so = a["o_rwkv_s"][0].rearrange("b h i j -> (b h) i j")
                for ih in range(2):
                    sp.dma_start(so[:, ih * HR:(ih + 1) * HR, :], S[ih * 64:ih * 64 + 64]).then_inc(out, 16)
                    for b in range(DB):
                        p0 = ih * 64 + b * 8
                        sp.dma_start(a["OD"][b * DT:(b + 1) * DT].rearrange("t (h d) -> h t d", h=8)[:, :, ih * HR:(ih + 1) * HR],
                                     o[p0:p0 + 8]).then_inc(out, 16)
                sp.wait_ge(out, 16 * 18)
                sp.dma_start(ot[:, :], a["OD"]).then_inc(back, 16)

            @block.vector
            def _(dve):
                c = Chain(dve, ch)
                dve.wait_ge(loaded, 16 * 34)
                B = [P, HR, HD]
                over_i = lambda x: x.unsqueeze(1).to_broadcast(B)
                over_j = lambda x: x.unsqueeze(2).to_broadcast(B)
                for t in range(DT):
                    r, d, k, v, kk, b = (q[:, t * 6 + j, :] for j in range(6))
                    c(dve.tensor_tensor(tmp[:, :, :], S[:, :, :], over_i(kk), ALU.mult))
                    c(dve.tensor_reduce(sa[:, :], tmp[:, :, :], AX, ALU.add, negate=True))
                    c(dve.tensor_tensor(S[:, :, :], S[:, :, :], over_i(d), ALU.mult))
                    c(dve.tensor_tensor(tmp[:, :, :], over_j(sa[:, :]), over_i(b), ALU.mult))
                    c(dve.tensor_tensor(S[:, :, :], S[:, :, :], tmp[:, :, :], ALU.add))
                    c(dve.tensor_tensor(tmp[:, :, :], over_j(vs[:, t, :]), over_i(k), ALU.mult))
                    c(dve.tensor_tensor(S[:, :, :], S[:, :, :], tmp[:, :, :], ALU.add))
                    c(dve.tensor_tensor(tmp[:, :, :], S[:, :, :], over_i(r), ALU.mult))
                    c(dve.tensor_reduce(o[:, t, :], tmp[:, :, :], AX, ALU.add))
                dve.tensor_copy(sa[:, :], sa[:, :]).then_inc(done, 1)
                dve.wait_ge(turned, 1)
                c(dve.tensor_copy(m["obT"][:, :, SEQ:NT], pt[:, :, :]))

            @block.tensor
            def _(pe):
                pe.wait_ge(back, 16)
                for t in range(4):
                    i = pe.transpose(pt[:, t, :], ot[:, t * P:(t + 1) * P], m["ident"][0:NS, 0:NS])
                i.then_inc(turned, 1)


def rwkv_chunks(nc, a, m, kk, kp, bb, r, k, v, cum, masks, gam):
    NL = 6
    STRICT, INCL, LOW0 = 6, 7, 8
    with ExitStack() as ctx:
        sem, sb, ps = (f(nc, ctx, "rwc") for f in (sem_maker, sb_maker, ps_maker))
        bt, kt = cum, k[:, :, 0:SEQ]
        vt = sb("vt", [P, 4, 512])
        lt = sb("lt", [P, 8, P])
        ltm = sb("ltm", [P, 8, P])
        T = sb("T", [P, 8, P])
        X = sb("X", [P, 8, P])
        TT = sb("TT", [P, 2, 8, P])
        ak = sb("ak", [P, 2, 8, P])
        arb = sb("arb", [P, 2, 8, P])
        ark = sb("ark", [P, 2, 8, P])
        S = sb("S", [P, 4, HD])
        X1 = sb("X1", [P, 512])
        akv = sb("akv", [P, 2, 512])
        U = sb("U", [P, 512])
        so = sb("so", [HD, 8, HD])
        pp = ps("pp", [P, 2, 2, 512])
        pX = ps("pX", [P, 2, 512])
        pU, pO = ps("pU", [P, 512]), ps("pO", [P, 512])
        pS = pX[:, 0, 256:512]
        pOs = pX[:, 1, 256:512]
        pA = pp[:, 0, 0]
        ch, turned, tkept, prod, pkept, lvx, xk, lvy, lvk, masked, x1, x1k, u, uk, od, ok, sd, sk, fin, fink, s0, akd, akk, osp, oadd = (
            sem(s) for s in ("ch", "turned", "tkept", "prod", "pkept", "lvx", "xk", "lvy", "lvk", "masked", "x1", "x1k",
                             "u", "uk", "od", "ok", "sd", "sk", "fin", "fink", "s0", "akd", "akk", "osp", "oadd"))
        out = m["prompt_state_out"]
        at = lambda h: (slice((h % 2) * 64, (h % 2) * 64 + 64), h // 2)
        pos = lambda h: (h % 2) * 4 + h // 2
        slot = lambda s: pp[:, s].rearrange("p a (h c) -> p (a h) c", h=4)
        NP = 5
        with nc.Block() as block:

            @block.tensor
            def _(pe):
                for n, src in enumerate((bb, kp, v)):
                    for t in range(4):
                        w = n * 4 + t
                        if w >= 4:
                            pe.wait_ge(tkept, w - 3)
                        bank = pp[:, w % 4 // 2, w % 2]
                        for f in range(4):
                            i = pe.transpose(bank[:, f * P:(f + 1) * P], src[:, f, t * P:(t + 1) * P], m["ident"][:, :])
                        i.then_inc(turned, 1)
                pe.wait_ge(tkept, 12)
                for t in range(5):
                    if t < 4:
                        cols = slice(t * P, (t + 1) * P)
                        for n, (lhs, rhs) in enumerate(((bb, kk), (kk, bb), (kp, kk), (bb, r), (kp, r))):
                            w = t * NP + n
                            if n >= 2:
                                pe.wait_ge(pkept, w - 1)
                            elif t:
                                pe.wait_ge(lvk, (NL - 1) * t)
                            for h in range(8):
                                p, f = at(h)
                                i = pe.matmul(slot(n % 2)[:, pos(h), :], lhs[p, f, cols], rhs[p, f, cols], start=True, stop=True)
                            i.then_inc(prod, 1)
                        pe.wait_ge(pkept, (t + 1) * NP)
                        for h in range(8):
                            i = pe.matmul(pA[:, pos(h) * HD:(pos(h) + 1) * HD], ak[:, t % 2, pos(h), :], vt[:, t, h * HD:(h + 1) * HD], start=True, stop=True)
                        i.then_inc(akd, 1)
                        pe.wait_ge(akk, t + 1)
                        for l in range(1, NL):
                            lv = t * (NL - 1) + l
                            pe.wait_ge(masked, lv)
                            pe.wait_ge(lvk, lv - 1) if lv > 1 else None
                            for h in range(8):
                                i = pe.matmul(slot(0)[:, h, :], ltm[:, h, :], T[:, h, :], start=True, stop=True)
                            i.then_inc(lvx, 1)
                            pe.wait_ge(xk, lv)
                            for h in range(8):
                                pe.matmul(slot(0)[:, h, :], TT[:, t % 2, h, :], X[:, h, :], start=True, stop=True)
                                i = pe.matmul(slot(1)[:, h, :], X[:, h, :], TT[:, t % 2, h, :], start=True, stop=True)
                            i.then_inc(lvy, 1)
                    if t == 0:
                        pe.wait_ge(s0, 1)
                        continue
                    s = t - 1
                    pe.wait_ge(lvk, (NL - 1) * t)
                    for c in (2 * s, 2 * s + 1):
                        cb = slice((c % 2) * 64, (c % 2) * 64 + 64)
                        tc = slice(c * CH, (c + 1) * CH)
                        hc = lambda h: slice(h * HD, (h + 1) * HD)
                        pc = lambda h: slice(pos(h) * HD, (pos(h) + 1) * HD)
                        if c:
                            pe.wait_ge(sk, c)
                            pe.wait_ge(ok, c)
                        for h in range(8):
                            p, f = at(h)
                            i = pe.matmul(pX[cb, h % 2, f * HD:(f + 1) * HD], kk[p, f, tc], S[p, f, :], start=True, stop=True)
                        i.then_inc(x1, 1)
                        pe.wait_ge(x1k, c + 1)
                        for h in range(8):
                            p, f = at(h)
                            i = pe.matmul(pOs[p, f * CH:(f + 1) * CH], S[p, f, :], r[p, f, tc], start=True, stop=True)
                        i.then_inc(osp, 1)
                        for h in range(8):
                            i = pe.matmul(pU[cb, pc(h)], TT[cb, s % 2, pos(h), cb], X1[cb, pc(h)], start=True, stop=True)
                        i.then_inc(u, 1)
                        pe.wait_ge(uk, c + 1)
                        for h in range(8):
                            p, f = at(h)
                            o = pS[p, f * HD:(f + 1) * HD]
                            pe.matmul(o, bt[cb, s, hc(h)], U[cb, pc(h)], start=True, stop=False)
                            i = pe.matmul(o, kt[cb, s, hc(h)], vt[cb, s, hc(h)], start=False, stop=True)
                        i.then_inc(sd, 1)
                        if c:
                            pe.wait_ge(oadd, c)
                        for h in range(8):
                            p, f = at(h)
                            o = pO[p, f * CH:(f + 1) * CH]
                            pe.matmul(o, U[cb, pc(h)], arb[cb, s % 2, pos(h), cb], start=True, stop=False)
                            i = pe.matmul(o, vt[cb, s, hc(h)], ark[cb, s % 2, pos(h), cb], start=False, stop=True)
                        i.then_inc(od, 1)
                pe.wait_ge(sk, NCH)
                for f in range(4):
                    i = pe.transpose(pA[0:HD, f * P:(f + 1) * P], S[:, f, :], m["ident"][:, :])
                i.then_inc(fin, 1)

            @block.gpsimd
            def _(pool):
                pool.memset(S[:, :, :], 0.0).then_inc(s0, 1)
                for t in range(4):
                    for l in range(1, NL):
                        lv = t * (NL - 1) + l
                        pool.wait_ge(pkept, t * NP + 1)
                        if lv > 1:
                            pool.wait_ge(lvx, lv - 1)
                        pool.tensor_tensor(ltm[:, :, :], lt[:, :, :], masks[:, l:l + 1, :].to_broadcast([P, 8, P]), ALU.mult).then_inc(masked, 1)

            @block.vector
            def _(dve):
                c_ = Chain(dve, ch)
                for n, dst in enumerate((bt, kt, vt)):
                    for t in range(4):
                        w = n * 4 + t
                        dve.wait_ge(turned, w + 1)
                        dve.tensor_copy(dst[:, t, :], pp[:, w % 4 // 2, w % 2]).then_inc(tkept, 1)
                mask = lambda n: masks[:, n:n + 1, :].to_broadcast([P, 8, P])
                eye = m["ident"][:, :].unsqueeze(1).to_broadcast([P, 8, P])
                for t in range(5):
                    if t < 4:
                        for n in range(NP):
                            w = t * NP + n
                            dve.wait_ge(prod, w + 1)
                            p = slot(n % 2)
                            if n == 0:
                                if t:
                                    dve.wait_ge(masked, t * (NL - 1))
                                c_(dve.tensor_copy(lt[:, :, :], p))
                                c_(dve.tensor_tensor(X[:, :, :], lt[:, :, :], mask(0), ALU.mult))
                                dve.tensor_tensor(TT[:, t % 2], eye, X[:, :, :], ALU.subtract).then_inc(pkept, 1)
                            elif n == 1:
                                dve.wait_ge(pkept, w)
                                c_(dve.tensor_tensor(X[:, :, :], p, mask(LOW0), ALU.mult))
                                dve.tensor_tensor(T[:, :, :], eye, X[:, :, :], ALU.subtract).then_inc(pkept, 1)
                            else:
                                dst = (ak, arb, ark)[n - 2]
                                dve.tensor_tensor(dst[:, t % 2], p, mask(STRICT if n == 2 else INCL), ALU.mult).then_inc(pkept, 1)
                        dve.wait_ge(akd, t + 1)
                        dve.tensor_copy(akv[:, t % 2], pA).then_inc(akk, 1)
                        for l in range(1, NL):
                            lv = t * (NL - 1) + l
                            dve.wait_ge(lvx, lv)
                            dve.tensor_copy(X[:, :, :], slot(0)).then_inc(xk, 1)
                            dve.wait_ge(lvy, lv)
                            c_(dve.tensor_tensor(T[:, :, :], T[:, :, :], slot(0), ALU.subtract))
                            dve.tensor_tensor(TT[:, t % 2], TT[:, t % 2], slot(1), ALU.subtract).then_inc(lvk, 1)
                    if t == 0:
                        dve.wait_ge(s0, 1)
                        continue
                    s = t - 1
                    for c in (2 * s, 2 * s + 1):
                        cb = slice((c % 2) * 64, (c % 2) * 64 + 64)
                        dve.wait_ge(x1, c + 1)
                        hp = lambda x: x.rearrange("p (a c) -> p a c", a=2)
                        dve.tensor_tensor(hp(X1[cb, :]), pX[cb, :, 0:256], hp(akv[cb, s % 2, :]), ALU.add).then_inc(x1k, 1)
                        dve.wait_ge(u, c + 1)
                        if c >= 1:
                            dve.wait_ge(od, c)
                        dve.tensor_scalar(U[cb, :], pU[cb, :], -1.0, None, ALU.mult).then_inc(uk, 1)
                        dve.wait_ge(sd, c + 1)
                        dve.wait_ge(od, c + 1)
                        c_(dve.tensor_tensor(S[:, :, :], S[:, :, :], pS.rearrange("p (f c) -> p f c", f=4), ALU.add))
                        dve.tensor_tensor(S[:, :, :], S[:, :, :], gam[:, :, c:c + 1].to_broadcast([P, 4, HD]), ALU.mult).then_inc(sk, 1)
                        dve.wait_ge(ok, c + 1)
                        oc = m["obT"][:, :, c * CH:(c + 1) * CH]
                        dve.tensor_tensor(oc, oc, pO[:, 0:256].rearrange("p (f c) -> p f c", f=4), ALU.add).then_inc(oadd, 1)
                dve.wait_ge(fin, 1)
                dve.tensor_copy(so[:, :, :], pA[0:HD, :].rearrange("p (h j) -> p h j", h=8)).then_inc(fink, 1)

            @block.scalar
            def _(act):
                for c in range(NCH):
                    act.wait_ge(osp, c + 1)
                    nc.scalar.activation(m["obT"][:, :, c * CH:(c + 1) * CH], pOs.rearrange("p (f c) -> p f c", f=4), ACT.Copy).then_inc(ok, 1)
                act.wait_ge(fink, 1)
                act.dma_start(a["o_rwkv_p"][0, 0].rearrange("h i j -> i h j"), so[:, :, :]).then_inc(out, 16)
                act.wait_ge(out, 16)


def rwkv_norm(nc, a, m, gate, bonus):
    o, prm = m["obT"], m["prm"]
    with ExitStack() as ctx:
        sem, sb, ps = (f(nc, ctx, "rwn") for f in (sem_maker, sb_maker, ps_maker))
        sq = sb("sq", [P, 4, NT])
        eps = sb("eps", [P, 1])
        acc = ps("acc", [P, 4, 2, 512])
        ch, mean, cen, var, std = (sem(s) for s in ("ch", "mean", "cen", "var", "std"))
        with nc.Block() as block:

            @block.tensor
            def _(pe):
                for t in range(4):
                    head_sums(pe, acc[:, t], m["headones"][:, :], o[:, t]).then_inc(mean, 1)
                for t in range(4):
                    pe.wait_ge(cen, t + 1)
                    head_sums(pe, acc[:, t], m["headones"][:, :], sq[:, t]).then_inc(var, 1)

            @block.scalar
            def _(act):
                for t in range(4):
                    act.wait_ge(var, t + 1)
                    nc.scalar.activation(halves(sq[:, t]), acc[:, t, :, 0:HN], ACT.Sqrt, bias=eps[:, :], scale=1.0 / HD).then_inc(std, 1)

            @block.vector
            def _(dve):
                c = Chain(dve, ch)
                c(dve.memset(eps[:, :], GN_EPS))
                for t in range(4):
                    dve.wait_ge(mean, t + 1)
                    c(dve.scalar_tensor_tensor(halves(o[:, t]), acc[:, t, :, 0:HN], -1.0 / HD, halves(o[:, t]), ALU.mult, ALU.add))
                    dve.tensor_tensor(sq[:, t], o[:, t], o[:, t], ALU.mult).then_inc(cen, 1)
                for t in range(4):
                    dve.wait_ge(std, t + 1)
                    c(dve.reciprocal(sq[:, t], sq[:, t]))
                    c(dve.tensor_tensor(o[:, t], o[:, t], sq[:, t], ALU.mult))
                    c(dve.tensor_scalar(o[:, t], o[:, t], prm[:, PROW["rw_gn_g"] + t:PROW["rw_gn_g"] + t + 1],
                                        prm[:, PROW["rw_gn_b"] + t:PROW["rw_gn_b"] + t + 1], ALU.mult, ALU.add))
                    c(dve.tensor_tensor(o[:, t], o[:, t], bonus[:, t], ALU.add))
                    c(dve.tensor_tensor(o[:, t], o[:, t], gate[:, t], ALU.mult))


def compress(nc, a, m):
    NSEQ = DB + 1
    work = [(s, c) for s in range(NSEQ) for c in range(4)]
    nhalf = lambda s: 2 if s < DB else 1
    rows = lambda s: P if s < DB else SEQ // 16
    nwin = lambda s: NC_S if s < DB else NC_P
    tmark, n = [], 0
    for s, c in work:
        tmark.append(n)
        n += 2 * nhalf(s)
    with ExitStack() as ctx:
        sem, sb, ps = (f(nc, ctx, "cmp") for f in (sem_maker, sb_maker, ps_maker))
        w1 = sb("w1", [P, 2, 16, P])
        w2 = sb("w2", [P, 2, HD])
        per = sb("per", [32, P])
        peT = sb("peT", [P, 32])
        hc = sb("hc", [P, 2])
        R = sb("R", [P, 2, 2, 4, 1024])
        RT = sb("RT", [P, 2, 8, 256])
        hid = sb("hid", [P, 2, 256])
        pt = sb("pt", [P, 2 * DB], I32)
        lane = sb("lane", [P, 1], I32)
        pT = ps("pT", [P, 4, 512])
        pH = ps("pH", [P, 2, 512])
        pK = ps("pK", [P, 2, 512])
        loaded, idx, ix, pet, pek, hcd, hck, turned, tkept, hd, act_, od, ok = (
            sem(s) for s in ("loaded", "idx", "ix", "pet", "pek", "hcd", "hck", "turned", "tkept", "hd", "act", "od", "ok"))
        got, got_p = [sem(f"got{i}") for i in range(2)], sem("gotp")
        with nc.Block() as block:

            @block.sync
            def _(sp):
                sp.dma_start(pt[:, :], a["page_lanes"]).then_inc(loaded, 16)
                sp.dma_start(lane[:, :], a["c_lane"]).then_inc(loaded, 16)
                sp.dma_start(w1[:, :, :, :], a["phi_w1"][0].rearrange("v l d h -> v (l d) h").rearrange("v (c p) h -> p v c h", p=P)).then_inc(loaded, 16)
                sp.dma_start(w2[:, :, :], a["phi_w2"][0].rearrange("v h d -> h v d")).then_inc(loaded, 16)
                sp.dma_start(per[:, :], a["phi_pe"][0].rearrange("v l d -> (v l d)").rearrange("(c p) -> c p", p=P)).then_inc(loaded, 16)
                sp.wait_ge(tkept, tmark[4 * (DB - 1)])
                sp.dma_start(R[0:32, DB % 2, 0, :, :],
                             a["o_cmp_p"][0, 0].rearrange("v g (c l) d -> c (v g) (l d)", l=16)).then_inc(got_p, 16)

            @block.gpsimd
            def _(pool):
                pool.wait_ge(idx, 5)
                src = a["cache_nsa_cmp"][0].rearrange("n v g (c l) d -> (n v g c) (l d)", l=16)
                for s in range(DB):
                    if s >= 2:
                        pool.wait_ge(tkept, tmark[4 * (s - 1)])
                    for h in range(2):
                        for c in range(4):
                            pool.indirect_dma_start(
                                out=R[:, s % 2, h, c, :], out_offset=None, in_=src,
                                in_offset=bass.IndirectOffsetOnAxis(ap=m["idx"][:, c, 2 * s + h:2 * s + h + 1], axis=0),
                            ).then_inc(got[s % 2], 16)

            @block.tensor
            def _(pe):
                pe.wait_ge(loaded, 80)
                pe.transpose(pK[:, 0, 0:32], per[:, :], m["ident"][0:32, 0:32]).then_inc(pet, 1)
                pe.wait_ge(pek, 1)
                for v in range(2):
                    for c in range(16):
                        i = pe.matmul(pH[:, 0, v:v + 1], w1[:, v, c, :], peT[:, v * 16 + c:v * 16 + c + 1], start=(c == 0), stop=(c == 15))
                i.then_inc(hcd, 1)
                pe.wait_ge(hck, 1)

                def turn(w):
                    s, c = work[w]
                    if c == 0:
                        if s < DB:
                            pe.wait_ge(got[s % 2], 128 * (s // 2 + 1))
                        else:
                            pe.wait_ge(got_p, 16)
                    k = tmark[w]
                    for h in range(nhalf(s)):
                        for kq in range(2):
                            if k >= 4:
                                pe.wait_ge(tkept, k - 3)
                            for j in range(4):
                                kc = kq * 4 + j
                                i = pe.transpose(pT[:, k % 4, j * P:j * P + rows(s)], R[0:rows(s), s % 2, h, c, kc * P:(kc + 1) * P],
                                                 m["ident"][0:rows(s), 0:rows(s)])
                            i.then_inc(turned, 1)
                            k += 1

                def hidden(w):
                    s, c = work[w]
                    pe.wait_ge(tkept, tmark[w] + 2 * nhalf(s))
                    if w >= 2:
                        pe.wait_ge(act_, w - 1)
                    nw = nwin(s)
                    for q in range(16):
                        i = pe.matmul(pH[:, w % 2, 0:nw], w1[:, c // 2, q, :], RT[:, w % 2, q % 8, q // 8:q // 8 + nw],
                                      start=(q == 0), stop=(q == 15))
                    i.then_inc(hd, 1)

                def project(w):
                    s, c = work[w]
                    v, g = c // 2, c % 2
                    pe.wait_ge(act_, w + 1)
                    if w >= 2:
                        pe.wait_ge(ok, w - 1)
                    nw = nwin(s)
                    if v == 0:
                        i = pe.matmul(pK[g * HD:(g + 1) * HD, w % 2, 0:nw], w2[:, 0, :], hid[:, w % 2, 0:nw], start=True, stop=True)
                    else:
                        for h in range(nhalf(s)):
                            n = min(P, nw - h * P)
                            i = pe.matmul(pK[0:n, w % 2, h * HD:(h + 1) * HD], hid[:, w % 2, h * P:h * P + n], w2[:, 1, :], start=True, stop=True)
                    i.then_inc(od, 1)

                turn(0)
                for w in range(len(work)):
                    if w + 1 < len(work):
                        turn(w + 1)
                    hidden(w)
                    if w:
                        project(w - 1)
                project(len(work) - 1)

            @block.scalar
            def _(act):
                act.wait_ge(hck, 1)
                for w, (s, c) in enumerate(work):
                    act.wait_ge(hd, w + 1)
                    if w >= 2:
                        act.wait_ge(od, w - 1)
                    nc.scalar.activation(hid[:, w % 2, 0:nwin(s)], pH[:, w % 2, 0:nwin(s)], ACT.Gelu_apprx_tanh,
                                         bias=hc[:, c // 2:c // 2 + 1]).then_inc(act_, 1)

            @block.vector
            def _(dve):
                ch = Chain(dve, ix)
                dve.wait_ge(loaded, 80)
                ch(dve.tensor_scalar(pt[:, :], pt[:, :], 32.0, None, ALU.mult))
                ch(dve.tensor_tensor(pt[:, :], pt[:, :], lane[:, 0:1].to_broadcast([P, 2 * DB]), ALU.add))
                for c in range(4):
                    dve.tensor_scalar(m["idx"][:, c, :], pt[:, :], float(8 * c), None, ALU.add).then_inc(idx, 1)
                dve.wait_ge(idx, 4)
                dve.sem_inc(idx, 1)
                dve.wait_ge(pet, 1)
                dve.tensor_copy(peT[:, :], pK[:, 0, 0:32]).then_inc(pek, 1)
                dve.wait_ge(hcd, 1)
                dve.tensor_copy(hc[:, :], pH[:, 0, 0:2]).then_inc(hck, 1)

                def keep(w):
                    s, c = work[w]
                    if w >= 2:
                        dve.wait_ge(hd, w - 1)
                    k = tmark[w]
                    for h in range(nhalf(s)):
                        for kq in range(2):
                            dve.wait_ge(turned, k + 1)
                            dve.tensor_copy(RT[:, w % 2, kq * 4:kq * 4 + 4, h * P:h * P + rows(s)],
                                            pT[:, k % 4, :].rearrange("p (j c) -> p j c", j=4)[:, :, 0:rows(s)]).then_inc(tkept, 1)
                            k += 1

                def result(w):
                    s, c = work[w]
                    v, g = c // 2, c % 2
                    dve.wait_ge(od, w + 1)
                    nw = nwin(s)
                    if v == 0:
                        gp = slice(g * HD, (g + 1) * HD)
                        dve.tensor_copy(m["kcT"][gp, s, 0:nw], pK[gp, w % 2, 0:nw]).then_inc(ok, 1)
                    else:
                        for h in range(nhalf(s)):
                            n = min(P, nw - h * P)
                            i = dve.tensor_copy(m["vc"][0:n, s, h, g * HD:(g + 1) * HD], pK[0:n, w % 2, h * HD:(h + 1) * HD])
                        i.then_inc(ok, 1)

                keep(0)
                for w in range(len(work)):
                    if w + 1 < len(work):
                        keep(w + 1)
                    if w:
                        result(w - 1)
                result(len(work) - 1)


def layer_norm_t(nc, a, m, tag, xin, out_tokens=None, gain="ln1"):
    prm = m["prm"]
    with ExitStack() as ctx:
        sem, sb, ps = (f(nc, ctx, tag) for f in (sem_maker, sb_maker, ps_maker))
        ones = sb("ones", [P, P])
        eps = sb("eps", [P, 1])
        mu = sb("mu", [P, NT])
        sq = sb("sq", [P, 2, NT])
        acc = ps("acc", [P, 2, 2, 512])
        y = sb("y", [P, 2, 512])
        pT = ps("pT", [P, 2, 512])
        ch, o1, summed, cen, var, std, ready, turned, kept = (sem(s) for s in (
            "ch", "o1", "summed", "cen", "var", "std", "ready", "turned", "kept"))
        stored = [m["y_out0"], m["y_out1"]]
        work = [(t, h) for t in range(5) for h in range(2)] if out_tokens else []
        rows = lambda t: P if t < 4 else NS
        with nc.Block() as block:

            @block.tensor
            def _(pe):
                pe.wait_ge(o1, 1)
                for k in range(KD):
                    for h in range(2):
                        i = pe.matmul(acc[:, 0, h, 0:HN], ones[:, :], xin[:, k, h * HN:(h + 1) * HN], start=(k == 0), stop=(k == KD - 1))
                i.then_inc(summed, 1)
                for k in range(KD):
                    pe.wait_ge(cen, k + 1)
                    for h in range(2):
                        i = pe.matmul(acc[:, 1, h, 0:HN], ones[:, :], sq[:, k % 2, h * HN:(h + 1) * HN], start=(k == 0), stop=(k == KD - 1))
                    i.then_inc(var, 1)
                for w, (t, h) in enumerate(work):
                    if w == 0:
                        pe.wait_ge(ready, KD)
                    if w >= 2:
                        pe.wait_ge(kept, w - 1)
                    for j in range(4):
                        i = pe.transpose(pT[0:rows(t), w % 2, j * P:(j + 1) * P], xin[:, 4 * h + j, t * P:t * P + rows(t)], m["ident"][:, :])
                    i.then_inc(turned, 1)

            @block.scalar
            def _(act):
                act.wait_ge(var, KD)
                nc.scalar.activation(halves(sq[:, 0]), acc[:, 1, :, 0:HN], ACT.Sqrt, bias=eps[:, :], scale=1.0 / D).then_inc(std, 1)
                if work:
                    for w, (t, h) in enumerate(work):
                        act.wait_ge(kept, w + 1)
                        if t < 4:
                            dst = a[out_tokens[0]][0, t * P:(t + 1) * P, h * 512:(h + 1) * 512]
                        else:
                            dst = a[out_tokens[1]].rearrange("b t d -> (b t) d")[:, h * 512:(h + 1) * 512]
                        act.dma_start(dst, y[0:rows(t), w % 2, :]).then_inc(stored[w % 2], 16)
                    for s in range(2):
                        act.wait_ge(stored[s], 16 * (len(work) // 2))

            @block.vector
            def _(dve):
                c = Chain(dve, ch)
                c(dve.memset(eps[:, :], LN_EPS))
                dve.memset(ones[:, :], 1.0).then_inc(o1, 1)
                dve.wait_ge(summed, 1)
                c(dve.tensor_scalar(halves(mu[:, :]), acc[:, 0, :, 0:HN], -1.0 / D, None, ALU.mult))
                for k in range(KD):
                    c(dve.tensor_tensor(xin[:, k], xin[:, k], mu[:, :], ALU.add))
                    if k >= 2:
                        dve.wait_ge(var, k - 1)
                    dve.tensor_tensor(sq[:, k % 2], xin[:, k], xin[:, k], ALU.mult).then_inc(cen, 1)
                dve.wait_ge(std, 1)
                c(dve.reciprocal(mu[:, :], sq[:, 0]))
                for k in range(KD):
                    c(dve.tensor_tensor(xin[:, k], xin[:, k], mu[:, :], ALU.mult))
                    g, b = PROW[gain + "_g"] + k, PROW[gain + "_b"] + k
                    dve.tensor_scalar(xin[:, k], xin[:, k], prm[:, g:g + 1], prm[:, b:b + 1], ALU.mult, ALU.add).then_inc(ready, 1)
                if gain == "ln1":
                    dve.wait_ge(ready, KD)
                    modulate(dve, c, m["hT"], m["xT"], m["modT"], 3 * KD, 4 * KD)
                for w, (t, h) in enumerate(work):
                    dve.wait_ge(turned, w + 1)
                    if w >= 2:
                        dve.wait_ge(stored[w % 2], 16 * (w // 2))
                    dve.tensor_copy(y[0:rows(t), w % 2, :], pT[0:rows(t), w % 2, :]).then_inc(kept, 1)


def gated_residual(dve, c, x, n, acc, modT, gate, tmp):
    g = gate + n
    flat = tmp
    c(dve.tensor_copy(halves(flat), acc))
    c(dve.tensor_scalar(flat[:, 0:SEQ], flat[:, 0:SEQ], modT[:, g, 0:1], None, ALU.mult))
    s = flat[:, SEQ:NT].rearrange("p (b t) -> p b t", t=DT)
    c(dve.tensor_tensor(s, s, modT[:, g, 1:9].unsqueeze(2).to_broadcast([P, DB, DT]), ALU.mult))
    c(dve.scalar_tensor_tensor(x[:, n], x[:, n], ALPHA, flat, ALU.mult, ALU.add))


def merge(nc, a, m):
    BR = (("w_br_a", "oaT", 4), ("w_br_b", "obT", 4), ("w_br_c", "ocT", 2))
    with ExitStack() as ctx:
        sem, sb, ps = (f(nc, ctx, "mrg") for f in (sem_maker, sb_maker, ps_maker))
        wb = sb("wb", [P, 10, D])
        wo = sb("wo", [P, KD, D])
        gt = sb("gt", [P, 6, NT])
        t1 = sb("t1", [P, NT])
        t2 = sb("t2", [P, NT])
        acc = ps("acc", [P, 4, 2, 512])
        mT = m["hT"]
        loaded, wol, sig, done, used, ch, out, oused = (sem(s) for s in ("loaded", "wol", "sig", "done", "used", "ch", "out", "oused"))
        gl = [sem(f"g{i}") for i in range(2)]
        with nc.Block() as block:

            @block.sync
            def _(sp):
                at = 0
                for name, _, n in BR:
                    sp.dma_start(wb[:, at:at + n, :], a[name][0].rearrange("(k p) n -> p k n", p=P)).then_inc(loaded, 16)
                    at += n
                for n in range(KD):
                    if n >= 2:
                        sp.wait_ge(used, 3 * (n - 1))
                    for b in range(3):
                        t = TILE0["gm"] + b * KD + n
                        sp.dma_start(gt[:, 3 * (n % 2) + b, :], a["PT"][t * P:(t + 1) * P, :]).then_inc(gl[n % 2], 16)
                    if n == 1:
                        sp.dma_start(wo[:, :, :], a["w_o"][0].rearrange("(k p) n -> p k n", p=P)).then_inc(wol, 16)

            @block.scalar
            def _(act):
                for n in range(KD):
                    act.wait_ge(gl[n % 2], 48 * (n // 2 + 1))
                    nc.scalar.activation(gt[:, 3 * (n % 2):3 * (n % 2) + 3, :], gt[:, 3 * (n % 2):3 * (n % 2) + 3, :], ACT.Sigmoid).then_inc(sig, 1)

            @block.tensor
            def _(pe):
                pe.wait_ge(loaded, 48)
                for n in range(KD):
                    at = 0
                    for b, (_, src, nk) in enumerate(BR):
                        w = 3 * n + b
                        if w >= 4:
                            pe.wait_ge(used, w - 3)
                        for k in range(nk):
                            for h in range(2):
                                i = pe.matmul(acc[:, w % 4, h, 0:HN], wb[:, at + k, n * P:(n + 1) * P],
                                              m[src][:, k, h * HN:(h + 1) * HN], start=(k == 0), stop=(k == nk - 1))
                        i.then_inc(done, 1)
                        at += nk
                pe.wait_ge(wol, 16)
                pe.wait_ge(used, 3 * KD)
                for n in range(KD):
                    if n >= 4:
                        pe.wait_ge(oused, n - 3)
                    for k in range(KD):
                        for h in range(2):
                            i = pe.matmul(acc[:, n % 4, h, 0:HN], wo[:, k, n * P:(n + 1) * P], mT[:, k, h * HN:(h + 1) * HN],
                                          start=(k == 0), stop=(k == KD - 1))
                    i.then_inc(out, 1)

            @block.vector
            def _(dve):
                c = Chain(dve, ch)
                for n in range(KD):
                    dve.wait_ge(sig, n + 1)
                    g = lambda b: halves(gt[:, 3 * (n % 2) + b])
                    ac = lambda w: acc[:, w % 4, :, 0:HN]
                    w = 3 * n
                    dve.wait_ge(done, w + 1)
                    c(dve.tensor_tensor(halves(t1[:, :]), ac(w), g(0), ALU.mult))
                    dve.sem_inc(used, 1)
                    dve.wait_ge(done, w + 2)
                    c(dve.tensor_tensor(halves(t2[:, :]), ac(w + 1), g(1), ALU.mult))
                    dve.sem_inc(used, 1)
                    c(dve.tensor_tensor(t1[:, :], t1[:, :], t2[:, :], ALU.add))
                    dve.wait_ge(done, w + 3)
                    c(dve.tensor_tensor(halves(t2[:, :]), ac(w + 2), g(2), ALU.mult))
                    dve.tensor_tensor(mT[:, n], t1[:, :], t2[:, :], ALU.add).then_inc(used, 1)
                    dve.wait_ge(used, 3 * n + 3)
                for n in range(KD):
                    dve.wait_ge(out, n + 1)
                    gated_residual(dve, c, m["xT"], n, acc[:, n % 4, :, 0:HN], m["modT"], 2 * KD, t1[:, :])
                    dve.sem_inc(oused, 1)
    layer_norm_t(nc, a, m, "ln1", m["xT"])


def feed_forward(nc, a, m):
    NF = FF // P
    CW = 2
    NL = NF // CW
    with ExitStack() as ctx:
        sem, sb, ps = (f(nc, ctx, "ffn") for f in (sem_maker, sb_maker, ps_maker))
        f = sb("f", [P, NF, NT])
        wg = sb("wg", [P, 3, 2, KD, CW * P])
        sil = sb("sil", [P, 2, NT])
        tmp = sb("tmp", [P, NT])
        w2 = wg[:, :, :, :, :].rearrange("p a b k c -> p (a b k c)")[:, 0:2 * NF * P].rearrange("p (s k c) -> p s k c", s=2, k=NF)
        acc = ps("acc", [P, 4, 2, 512])
        wl = [sem(f"w{i}") for i in range(3)]
        w2l = [sem(f"v{i}") for i in range(2)]
        done, sd, used, done2, used2, ch = (sem(s) for s in ("done", "sd", "used", "done2", "used2", "ch"))
        w1r = a["w_ffn1"][0].rearrange("(k p) n -> p k n", p=P)
        w2r = a["w_ffn2"][0].rearrange("(k p) n -> p k n", p=P)
        with nc.Block() as block:

            @block.sync
            def _(sp):
                for l in range(NL):
                    if l >= 3:
                        sp.wait_ge(done, 2 * CW * (l - 2))
                    for u in range(2):
                        c = u * FF + l * CW * P
                        sp.dma_start(wg[:, l % 3, u, :, :], w1r[:, :, c:c + CW * P]).then_inc(wl[l % 3], 16)
                for n in range(KD):
                    if n == 0:
                        sp.wait_ge(done, 2 * NF)
                    if n >= 2:
                        sp.wait_ge(done2, n - 1)
                    sp.dma_start(w2[:, n % 2, :, :], w2r[:, :, n * P:(n + 1) * P]).then_inc(w2l[n % 2], 16)

            @block.tensor
            def _(pe):
                for t in range(NF):
                    l = t // CW
                    if t % CW == 0:
                        pe.wait_ge(wl[l % 3], 32 * (l // 3 + 1))
                    for u in range(2):
                        w = 2 * t + u
                        if w >= 4:
                            pe.wait_ge(used, (w - 4) // 2 + 1)
                        for k in range(KD):
                            for h in range(2):
                                i = pe.matmul(acc[:, w % 4, h, 0:HN], wg[:, l % 3, u, k, (t % CW) * P:(t % CW + 1) * P],
                                              m["hT"][:, k, h * HN:(h + 1) * HN], start=(k == 0), stop=(k == KD - 1))
                        i.then_inc(done, 1)
                pe.wait_ge(used, NF)
                for n in range(KD):
                    pe.wait_ge(w2l[n % 2], 16 * (n // 2 + 1))
                    if n >= 4:
                        pe.wait_ge(used2, n - 3)
                    for k in range(NF):
                        for h in range(2):
                            i = pe.matmul(acc[:, n % 4, h, 0:HN], w2[:, n % 2, k, :], f[:, k, h * HN:(h + 1) * HN],
                                          start=(k == 0), stop=(k == NF - 1))
                    i.then_inc(done2, 1)

            @block.scalar
            def _(act):
                for t in range(NF):
                    act.wait_ge(done, 2 * t + 1)
                    if t >= 2:
                        act.wait_ge(used, t - 1)
                    nc.scalar.activation(halves(sil[:, t % 2]), acc[:, 2 * t % 4, :, 0:HN], ACT.Silu).then_inc(sd, 1)

            @block.vector
            def _(dve):
                c = Chain(dve, ch)
                for t in range(NF):
                    dve.wait_ge(sd, t + 1)
                    dve.wait_ge(done, 2 * t + 2)
                    dve.tensor_tensor(halves(f[:, t]), acc[:, (2 * t + 1) % 4, :, 0:HN], halves(sil[:, t % 2]), ALU.mult).then_inc(used, 1)
                for n in range(KD):
                    dve.wait_ge(done2, n + 1)
                    gated_residual(dve, c, m["xT"], n, acc[:, n % 4, :, 0:HN], m["modT"], 5 * KD, tmp[:, :])
                    dve.sem_inc(used2, 1)
    layer_norm_t(nc, a, m, "ln2", m["xT"], out_tokens=("o_y_p", "o_y_s"), gain="ln2")


def prompt_attention(nc, a, m):
    SA = slopes(GRP * HPG)
    SC = slopes(12)
    units = [(qt, "A", h) for qt in range(4) for h in range(8)] + [(qt, "C", h) for qt in range(4) for h in range(4)]
    NU = len(units)
    with ExitStack() as ctx:
        sem, sb, ps = (f(nc, ctx, "pat") for f in (sem_maker, sb_maker, ps_maker))
        qA = sb("qA", [P, HPG, SEQ])
        kA = sb("kA", [P, 2, SEQ])
        vA = sb("vA", [P, 2, 4, P])
        qC = sb("qC", [P, 6, SEQ])
        kC = sb("kC", [P, 6, SEQ])
        vC = sb("vC", [P, 4, 768])
        dist = sb("dist", [P, 4, SEQ])
        distc = sb("distc", [P, 4, 32])
        s = sb("s", [P, 2, 3, SEQ])
        pT = sb("pT", [P, 2, 3, SEQ])
        st = sb("st", [P, 4, 4, 4])
        tot = sb("tot", [P, 4, 2])
        pS = ps("pS", [P, 3, 512])
        pX = ps("pX", [P, 2, 512])
        pO = ps("pO", [P, 2, 512])
        loaded, qs, sc, sx, ex, wt, sd, tr, tk, pv, oe, ch = (
            sem(n) for n in ("loaded", "qs", "sc", "sx", "ex", "wt", "sd", "tr", "tk", "pv", "oe", "ch"))

        def branch(u, b):
            qt, kind, h = units[u]
            qc = slice(qt * P, (qt + 1) * P)
            if kind == "A":
                g, n = h // HPG, h % HPG
                r = slice(g * HD, (g + 1) * HD)
                if b == 0:
                    return qA[r, n, qc], m["kcT"][r, DB, 0:NC_P], 0, NC_P, [m["vc"][0:NC_P, DB, 0, r]], SA[h], distc[:, qt, 0:NC_P]
                return (qA[r, n, qc], kA[r, b - 1, 0:(qt + 1) * P], 0, (qt + 1) * P,
                        [vA[:, b - 1, k, r] for k in range(qt + 1)], SA[h], dist[:, 0, (3 - qt) * P:SEQ])
            r = slice((h % 2) * HD, (h % 2) * HD + HD)
            t = 2 * b + h // 2
            k0 = max(0, qt - 1) if b == 0 else 0
            c0 = (4 * b + h) * HD
            return (qC[r, t, qc], kC[r, t, k0 * P:(qt + 1) * P], k0 * P, (qt + 1 - k0) * P,
                    [vC[:, k, c0:c0 + HD] for k in range(k0, qt + 1)], SC[4 * b + h],
                    dist[:, 1 + b, (3 - qt + k0) * P:SEQ])

        with nc.Block() as block:

            @block.sync
            def _(sp):
                t = TILE0["qa"] * P
                for g in range(GRP):
                    sp.dma_start(qA[g * HD:(g + 1) * HD, :, :],
                                 a["PT"][t + g * 256:t + (g + 1) * 256, 0:SEQ].rearrange("(n d) t -> d n t", d=HD)).then_inc(loaded, 16)
                for i, (name, col) in enumerate((("kvs", "slc"), ("kvw", "win"))):
                    t = TILE0[name] * P
                    sp.dma_start(kA[:, i, :], a["PT"][t:t + P, 0:SEQ]).then_inc(loaded, 16)
                    c = TM_COL[col] + P
                    sp.dma_start(vA[:, i, :, :], a["TM"][0:SEQ, c:c + P].rearrange("(k p) c -> p k c", p=P)).then_inc(loaded, 16)
                for buf, name in ((qC, "qc"), (kC, "kc")):
                    t = TILE0[name] * P
                    sp.dma_start(buf[:, :, :], a["PT"][t:t + 768, 0:SEQ].rearrange("(n p) t -> p n t", p=P)).then_inc(loaded, 16)
                c = TM_COL["vc"]
                sp.dma_start(vC[:, :, :], a["TM"][0:SEQ, c:c + 768].rearrange("(k p) c -> p k c", p=P)).then_inc(loaded, 16)
                sp.dma_start(dist[:, :, :], a["c_dist"].rearrange("n p k -> p n k")).then_inc(loaded, 16)
                sp.dma_start(distc[:, :, :], a["c_distc"].rearrange("n p k -> p n k")).then_inc(loaded, 16)
            NLOAD = 16 * 11

            @block.tensor
            def _(pe):
                pe.wait_ge(qs, 2)

                def scores(u):
                    if u:
                        pe.wait_ge(sx, u)
                    for b in range(3):
                        q, k, _, n, _, _, _ = branch(u, b)
                        i = pe.matmul(pS[:, b, 0:n], q, k, start=True, stop=True)
                    i.then_inc(sc, 1)

                def turn(u):
                    for b in range(3):
                        w = 3 * u + b
                        pe.wait_ge(sd, w + 1)
                        if w >= 2:
                            pe.wait_ge(tk, w - 1)
                        n = branch(u, b)[3]
                        for k in range(-(-n // P)):
                            c = min(P, n - k * P)
                            i = pe.transpose(pX[0:c, w % 2, k * P:(k + 1) * P], s[:, u % 2, b, k * P:k * P + c], m["ident"][:, :])
                        i.then_inc(tr, 1)

                def values(u):
                    qt, kind, h = units[u]
                    o = pO[(h % 2) * HD:(h % 2) * HD + HD, u % 2, 0:P]
                    if u >= 2:
                        pe.wait_ge(oe, u - 1)
                    for b in (1, 2, 0):
                        if b == 1:
                            pe.wait_ge(tk, 3 * u + 3)
                        vs = branch(u, b)[4]
                        for k, v in enumerate(vs):
                            i = pe.matmul(o, v, pT[0:v.shape[0], u % 2, b, k * P:(k + 1) * P],
                                          start=(b == 1 and k == 0), stop=(b == 0 and k == len(vs) - 1))
                    i.then_inc(pv, 1)

                for i in range(NU + 2):
                    if i < NU:
                        scores(i)
                    if 1 <= i <= NU:
                        turn(i - 1)
                    if i >= 2:
                        values(i - 2)

            @block.scalar
            def _(act):
                act.wait_ge(loaded, NLOAD)
                nc.scalar.activation(qA[:, :, :], qA[:, :, :], ACT.Copy, scale=HD ** -0.5).then_inc(qs, 1)
                nc.scalar.activation(qC[:, :, :], qC[:, :, :], ACT.Copy, scale=HD ** -0.5).then_inc(qs, 1)
                for i in range(NU + 1):
                    if i < NU:
                        act.wait_ge(sx, i + 1)
                        for b in range(3):
                            n = branch(i, b)[3]
                            nc.scalar.activation(s[:, i % 2, b, 0:n], s[:, i % 2, b, 0:n], ACT.Exp, bias=st[:, i % 4, 0, b:b + 1],
                                                 accum_out=st[:, i % 4, 1, b:b + 1]).then_inc(ex, 1)
                        if units[i][1] == "C":
                            nc.scalar.activation(st[:, i % 4, 3, 0:3], st[:, i % 4, 0, 0:3], ACT.Exp, scale=-1.0,
                                                 bias=tot[:, i % 4, 0:1]).then_inc(ex, 1)
                        else:
                            act.wait_ge(ex, 4 * i + 3)
                            act.sem_inc(ex, 1)
                    if i >= 1:
                        u = i - 1
                        if u >= 2:
                            act.wait_ge(pv, u - 1)
                        for b in range(3):
                            n = branch(u, b)[3]
                            r = min(n, P)
                            c = -(-n // P) * P
                            act.wait_ge(tr, 3 * u + b + 1)
                            nc.scalar.activation(pT[0:r, u % 2, b, 0:c], pX[0:r, (3 * u + b) % 2, 0:c], ACT.Copy).then_inc(tk, 1)

            @block.gpsimd
            def _(pool):
                for u in range(NU):
                    pool.wait_ge(wt, u + 1)
                    for b in range(3):
                        n = branch(u, b)[3]
                        pool.tensor_scalar(s[:, u % 2, b, 0:n], s[:, u % 2, b, 0:n], st[:, u % 4, 2, b:b + 1], None, ALU.mult).then_inc(sd, 1)

            @block.vector
            def _(dve):
                c = Chain(dve, ch)

                def softmax_in(u):
                    dve.wait_ge(sc, u + 1)
                    if u >= 2:
                        dve.wait_ge(tr, 3 * (u - 1))
                    for b in range(3):
                        _, _, _, n, _, slope, dm = branch(u, b)
                        c(dve.scalar_tensor_tensor(s[:, u % 2, b, 0:n], dm, -slope, pS[:, b, 0:n], ALU.mult, ALU.add))
                        c(dve.tensor_reduce(st[:, u % 4, 0, b:b + 1], s[:, u % 2, b, 0:n], AX, ALU.max, negate=True))
                    if units[u][1] == "A":
                        dve.tensor_scalar(st[:, u % 4, 0, 0:1], st[:, u % 4, 0, 0:1], 1e20, None, ALU.min).then_inc(sx, 1)
                    else:
                        dve.tensor_reduce(tot[:, u % 4, 0:1], st[:, u % 4, 0, 0:3], AX, ALU.min).then_inc(sx, 1)

                def weights(u):
                    qt, kind, h = units[u]
                    dve.wait_ge(ex, 4 * u + 4)
                    den, w, e = (st[:, u % 4, j, 0:3] for j in (1, 2, 3))
                    if kind == "A":
                        g = m["gateP"][:, qt, 3 * h:3 * h + 3]
                        c(dve.tensor_scalar(den, den, 1e-30, None, ALU.max))
                        c(dve.reciprocal(den, den))
                        dve.tensor_tensor(w, den, g, ALU.mult).then_inc(wt, 1)
                    else:
                        c(dve.tensor_tensor(den, den, e, ALU.mult))
                        c(dve.tensor_reduce(tot[:, u % 4, 1:2], den, AX, ALU.add))
                        c(dve.reciprocal(tot[:, u % 4, 1:2], tot[:, u % 4, 1:2]))
                        dve.tensor_scalar(w, e, tot[:, u % 4, 1:2], None, ALU.mult).then_inc(wt, 1)

                def output(u):
                    qt, kind, h = units[u]
                    r = slice((h % 2) * HD, (h % 2) * HD + HD)
                    dve.wait_ge(pv, u + 1)
                    dve.tensor_copy(m["oaT" if kind == "A" else "ocT"][r, h // 2, qt * P:(qt + 1) * P], pO[r, u % 2, 0:P]).then_inc(oe, 1)

                for i in range(NU + 3):
                    if i < NU:
                        softmax_in(i)
                    if 1 <= i <= NU:
                        weights(i - 1)
                    if i >= 3:
                        output(i - 3)


def sample_nsa(nc, a, m):
    with ExitStack() as ctx:
        sb = sb_maker(nc, ctx, "sna")
        m = dict(m)
        m["QD"] = sb("QD", [P, DB, 32])
        m["gd"] = sb("gd", [P, 2, 3])
        m["osum"] = sb("osum", [P, 2, P])
        m["selb"] = sb("selb", [P, 2, NBLK])
        m["slope"] = sb("slope", [P, 1])
        sample_compressed(nc, a, m)
        sample_window(nc, a, m)
        sample_selected(nc, a, m)


def sample_compressed(nc, a, m):
    QD, gd, osum, selb = m["QD"], m["gd"], m["osum"], m["selb"]
    with ExitStack() as ctx:
        sem, sb, ps = (f(nc, ctx, "sco") for f in (sem_maker, sb_maker, ps_maker))
        qd = sb("qd", [P, HPG, NS])
        bias = sb("bias", [P, NC_S])
        ovl = sb("ovl", [P, 2, NBLK])
        same = sb("same", [P, P])
        forced = sb("forced", [P, NBLK])
        tri = sb("tri", [P, NBLK, NBLK])
        s = sb("s", [P, 2, NC_S])
        st = sb("st", [P, 2, 2])
        pT = sb("pT", [P, 2, 2, P])
        imp = sb("imp", [P, 2, NBLK])
        score = sb("score", [P, 2, NBLK])
        cmpb = sb("cmpb", [P, NBLK, NBLK])
        rank = sb("rank", [P, 2, NBLK])
        pS = ps("pS", [P, 2, 512])
        pX = ps("pX", [P, 2, 512])
        pI = ps("pI", [P, 2, 512])
        pO = ps("pO", [P, 2, 512])
        loaded, qz, qdd, sc, sx, ex, pn, tr, tk, im, ik, gs, od, ch = (sem(n) for n in (
            "loaded", "qz", "qdd", "sc", "sx", "ex", "pn", "tr", "tk", "im", "ik", "gs", "od", "ch"))
        with nc.Block() as block:

            @block.sync
            def _(sp):
                n = 0
                t = TILE0["qa"] * P
                for g in range(GRP):
                    sp.dma_start(qd[g * HD:(g + 1) * HD, :, :],
                                 a["PT"][t + g * 256:t + (g + 1) * 256, SEQ:NT].rearrange("(n d) t -> d n t", d=HD)).then_inc(loaded, 16)
                    n += 1
                for b in range(DB):
                    for g in range(GRP):
                        p0 = 32 * (b % 4) + 16 * g
                        for q in range(DT):
                            sp.dma_start(gd[p0 + 4 * q:p0 + 4 * q + 4, b // 4, :],
                                         a["GA"][SEQ + b * DT + q, 12 * g:12 * g + 12].rearrange("(n r) -> n r", r=3)).then_inc(loaded, 16)
                            n += 1
                for buf, name in ((bias[:, :], "c_cbias"), (same[:, :], "c_same"), (forced[:, :], "c_forced"),
                                  (m["slope"][:, :], "c_slope")):
                    sp.dma_start(buf, a[name]).then_inc(loaded, 16)
                    n += 1
                sp.dma_start(ovl[:, :, :], a["c_ovl"].rearrange("(h p) j -> p h j", p=P)).then_inc(loaded, 16)
                sp.dma_start(tri[:, :, :], a["c_tri"].partition_broadcast(P)).then_inc(loaded, 16)
            NLOAD = 16 * (2 + 64 + 4 + 2)

            @block.gpsimd
            def _(pool):
                pool.memset(QD[:, :, :], 0.0).then_inc(qz, 1)

            @block.tensor
            def _(pe):
                pe.wait_ge(qdd, 2)
                for b in range(DB):
                    i = pe.matmul(pS[32 * (b % 4):32 * (b % 4) + 32, b // 4, 0:NC_S], QD[:, b, :], m["kcT"][:, b, 0:NC_S], start=True, stop=True)
                    if b % 4 == 3:
                        i.then_inc(sc, 1)
                for g in range(2):
                    pe.wait_ge(pn, g + 1)
                    for h in range(2):
                        n = min(P, NC_S - h * P)
                        i = pe.transpose(pX[0:n, g, h * P:(h + 1) * P], s[:, g, h * P:h * P + n], m["ident"][:, :])
                    i.then_inc(tr, 1)
                for g in range(2):
                    pe.wait_ge(tk, g + 1)
                    for h in range(2):
                        n = min(P, NC_S - h * P)
                        i = pe.matmul(pI[:, g, 0:NBLK], pT[0:n, g, h, :], ovl[0:n, h, :], start=(h == 0), stop=(h == 1))
                    i.then_inc(im, 1)
                for g in range(2):
                    pe.wait_ge(ik, g + 1)
                    pe.matmul(pI[:, g, 128:128 + NBLK], same[:, :], imp[:, g, :], start=True, stop=True).then_inc(gs, 1)
                for g in range(2):
                    for b in range(4):
                        for h in range(2):
                            n = min(P, NC_S - h * P)
                            i = pe.matmul(pO[32 * b:32 * b + 32, g, 0:P], pT[0:n, g, h, 32 * b:32 * b + 32], m["vc"][0:n, 4 * g + b, h, :],
                                          start=(h == 0), stop=(h == 1))
                    i.then_inc(od, 1)

            @block.scalar
            def _(act):
                for g in range(2):
                    act.wait_ge(sx, g + 1)
                    nc.scalar.activation(s[:, g, :], s[:, g, :], ACT.Exp, bias=st[:, g, 0:1], accum_out=st[:, g, 1:2]).then_inc(ex, 1)

            @block.vector
            def _(dve):
                c = Chain(dve, ch)
                dve.wait_ge(loaded, NLOAD)
                dve.wait_ge(qz, 1)
                for g in range(GRP):
                    gp = slice(g * HD, (g + 1) * HD)
                    dve.tensor_scalar(QD[gp, :, 16 * g:16 * g + 16].rearrange("p b (q n) -> p b q n", q=DT),
                                      qd[gp].rearrange("p n (b q) -> p b q n", q=DT), HD ** -0.5, None, ALU.mult).then_inc(qdd, 1)
                for g in range(2):
                    dve.wait_ge(sc, g + 1)
                    c(dve.tensor_tensor(s[:, g, :], pS[:, g, 0:NC_S], bias[:, :], ALU.add))
                    dve.tensor_reduce(st[:, g, 0:1], s[:, g, :], AX, ALU.max, negate=True).then_inc(sx, 1)
                for g in range(2):
                    dve.wait_ge(ex, g + 1)
                    c(dve.reciprocal(st[:, g, 1:2], st[:, g, 1:2]))
                    dve.tensor_scalar(s[:, g, :], s[:, g, :], st[:, g, 1:2], None, ALU.mult).then_inc(pn, 1)
                for g in range(2):
                    dve.wait_ge(tr, g + 1)
                    c(dve.tensor_copy(pT[:, g, 0, :], pX[:, g, 0:P]))
                    n = NC_S - P
                    dve.tensor_copy(pT[0:n, g, 1, :], pX[0:n, g, P:2 * P]).then_inc(tk, 1)
                for g in range(2):
                    dve.wait_ge(im, g + 1)
                    dve.tensor_copy(imp[:, g, :], pI[:, g, 0:NBLK]).then_inc(ik, 1)
                B = [P, NBLK, NBLK]
                for g in range(2):
                    dve.wait_ge(gs, g + 1)
                    c(dve.tensor_tensor(score[:, g, :], pI[:, g, 128:128 + NBLK], forced[:, :], ALU.add))
                    si = score[:, g, :].unsqueeze(1).to_broadcast(B)
                    sj = score[:, g, :].unsqueeze(2).to_broadcast(B)
                    c(dve.tensor_tensor(cmpb[:, :, :], si, sj, ALU.is_equal))
                    c(dve.tensor_tensor(cmpb[:, :, :], cmpb[:, :, :], tri[:, :, :], ALU.mult))
                    c(dve.tensor_reduce(rank[:, g, :], cmpb[:, :, :], AX, ALU.add))
                    c(dve.tensor_tensor(cmpb[:, :, :], si, sj, ALU.is_gt))
                    c(dve.tensor_reduce(selb[:, g, :], cmpb[:, :, :], AX, ALU.add))
                    c(dve.tensor_tensor(rank[:, g, :], rank[:, g, :], selb[:, g, :], ALU.add))
                    c(dve.tensor_scalar(selb[:, g, :], rank[:, g, :], TOPN - 0.5, -BIG, ALU.is_gt, ALU.mult))
                    dve.wait_ge(od, g + 1)
                    c(dve.tensor_scalar(osum[:, g, :], pO[:, g, 0:P], gd[:, g, 0:1], None, ALU.mult))


def sample_window(nc, a, m):
    QD, gd, osum = m["QD"], m["gd"], m["osum"]
    W = 512
    with ExitStack() as ctx:
        sem, sb, ps = (f(nc, ctx, "swi") for f in (sem_maker, sb_maker, ps_maker))
        K = sb("K", [P, DB, 4, P])
        V = sb("V", [P, DB, 4, P])
        KN = sb("KN", [P, NS])
        VN = sb("VN", [DT, DB, P])
        KT = sb("KT", [P, 2, 512])
        s = sb("s", [P, 2, W + DT])
        bias = sb("bias", [P, W + DT])
        pT = sb("pT", [P, 2, 5, P])
        st = sb("st", [P, 2, 3])
        pK = ps("pK", [P, 2, 512])
        pS = ps("pS", [P, 2, 512])
        pN = ps("pN", [P, 512])
        pX = ps("pX", [P, 2, 512])
        pO = ps("pO", [P, 512])
        loaded, kt, kk, sc, scn, sx, ex, tr, tk, od, ch, ok = (sem(n) for n in (
            "loaded", "kt", "kk", "sc", "scn", "sx", "ex", "tr", "tk", "od", "ch", "ok"))
        with nc.Block() as block:

            @block.sync
            def _(sp):
                for b in range(DB):
                    for v, buf in ((0, K), (1, V)):
                        for g in range(GRP):
                            sp.dma_start(buf[:, b, :, g * HD:(g + 1) * HD], a["cache_nsa_win"][0, b, v, g].rearrange("(p l) d -> p l d", l=4)).then_inc(loaded, 16)
                t = TILE0["kvw"] * P
                sp.dma_start(KN[:, :], a["PT"][t:t + P, SEQ:NT]).then_inc(loaded, 16)
                c = TM_COL["win"] + P
                sp.dma_start(VN[:, :, :], a["TM"][SEQ:NT, c:c + P].rearrange("(b q) c -> q b c", q=DT)).then_inc(loaded, 16)
                sp.dma_start(bias[:, :], a["c_wbias"]).then_inc(loaded, 16)
            NLOAD = 16 * (4 * DB + 3)

            @block.tensor
            def _(pe):
                pe.wait_ge(loaded, NLOAD)

                def score(b):
                    pe.wait_ge(kk, b + 1)
                    if b >= 2:
                        pe.wait_ge(sx, b - 1)
                    pe.matmul(pS[32 * (b % 4):32 * (b % 4) + 32, b % 2, :], QD[:, b, :], KT[:, b % 2, :], start=True, stop=True).then_inc(sc, 1)

                for b in range(DB):
                    if b >= 2:
                        pe.wait_ge(kk, b - 1)
                    for l in range(4):
                        i = pe.transpose(pK[:, b % 2, l * P:(l + 1) * P], K[:, b, l, :], m["ident"][:, :])
                    i.then_inc(kt, 1)
                    if b:
                        score(b - 1)
                score(DB - 1)
                for b in range(DB):
                    i = pe.matmul(pN[32 * (b % 4):32 * (b % 4) + 32, 8 * (b // 4):8 * (b // 4) + DT], QD[:, b, :], KN[:, b * DT:(b + 1) * DT], start=True, stop=True)
                i.then_inc(scn, 1)
                for g in range(2):
                    pe.wait_ge(ex, g + 1)
                    if g:
                        pe.wait_ge(tk, 2)
                    for l in range(4):
                        i = pe.transpose(pX[:, 0, l * P:(l + 1) * P], s[:, g, l * P:(l + 1) * P], m["ident"][:, :])
                    i = pe.transpose(pX[0:DT, 1, 0:P], s[:, g, W:W + DT], m["ident"][:, :])
                    i.then_inc(tr, 1)
                    pe.wait_ge(tk, 2 * g + 2)
                    if g:
                        pe.wait_ge(ok, 1)
                    for b in range(4):
                        o = pO[32 * b:32 * b + 32, 0:P]
                        rows = slice(32 * b, 32 * b + 32)
                        for l in range(4):
                            pe.matmul(o, pT[:, g, l, rows], V[:, 4 * g + b, l, :], start=(l == 0), stop=False)
                        i = pe.matmul(o, pT[0:DT, g, 4, rows], VN[:, 4 * g + b, :], start=False, stop=True)
                    i.then_inc(od, 1)

            @block.scalar
            def _(act):
                for g in range(2):
                    act.wait_ge(sx, DB + g + 1)
                    nc.scalar.activation(s[:, g, :], s[:, g, :], ACT.Exp, bias=st[:, g, 0:1], accum_out=st[:, g, 1:2]).then_inc(ex, 1)

            @block.vector
            def _(dve):
                c = Chain(dve, ch)

                def score(b):
                    r = slice(32 * (b % 4), 32 * (b % 4) + 32)
                    dve.wait_ge(sc, b + 1)
                    dve.tensor_tensor(s[r, b // 4, 0:W], pS[r, b % 2, :], bias[r, 0:W], ALU.add).then_inc(sx, 1)

                dve.wait_ge(loaded, NLOAD)
                for b in range(DB):
                    dve.wait_ge(kt, b + 1)
                    if b >= 2:
                        dve.wait_ge(sc, b - 1)
                    dve.tensor_copy(KT[:, b % 2, :], pK[:, b % 2, :]).then_inc(kk, 1)
                    if b:
                        score(b - 1)
                score(DB - 1)
                dve.wait_ge(scn, 1)
                dve.wait_ge(sx, DB)
                for g in range(2):
                    c(dve.tensor_tensor(s[:, g, W:W + DT], pN[:, 8 * g:8 * g + DT], bias[:, W:W + DT], ALU.add))
                    dve.tensor_reduce(st[:, g, 0:1], s[:, g, :], AX, ALU.max, negate=True).then_inc(sx, 1)
                for g in range(2):
                    dve.wait_ge(tr, g + 1)
                    dve.tensor_copy(pT[:, g, 0:4, :], pX[:, 0, :].rearrange("p (l r) -> p l r", l=4)).then_inc(tk, 1)
                    dve.tensor_copy(pT[0:DT, g, 4, :], pX[0:DT, 1, 0:P]).then_inc(tk, 1)
                    c(dve.reciprocal(st[:, g, 1:2], st[:, g, 1:2]))
                    c(dve.tensor_tensor(st[:, g, 2:3], st[:, g, 1:2], gd[:, g, 2:3], ALU.mult))
                    dve.wait_ge(od, g + 1)
                    c(dve.scalar_tensor_tensor(osum[:, g, :], pO[:, 0:P], st[:, g, 2:3], osum[:, g, :], ALU.mult, ALU.add))
                    dve.sem_inc(ok, 1)


def sample_selected(nc, a, m):
    QD, gd, osum, selb, idx = m["QD"], m["gd"], m["osum"], m["selb"], m["idx"]
    NKS = 2
    with ExitStack() as ctx:
        sem, sb, ps = (f(nc, ctx, "ssl") for f in (sem_maker, sb_maker, ps_maker))
        K = sb("K", [P, NKS, 2, 1024])
        KR = sb("KR", [P, 2, 16, P])
        V = sb("V", [P, 4, 2, 2, 1024])
        KN = sb("KN", [P, NS])
        VN = sb("VN", [DT, DB, P])
        KT = sb("KT", [P, 2, 512])
        s = sb("s", [P, PAST + DT])
        nbias = sb("nbias", [P, DT])
        pn = sb("pn", [DT, P])
        pT = KT
        st = sb("st", [P, 2, 3])
        rel = m["hT"][:, :, :].rearrange("p k t -> p (k t)")[:, 0:PAST]
        pK = ps("pK", [P, 2, 512])
        pS = ps("pS", [P, 2, 512])
        pN = ps("pN", [P, 512])
        pO = ps("pO", [P, 512])
        pF = ps("pF", [P, 2, 512])
        loaded, kt, kk, sc, sx, scn, snk, mx, ex, tr, tk, od, ok, ch, ft, kr = (sem(n) for n in (
            "loaded", "kt", "kk", "sc", "sx", "scn", "snk", "mx", "ex", "tr", "tk", "od", "ok", "ch", "ft", "kr"))
        kg = [sem(f"kg{i}") for i in range(NKS)]
        vg = [sem(f"vg{i}") for i in range(4)]
        NU = 64
        with nc.Block() as block:

            @block.sync
            def _(sp):
                t = TILE0["kvs"] * P
                sp.dma_start(KN[:, :], a["PT"][t:t + P, SEQ:NT]).then_inc(loaded, 16)
                c = TM_COL["slc"] + P
                sp.dma_start(VN[:, :, :], a["TM"][SEQ:NT, c:c + P].rearrange("(b q) c -> q b c", q=DT)).then_inc(loaded, 16)
                sp.dma_start(rel, a["c_rel"].partition_broadcast(P)).then_inc(loaded, 16)
                sp.dma_start(nbias[:, :], a["c_nbias"]).then_inc(loaded, 16)

            @block.gpsimd
            def _(pool):
                src = a["cache_nsa_slc"][0].rearrange("n v g (c l) d -> (n v g c) (l d)", l=16)

                def gather(dst, c, h, done):
                    pool.indirect_dma_start(out=dst, out_offset=None, in_=src,
                                            in_offset=bass.IndirectOffsetOnAxis(ap=idx[:, c, h:h + 1], axis=0)).then_inc(done, 16)

                for b in range(DB):
                    for h in range(2):
                        u = 2 * b + h
                        if u >= NKS:
                            pool.wait_ge(kr, u - NKS + 1)
                        for g in range(GRP):
                            gather(K[:, u % NKS, g, :], g, u, kg[u % NKS])
                    if b == 4:
                        pool.wait_ge(od, 1)
                    for h in range(2):
                        for g in range(GRP):
                            gather(V[:, b % 4, h, g, :], 2 + g, 2 * b + h, vg[b % 4])

            @block.tensor
            def _(pe):
                pe.wait_ge(loaded, 64)

                def turn(w):
                    u, lq = w // 4, w % 4
                    if lq == 0:
                        pe.wait_ge(kr, u + 1)
                    k = w + (w // 32) * 8
                    if k >= 2:
                        pe.wait_ge(kk, k - 1)
                    for j in range(4):
                        l = 4 * lq + j
                        i = pe.transpose(pK[:, k % 2, j * P:(j + 1) * P], KR[:, u % 2, l, :], m["ident"][:, :])
                    i.then_inc(kt, 1)

                def score(w):
                    b = w // 8
                    k = w + (w // 32) * 8
                    pe.wait_ge(kk, k + 1)
                    if w >= 2:
                        pe.wait_ge(sx, w - 1)
                    pe.matmul(pS[32 * (b % 4):32 * (b % 4) + 32, w % 2, :], QD[:, b, :], KT[:, k % 2, :], start=True, stop=True).then_inc(sc, 1)

                for g in range(2):
                    if g:
                        pe.wait_ge(snk, 1)
                    for b in range(4 * g, 4 * g + 4):
                        i = pe.matmul(pN[32 * (b % 4):32 * (b % 4) + 32, 0:DT], QD[:, b, :], KN[:, b * DT:(b + 1) * DT], start=True, stop=True)
                    i.then_inc(scn, 1)
                    turn(32 * g)
                    for w in range(32 * g, 32 * g + 32):
                        if w + 1 < 32 * g + 32:
                            turn(w + 1)
                        score(w)
                    pe.wait_ge(ex, g + 1)
                    pe.transpose(pN[0:DT, 128:256], s[:, PAST:PAST + DT], m["ident"][:, :]).then_inc(tr, 1)
                    for b in range(4):
                        pe.wait_ge(vg[b], 64 * (g + 1))
                    if g:
                        pe.wait_ge(ok, 1)

                    def turn_p(t):
                        k = 40 * g + 32 + t
                        pe.wait_ge(kk, k - 1)
                        for j in range(4):
                            n = 4 * t + j
                            i = pe.transpose(pK[:, k % 2, j * P:(j + 1) * P], s[:, n * P:(n + 1) * P], m["ident"][:, :])
                        i.then_inc(tr, 1)

                    def values(t):
                        k = 40 * g + 32 + t
                        pe.wait_ge(kk, k + 1)
                        for b in range(4):
                            for j in range(4):
                                n = 4 * t + j
                                h, l = n // 16, n % 16
                                
                                i = pe.matmul(pO[32 * b:32 * b + 32, 0:P], pT[:, k % 2, j * P + 32 * b:j * P + 32 * b + 32],
                                              V[:, b, h, :, l * HD:(l + 1) * HD], start=(n == 0), stop=False)
                        i.then_inc(tk, 1)

                    turn_p(0)
                    for t in range(8):
                        if t + 1 < 8:
                            turn_p(t + 1)
                        values(t)
                    pe.wait_ge(snk, g + 1)
                    for b in range(4):
                        i = pe.matmul(pO[32 * b:32 * b + 32, 0:P], pn[0:DT, 32 * b:32 * b + 32], VN[:, 4 * g + b, :], start=False, stop=True)
                    i.then_inc(od, 1)
                pe.wait_ge(ok, 2)
                for g in range(2):
                    i = pe.transpose(pF[:, g, 0:P], osum[:, g, :], m["ident"][:, :])
                i.then_inc(ft, 1)

            @block.scalar
            def _(act):
                for g in range(2):
                    for u in range(8 * g, 8 * g + 8):
                        act.wait_ge(kg[u % NKS], 32 * (u // NKS + 1))
                        if u >= 2:
                            act.wait_ge(kt, 4 * (u - 1))
                        nc.scalar.activation(KR[:, u % 2].rearrange("p l (g d) -> p g l d", g=GRP),
                                             K[:, u % NKS].rearrange("p g (l d) -> p g l d", l=16), ACT.Copy).then_inc(kr, 1)
                    act.wait_ge(mx, g + 1)
                    nc.scalar.activation(s[:, :], s[:, :], ACT.Exp, bias=st[:, g, 0:1], accum_out=st[:, g, 1:2]).then_inc(ex, 1)

            @block.vector
            def _(dve):
                c = Chain(dve, ch)
                dve.wait_ge(loaded, 64)

                def keep(k, last_read):
                    last_read()
                    dve.tensor_copy(KT[:, k % 2, :], pK[:, k % 2, :]).then_inc(kk, 1)

                def score(w):
                    b = w // 8
                    r = slice(32 * (b % 4), 32 * (b % 4) + 32)
                    dve.wait_ge(sc, w + 1)
                    if w % 8 == 0 and w >= 32:
                        dve.wait_ge(tr, 9 * (w // 32))
                    dve.scalar_tensor_tensor(s[r, (w % 8) * 512:(w % 8 + 1) * 512], rel[r, (w % 8) * 512:(w % 8 + 1) * 512],
                                             m["slope"][r, :], pS[r, w % 2, :], ALU.mult, ALU.add).then_inc(sx, 1)

                for g in range(2):
                    for w in range(32 * g, 32 * g + 32):
                        dve.wait_ge(kt, w + 1)
                        k = w + 8 * g

                        def free():
                            if w - 32 * g >= 2:
                                dve.wait_ge(sc, w - 1)
                            elif g:
                                dve.wait_ge(tk, 7 + (w - 32 * g))
                        keep(k, free)
                        if w > 32 * g:
                            score(w - 1)
                    score(32 * g + 31)
                    dve.wait_ge(scn, g + 1)
                    dve.wait_ge(sx, 32 * g + 32)
                    c(dve.tensor_tensor(s[:, PAST:PAST + DT], pN[:, 0:DT], nbias[:, :], ALU.add))
                    c(dve.tensor_scalar(s[:, PAST:PAST + DT], s[:, PAST:PAST + DT], selb[:, g, NBLK - 1:NBLK], None, ALU.add))
                    for h in range(2):
                        v = s[:, h * 2048:(h + 1) * 2048].rearrange("p (l j i) -> p l j i", l=16, i=4)
                        sel = selb[:, g, 32 * h:32 * h + 32].unsqueeze(1).unsqueeze(3).to_broadcast([P, 16, 32, 4])
                        c(dve.tensor_tensor(v, v, sel, ALU.add))
                    dve.tensor_reduce(st[:, g, 0:1], s[:, :], AX, ALU.max, negate=True).then_inc(mx, 1)
                    dve.wait_ge(tr, 9 * g + 1)
                    if g:
                        dve.wait_ge(od, g)
                    dve.tensor_copy(pn[:, :], pN[0:DT, 128:256]).then_inc(snk, 1)
                    for t in range(8):
                        dve.wait_ge(tr, 9 * g + 2 + t)

                        def free():
                            if t >= 2:
                                dve.wait_ge(tk, 8 * g + t - 1)
                            else:
                                dve.wait_ge(sc, 32 * g + 31 + t)
                        keep(40 * g + 32 + t, free)
                    c(dve.reciprocal(st[:, g, 1:2], st[:, g, 1:2]))
                    c(dve.tensor_tensor(st[:, g, 2:3], st[:, g, 1:2], gd[:, g, 1:2], ALU.mult))
                    dve.wait_ge(od, g + 1)
                    dve.scalar_tensor_tensor(osum[:, g, :], pO[:, 0:P], st[:, g, 2:3], osum[:, g, :], ALU.mult, ALU.add).then_inc(ok, 1)
                dve.wait_ge(ft, 1)
                for f in range(2):
                    for g in range(GRP):
                        for n in range(HPG):
                            r = slice((n % 2) * HD, (n % 2) * HD + HD)
                            src = pF[g * HD:(g + 1) * HD, f, 0:P].rearrange("p (b g q n) -> p g n b q", b=4, g=2, q=DT)[:, g, n]
                            dst = m["oaT"][r, 2 * g + n // 2, SEQ + 16 * f:SEQ + 16 * f + 16].rearrange("p (b q) -> p b q", q=DT)
                            dve.tensor_copy(dst, src)


def sample_dilated(nc, a, m):
    NK = 129
    with ExitStack() as ctx:
        sem, sb, ps = (f(nc, ctx, "sdi") for f in (sem_maker, sb_maker, ps_maker))
        K = sb("K", [P, NK, HD])
        V = sb("V", [P, NK, HD])
        tmp = sb("tmp", [P, NK * HD])
        qf = sb("qf", [P, 6, NS])
        qt = sb("qt", [NS, 768])
        q = sb("q", [P, 3, HD])
        bias = sb("bias", [P, 3, NK])
        s = sb("s", [P, 3, NK])
        st = sb("st", [P, 4, 3])
        tot = sb("tot", [P, 2])
        o = sb("o", [P, 3, HD])
        oo = sb("oo", [P, HD])
        pq = ps("pq", [P, 2, 512])
        pf = ps("pf", [P, 512])
        fl, qtr, qk, qst, loaded, qkd, pvd, sx, ex, ch, fin, ft = (sem(n) for n in (
            "fl", "qtr", "qk", "qst", "loaded", "qkd", "pvd", "sx", "ex", "ch", "fin", "ft"))
        kl, vl = sem("kl"), sem("vl")

        def rows(sp, g, v, buf, done):
            cache, (win, dil) = a[f"cache_dil{g}"][0], DIL[g]
            c = TM_COL["kc" if v == 0 else "vc"] + 256 * g
            n = 0
            if g == 0:
                for t in range(DT):
                    for b in range(DB):
                        p0 = 16 * b + t
                        sp.dma_start(buf[p0:p0 + 13:4, 0:win - t, :], cache[b, v, :, t:win, :]).then_inc(done, 16)
                        new = a["TM"][SEQ + b * DT:SEQ + b * DT + t + 1, c:c + 256].rearrange("i (h d) -> h i d", h=4)
                        sp.dma_start(buf[p0:p0 + 13:4, win - t:NK, :], new).then_inc(done, 16)
                        n += 2
            else:
                for b in range(DB):
                    for h in range(4):
                        p0 = 16 * b + 4 * h
                        src = cache[b, v, h].rearrange("(i r) d -> r i d", r=dil)[0:DT]
                        sp.dma_start(buf[p0:p0 + DT, 0:NK - 1, :], src).then_inc(done, 16)
                        sp.dma_start(buf[p0:p0 + DT, NK - 1, :], a["TM"][SEQ + b * DT:SEQ + b * DT + DT, c + h * HD:c + (h + 1) * HD]).then_inc(done, 16)
                        n += 2
            return n

        with nc.Block() as block:

            @block.sync
            def _(sp):
                t = TILE0["qc"] * P
                sp.dma_start(qf[:, :, :], a["PT"][t:t + 768, SEQ:NT].rearrange("(n p) t -> p n t", p=P)).then_inc(fl, 16)
                sp.dma_start(bias[:, :, :], a["c_dbias"]).then_inc(loaded, 16)
                rows(sp, 0, 0, K, kl)
                sp.wait_ge(qk, 2)
                sp.dma_start(a["QC"], qt[:, :]).then_inc(qst, 16)
                sp.wait_ge(qst, 16)
                for b in range(DB):
                    for h in range(4):
                        sp.dma_start(q[16 * b + 4 * h:16 * b + 4 * h + 4, :, :],
                                     a["QC"][b * DT:(b + 1) * DT].rearrange("q (g h d) -> q g h d", g=3, h=4)[:, :, h, :]).then_inc(loaded, 16)
                for g in range(1, 3):
                    sp.wait_ge(qkd, g)
                    rows(sp, g, 0, K, kl)

            @block.scalar
            def _(act):
                rows(act, 0, 1, V, vl)
                for g in range(3):
                    act.wait_ge(sx, g + 1)
                    nc.scalar.activation(s[:, g, :], s[:, g, :], ACT.Exp, bias=st[:, 0, g:g + 1], accum_out=st[:, 1, g:g + 1]).then_inc(ex, 1)
                    if g < 2:
                        act.wait_ge(pvd, g + 1)
                        rows(act, g + 1, 1, V, vl)
                act.wait_ge(sx, 4)
                nc.scalar.activation(st[:, 3, :], st[:, 0, :], ACT.Exp, scale=-1.0, bias=tot[:, 0:1]).then_inc(ex, 1)

            @block.tensor
            def _(pe):
                pe.wait_ge(fl, 16)
                for n in range(6):
                    i = pe.transpose(pq[0:NS, n // 4, (n % 4) * P:(n % 4 + 1) * P], qf[:, n, :], m["ident"][:, :])
                i.then_inc(qtr, 1)
                pe.wait_ge(fin, 1)
                pe.transpose(pf[0:HD, 0:P], oo[:, :], m["ident"][:, :]).then_inc(ft, 1)

            @block.vector
            def _(dve):
                c = Chain(dve, ch)
                dve.wait_ge(qtr, 1)
                dve.tensor_scalar(qt[:, 0:512], pq[0:NS, 0, :], HD ** -0.5, None, ALU.mult).then_inc(qk, 1)
                dve.tensor_scalar(qt[:, 512:768], pq[0:NS, 1, 0:256], HD ** -0.5, None, ALU.mult).then_inc(qk, 1)
                dve.wait_ge(loaded, 16 * 33)
                for g in range(3):
                    dve.wait_ge(kl, 16 * 64 * (g + 1))
                    t3 = tmp[:, :].rearrange("p (n d) -> p n d", d=HD)
                    c(dve.tensor_tensor(t3, K[:, :, :], q[:, g, :].unsqueeze(1).to_broadcast([P, NK, HD]), ALU.mult))
                    dve.sem_inc(qkd, 1)
                    c(dve.tensor_reduce(s[:, g, :], t3, AX, ALU.add))
                    c(dve.tensor_tensor(s[:, g, :], s[:, g, :], bias[:, g, :], ALU.add))
                    dve.tensor_reduce(st[:, 0, g:g + 1], s[:, g, :], AX, ALU.max, negate=True).then_inc(sx, 1)
                    dve.wait_ge(ex, g + 1)
                    dve.wait_ge(vl, 16 * 64 * (g + 1))
                    t3 = tmp[:, :].rearrange("p (d n) -> p d n", d=HD)
                    c(dve.tensor_tensor(t3, V[:, :, :].rearrange("p n d -> p d n"), s[:, g, :].unsqueeze(1).to_broadcast([P, HD, NK]), ALU.mult))
                    dve.sem_inc(pvd, 1)
                    c(dve.tensor_reduce(o[:, g, :], t3, AX, ALU.add))
                dve.tensor_reduce(tot[:, 0:1], st[:, 0, :], AX, ALU.min).then_inc(sx, 1)
                dve.wait_ge(ex, 4)
                c(dve.tensor_tensor(st[:, 1, :], st[:, 1, :], st[:, 3, :], ALU.mult))
                c(dve.tensor_reduce(tot[:, 1:2], st[:, 1, :], AX, ALU.add))
                c(dve.reciprocal(tot[:, 1:2], tot[:, 1:2]))
                c(dve.tensor_scalar(st[:, 2, :], st[:, 3, :], tot[:, 1:2], None, ALU.mult))
                c(dve.tensor_scalar(oo[:, :], o[:, 0, :], st[:, 2, 0:1], None, ALU.mult))
                c(dve.scalar_tensor_tensor(oo[:, :], o[:, 1, :], st[:, 2, 1:2], oo[:, :], ALU.mult, ALU.add))
                dve.scalar_tensor_tensor(oo[:, :], o[:, 2, :], st[:, 2, 2:3], oo[:, :], ALU.mult, ALU.add).then_inc(fin, 1)
                dve.wait_ge(ft, 1)
                for h in range(4):
                    r = slice((h % 2) * HD, (h % 2) * HD + HD)
                    src = pf[0:HD, 0:P].rearrange("p (b h q) -> p h b q", b=DB, h=4)[:, h]
                    dve.tensor_copy(m["ocT"][r, h // 2, SEQ:NT].rearrange("p (b q) -> p b q", q=DT), src)


def build(nc, a):
    with ExitStack() as ctx:
        def sb(name, shape, dt=F32):
            return ctx.enter_context(nc.sbuf_tensor(name, shape, dt))

        m = {
            "ident": sb("ident", [P, P]), "headones": sb("headones", [P, P]),
            "reset": sb("reset", [P, SEQ]), "prm": sb("prm", [P, NPROW]), "gateP": sb("gateP", [P, 4, 24]),

            "xT": sb("xT", [P, KD, NT]), "modT": sb("modT", [P, MODT, 1 + DB]), "hT": sb("hT", [P, KD, NT]),
            "oaT": sb("oaT", [P, 4, NT]), "obT": sb("obT", [P, 4, NT]), "ocT": sb("ocT", [P, 2, NT]),
        }
        phases = PHASES
        for name in ("copied", "token_rows_out", "sample_state_out", "prompt_state_out", "y_out0", "y_out1"):
            m[name] = ctx.enter_context(nc.semaphore(name))
        for phase in phases:
            if phase is compress:
                m["kcT"] = sb("kcT", [P, DB + 1, 256])
                m["vc"] = sb("vc", [P, DB + 1, 2, P])
                m["idx"] = sb("idx", [P, 4, 2 * DB], I32)
            phase(nc, a, m)
        finish(nc, m)


def finish(nc, m):
    with nc.Block() as block:

        @block.gpsimd
        def _(pool):
            pool.wait_ge(m["copied"], 16 * 4)


PHASES = [conditioning, in_projection, token_major, rwkv, compress, prompt_attention, sample_nsa, sample_dilated, merge, feed_forward]


def constants():
    c = {}
    c["ident"] = np.eye(P, dtype=np.float32)
    c["headones"] = np.kron(np.eye(2), np.ones((HD, HD))).astype(np.float32)
    c["reset"] = np.tile((np.arange(SEQ) % CH != 0).astype(np.float32), (P, 1))
    s, t = np.arange(P)[:, None], np.arange(P)[None, :]
    mk = [((s // (2 * n) == t // (2 * n)) & (s // n % 2 == 0) & (t // n % 2 == 1)) for n in (1, 2, 4, 8, 16, 32)]
    mk += [(s // CH == t // CH) & (s < t), (s // CH == t // CH) & (s <= t), mk[0].T]
    c["masks"] = np.stack(mk).astype(np.float32)
    c["lane"] = (np.arange(P, dtype=np.int32) % 8).reshape(P, 1)
    rel = np.arange(P)[:, None] - np.arange(SEQ)[None, :] + SEQ - P
    ok = [rel >= 0] + [(rel >= 0) & (rel <= w) & (rel % d == 0) for w, d in DIL]
    c["dist"] = np.stack([np.where(o, rel, BIG) for o in ok]).astype(np.float32)
    rel = np.arange(SEQ).reshape(4, P, 1) - (16 * np.arange(32) + 31)
    c["distc"] = np.where(rel >= 0, rel, BIG).astype(np.float32)
    r = np.arange(P)
    q, slope = r // 4 % 4, np.array(slopes(8))[r // 16 % 2 * 4 + r % 4]
    c["slope"] = slope.reshape(P, 1).astype(np.float32)
    c["cbias"] = (-slope[:, None] * (PAST + q[:, None] - 16 * np.arange(NC_S) - 31)).astype(np.float32)
    c["same"] = (r[:, None] // 4 == r[None, :] // 4).astype(np.float32)
    w, j = np.arange(2 * P)[:, None] * 16, np.arange(NBLK)[None, :] * 64
    c["ovl"] = ((w < j + 64) & (w + 31 >= j)).astype(np.float32)
    c["forced"] = np.tile(1e4 * np.isin(np.arange(NBLK), (0, NBLK - 2, NBLK - 1)), (P, 1)).astype(np.float32)
    c["tri"] = np.tril(np.ones((NBLK, NBLK)), -1).astype(np.float32)
    x = np.concatenate([(4 * np.arange(P)[None, :] + np.arange(4)[:, None]).ravel(), 512 + np.arange(DT)])
    rel = 512 + q[:, None] - x[None, :]
    c["wbias"] = np.where((rel >= 0) & (rel <= 512), -slope[:, None] * rel, -BIG).astype(np.float32)
    tok = 2048 * np.arange(2)[:, None, None] + 16 * np.arange(P)[None, None, :] + np.arange(16)[None, :, None]
    c["rel"] = (tok.ravel() - PAST).astype(np.float32)
    d = q[:, None] - np.arange(DT)
    c["nbias"] = np.where(d >= 0, slope[:, None] * np.arange(DT), -BIG).astype(np.float32)
    h = r // 4 % 4
    c["dbias"] = np.stack([-np.array(slopes(12))[4 * g + h][:, None] * d * (128 - np.arange(129))
                           for g, (_, d) in enumerate(DIL)], 1).astype(np.float32)
    return c


_INS = ["x_prompt", "x_sample", "cache_nsa_cmp", "cache_nsa_slc", "cache_nsa_win", "state_rwkv",
        "state_rwkv_shift", "cache_dil0", "cache_dil1", "cache_dil2", "page_table", "c_prompt", "c_sample",
        "w_ada", "b_ada", "w_in", "phi_w1", "phi_pe", "phi_w2", "rw_mu", "rw_w0", "rw_w2", "rw_a0", "rw_a2",
        "rw_g2", "rw_kk", "rw_ka", "rw_rk", "rw_gn_g", "rw_gn_b", "w_br_a", "w_br_b", "w_br_c", "w_o",
        "ln1_g", "ln1_b", "ln2_g", "ln2_b", "w_ffn1", "w_ffn2"]
_OUTS = [((1, 512, 1024), "y_p"), ((8, 4, 1024), "y_s"),
         ((1, 1, 2, 2, 512, 64), "cmp_p"), ((1, 8, 2, 2, 4, 64), "cmp_s"),
         ((1, 1, 2, 2, 512, 64), "slc_p"), ((1, 8, 2, 2, 4, 64), "slc_s"),
         ((1, 1, 2, 2, 512, 64), "win_p"), ((1, 8, 2, 2, 512, 64), "win_s"),
         ((1, 1, 8, 64, 64), "rwkv_p"), ((1, 8, 8, 64, 64), "rwkv_s"),
         ((1, 1, 1, 1792), "shift_p"), ((1, 8, 1, 1792), "shift_s"),
         ((1, 1, 2, 4, 128, 64), "dil0_p"), ((1, 8, 2, 4, 128, 64), "dil0_s"),
         ((1, 1, 2, 4, 512, 64), "dil1_p"), ((1, 8, 2, 4, 512, 64), "dil1_s"),
         ((1, 1, 2, 4, 512, 64), "dil2_p"), ((1, 8, 2, 4, 2048, 64), "dil2_s")]
_SCRATCH = [("PT", (NTILE * P, NT)), ("TM", (NT, TM_W)), ("GA", (NT, 24)), ("PBS", (33, SHIFT_W)),
            ("DQ", (NS, 6, 512)), ("OD", (NS, 512)), ("QC", (NS, 768))]


def kernel(**inputs):
    import concourse.bacc as _bacc
    from concourse.bass_utils import run_bass_kernel_spmd as _run

    nc = _bacc.Bacc("TRN2", target_bir_lowering=False, num_devices=1)
    arrays, args = {}, {}
    named = {n: np.ascontiguousarray(inputs[n]) for n in _INS}
    named["page_lanes"] = np.ascontiguousarray(np.repeat(named.pop("page_table").reshape(2 * DB, NPAGE // 2).T, 8, axis=0))
    named.update({f"c_{n}": v for n, v in constants().items()})
    for name, v in named.items():
        arrays[f"in_{name}_dram"] = v
        args[name] = nc.dram_tensor(f"in_{name}_dram", v.shape, mybir.dt.from_np(v.dtype), kind="ExternalInput").ap()
    for i, (shape, name) in enumerate(_OUTS):
        args["o_" + name] = nc.dram_tensor(f"out_{i}_dram", shape, F32, kind="ExternalOutput").ap()
    for name, shape in _SCRATCH:
        args[name] = nc.dram_tensor(name, shape, F32).ap()
    build(nc, args)
    r = _run(nc, [arrays], core_ids=[0])
    return tuple(r.results[0][f"out_{i}_dram"] for i in range(len(_OUTS)))
```

```python
import math
from contextlib import ExitStack

import numpy as np

import concourse.bass as bass
from concourse import mybir

P = 128
D = 1024
KD = D // P
SEQ = 512
DB, DT = 8, 4
NS = DB * DT
NT = SEQ + NS
HN = NT // 2
HD = 64
PAST = 4096
PAGE = 128
NPAGE = PAST // PAGE
GRP = 2
HPG = 4
SHIFT_W = 1792
FF = 2816
ALPHA = 2.0 ** 0.25
GN_EPS = 64e-5
LN_EPS = 1e-5
BIG = 1e30
DIL = ((128, 1), (512, 4), (2048, 16))
NC_P = (SEQ - 32) // 16 + 1
NC_S = (PAST + DT - 32) // 16 + 1
NBLK = PAST // 64 + 1
TOPN = 16
MODT = 6 * KD

F32 = mybir.dt.float32
I32 = mybir.dt.int32
F32R = mybir.dt.float32r
ALU = mybir.AluOpType
ACT = mybir.ActivationFunctionType
AX = mybir.AxisListType.X

SEGMENTS = [
    ("qa", 0, 512), ("kvc", 512, 256), ("kvs", 768, 256), ("kvw", 1024, 256), ("ga", 1280, 24),
    ("pb", 1304, 1792), ("qc", 3096, 768), ("kc", 3864, 768), ("vc", 4632, 768), ("gm", 5400, 3072),
]
TILE0 = {}
GROUPS = []
_t = 0
for _n, _c, _w in SEGMENTS:
    TILE0[_n] = _t
    for _o in range(0, _w, 512):
        GROUPS.append((_c + _o, min(512, _w - _o), _t + _o // P))
    _t += -(-_w // P)
NTILE = _t

TM_TILES = [TILE0["kvc"] + i for i in range(6)] + [TILE0["kc"] + i for i in range(12)]
TM_W = len(TM_TILES) * P
TM_COL = {"cmp": 0, "slc": 256, "win": 512, "kc": 768, "vc": 1536}

PROWS = [("rw_mu", 14), ("rw_w0", 4), ("rw_a0", 4), ("rw_kk", 4), ("rw_ka", 4), ("rw_rk", 4),
         ("rw_gn_g", 4), ("rw_gn_b", 4), ("ln1_g", 8), ("ln1_b", 8), ("ln2_g", 8), ("ln2_b", 8),
         ("b_ada", 48)]
PROW = {}
_r = 0
for _n, _c in PROWS:
    PROW[_n] = _r
    _r += _c
NPROW = _r


def slopes(n):
    return [2.0 ** (-8.0 * (i + 1) / n) for i in range(n)]


class Chain:

    def __init__(self, eng, sem):
        self.eng, self.sem, self.n = eng, sem, 0

    def __call__(self, ins):
        ins.then_inc(self.sem, 1)
        self.n += 1
        self.eng.wait_ge(self.sem, self.n)


def sem_maker(nc, ctx, phase):
    held = []

    def clear():
        nc.clear_and_free_semaphores(held)
        nc.all_engine_barrier()

    def make(name):
        held.append(nc.alloc_semaphore(f"{phase}_{name}"))
        return held[-1]

    ctx.callback(clear)
    return make


def sb_maker(nc, ctx, phase):
    return lambda name, shape, dt=F32: ctx.enter_context(nc.sbuf_tensor(f"{phase}_{name}", shape, dt))


def ps_maker(nc, ctx, phase):
    return lambda name, shape: ctx.enter_context(nc.psum_tensor(f"{phase}_{name}", shape, F32))


def conditioning(nc, a, m):
    NG = 2 * KD * P // 512
    with ExitStack() as ctx:
        sem, sb, ps = (f(nc, ctx, "ada") for f in (sem_maker, sb_maker, ps_maker))
        xtok = sb("xtok", [P, 5, D])
        c9 = sb("c9", [1 + DB, D])
        prow = sb("prow", [NPROW, P])
        wada = sb("wada", [P, 3, KD, 512])
        cT = m["cT"]
        psx = ps("psx", [P, 2, 512])
        psd = ps("psd", [P, KD, NS])
        psc = ps("psc", [P, 512])
        psm = ps("psm", [P, 2, 512])
        loaded = sem("loaded")
        w_in = [sem(f"w{i}") for i in range(3)]
        silu = sem("silu")
        xps, xev, cps, cev, mps, mev = (sem(s) for s in ("xps", "xev", "cps", "cev", "mps", "mev"))
        vch = sem("vch")
        w_r = a["w_ada"][0].rearrange("(k p) n -> p k n", p=P)
        with nc.Block() as block:

            @block.sync
            def _(sp):
                sp.dma_start(m["ident"][:, :], a["c_ident"]).then_inc(loaded, 16)
                sp.dma_start(m["headones"][:, :], a["c_headones"]).then_inc(loaded, 16)
                sp.dma_start(m["reset"][:, :], a["c_reset"]).then_inc(loaded, 16)
                sp.dma_start(c9[0:1, :], a["c_prompt"]).then_inc(loaded, 16)
                sp.dma_start(c9[1:1 + DB, :], a["c_sample"]).then_inc(loaded, 16)
                sp.dma_start(xtok[:, 0:4, :], a["x_prompt"][0].rearrange("(t p) d -> p t d", p=P)).then_inc(loaded, 16)
                sp.dma_start(xtok[0:NS, 4, :], a["x_sample"].rearrange("b t d -> (b t) d")).then_inc(loaded, 16)
                for name, rows in PROWS:
                    v = a[name][0]
                    if name == "rw_rk":
                        v = v.rearrange("h d -> (h d)")
                    sp.dma_start(prow[PROW[name]:PROW[name] + rows, :],
                                 v.rearrange("(r c) -> r c", c=P)).then_inc(loaded, 16)
                for g in range(NG):
                    if g >= 3:
                        sp.wait_ge(mps, g - 2)
                    sp.dma_start(wada[:, g % 3, :, :], w_r[:, :, g * 512:(g + 1) * 512]).then_inc(w_in[g % 3], 16)

            NLOAD = 16 * (7 + len(PROWS))

            @block.scalar
            def _(act):
                act.wait_ge(loaded, NLOAD)
                nc.scalar.activation(c9[:, :], c9[:, :], ACT.Silu).then_inc(silu, 1)

            @block.tensor
            def _(pe):
                pe.wait_ge(loaded, NLOAD)
                pe.wait_ge(silu, 1)
                pe.transpose(psc[:, 0:NPROW], prow[:, :], m["ident"][0:NPROW, 0:NPROW])
                for k in range(KD):
                    i = pe.transpose(psc[:, P + k * 9:P + k * 9 + 9], c9[:, k * P:(k + 1) * P], m["ident"][0:9, 0:9])
                i.then_inc(cps, 1)
                for k in range(KD):
                    i = pe.transpose(psd[:, k, :], xtok[0:NS, 4, k * P:(k + 1) * P], m["ident"][0:NS, 0:NS])
                i.then_inc(cps, 1)
                for k in range(KD):
                    if k >= 2:
                        pe.wait_ge(xev, k - 1)
                    for t in range(4):
                        i = pe.transpose(psx[:, k % 2, t * P:(t + 1) * P], xtok[:, t, k * P:(k + 1) * P], m["ident"][:, :])
                    i.then_inc(xps, 1)
                pe.wait_ge(cev, 2)
                for g in range(NG):
                    pe.wait_ge(w_in[g % 3], 16 * (g // 3 + 1))
                    if g >= 2:
                        pe.wait_ge(mev, g - 1)
                    for j in range(4):
                        for k in range(KD):
                            i = pe.matmul(psm[:, g % 2, j * 9:j * 9 + 9], wada[:, g % 3, k, j * P:(j + 1) * P],
                                          cT[:, k, :], start=(k == 0), stop=(k == KD - 1))
                    i.then_inc(mps, 1)

            @block.vector
            def _(dve):
                chain = Chain(dve, vch)
                dve.wait_ge(cps, 1)
                dve.tensor_copy(m["prm"][:, :], psc[:, 0:NPROW]).then_inc(cev, 1)
                dve.tensor_copy(cT[:, :, :], psc[:, P:P + 72].rearrange("p (k c) -> p k c", k=KD)).then_inc(cev, 1)
                dve.wait_ge(cps, 2)
                chain(dve.tensor_copy(m["xT"][:, :, SEQ:NT], psd[:, :, :]))
                for k in range(KD):
                    dve.wait_ge(xps, k + 1)
                    dve.tensor_copy(m["xT"][:, k, 0:SEQ], psx[:, k % 2, :]).then_inc(xev, 1)
                dve.wait_ge(cev, 2)
                for g in range(NG):
                    dve.wait_ge(mps, g + 1)
                    dve.tensor_tensor(m["modT"][:, 4 * g:4 * g + 4, :],
                                      psm[:, g % 2, 0:36].rearrange("p (j c) -> p j c", j=4),
                                      m["prm"][:, PROW["b_ada"] + 4 * g:PROW["b_ada"] + 4 * g + 4]
                                      .unsqueeze(2).to_broadcast([P, 4, 9]), ALU.add).then_inc(mev, 1)
                dve.wait_ge(mev, NG)
                chain(dve.tensor_scalar(m["modT"][:, KD:2 * KD, :], m["modT"][:, KD:2 * KD, :], 1.0, None, ALU.add))
                dve.wait_ge(xev, KD)
                modulate(dve, chain, m["hT"], m["xT"], m["modT"], 0, KD)


def modulate(dve, chain, out, x, modT, shift, scale):
    for k in range(KD):
        dve.tensor_scalar(out[:, k, 0:SEQ], x[:, k, 0:SEQ], modT[:, scale + k, 0:1], modT[:, shift + k, 0:1],
                          ALU.mult, ALU.add).then_inc(chain.sem, 1)
        chain.n += 1
    xs = x[:, :, SEQ:NT].rearrange("p k (b t) -> p k b t", t=DT)
    os = out[:, :, SEQ:NT].rearrange("p k (b t) -> p k b t", t=DT)
    chain(dve.tensor_tensor(os, xs, modT[:, scale:scale + KD, 1:9].unsqueeze(3).to_broadcast([P, KD, DB, DT]), ALU.mult))
    chain(dve.tensor_tensor(os, os, modT[:, shift:shift + KD, 1:9].unsqueeze(3).to_broadcast([P, KD, DB, DT]), ALU.add))


def split_high(eng, hi, x):
    return eng.tensor_copy(hi, x)


def split_low(eng, lo, x, hi):
    return eng.tensor_tensor(lo, x, hi.bitcast(F32), ALU.subtract)


def split_product(pe, out, w, x, first, last):
    parts = ((w[0], x[0]), (w[0], x[1]), (w[1], x[0]))
    for n, (l, r) in enumerate(parts):
        for h in range(2):
            i = pe.matmul(out[:, h, 0:HN], l, r[:, h * HN:(h + 1) * HN], start=(first and n == 0), stop=(last and n == 2))
    return i


def in_projection(nc, a, m):
    NW = 2
    groups = [g for g in GROUPS if g[2] < TILE0["gm"]]
    tiles = [(g, j, t0 + j, min(P, w - j * P)) for g, (_, w, t0) in enumerate(groups) for j in range(-(-w // P))]
    with ExitStack() as ctx:
        sem, sb, ps = (f(nc, ctx, "inp") for f in (sem_maker, sb_maker, ps_maker))
        w = sb("w", [P, NW, KD, 512])
        wh, wl_ = sb("wh", [P, 3, KD, P], F32R), sb("wl", [P, 3, KD, P], F32R)
        hh, hl = sb("hh", [P, KD, NT], F32R), sb("hl", [P, KD, NT], F32R)
        o = sb("o", [P, 4, NT])
        acc = ps("acc", [P, 4, 2, 512])
        wl = [sem(f"w{i}") for i in range(NW)]
        hsplit, wsplit, ch, done, evac, stored = sem("hsplit"), sem("wsplit"), sem("ch"), sem("done"), sem("evac"), [sem(f"st{i}") for i in range(4)]
        last = {g: n for n, (g, *_) in enumerate(tiles)}
        w_r = a["w_in"][0].rearrange("(k p) n -> p k n", p=P)
        with nc.Block() as block:

            @block.sync
            def _(sp):
                for g, (c, n, _) in enumerate(groups):
                    if g >= NW:
                        sp.wait_ge(wsplit, last[g - NW] + 1)
                    sp.dma_start(w[:, g % NW, :, 0:n], w_r[:, :, c:c + n]).then_inc(wl[g % NW], 16)

            @block.tensor
            def _(pe):
                for n, (g, j, t, rows) in enumerate(tiles):
                    pe.wait_ge(wsplit, n + 1)
                    if n >= 4:
                        pe.wait_ge(evac, n - 3)
                    for k in range(KD):
                        if n == 0:
                            pe.wait_ge(hsplit, k + 1)
                        i = split_product(pe, acc[0:rows, n % 4], (wh[:, n % 3, k, 0:rows], wl_[:, n % 3, k, 0:rows]),
                                          (hh[:, k], hl[:, k]), k == 0, k == KD - 1)
                    i.then_inc(done, 1)

            @block.vector
            def _(dve):
                c = Chain(dve, ch)
                for k in range(KD):
                    c(split_high(dve, hh[:, k], m["hT"][:, k]))
                    split_low(dve, hl[:, k], m["hT"][:, k], hh[:, k]).then_inc(hsplit, 1)
                for n, (g, j, t, rows) in enumerate(tiles):
                    if j == 0:
                        dve.wait_ge(wl[g % NW], 16 * (g // NW + 1))
                    if n >= 3:
                        dve.wait_ge(done, n - 2)
                    x = w[:, g % NW, :, j * P:j * P + rows]
                    c(split_high(dve, wh[:, n % 3, :, 0:rows], x))
                    split_low(dve, wl_[:, n % 3, :, 0:rows], x, wh[:, n % 3, :, 0:rows]).then_inc(wsplit, 1)

            @block.scalar
            def _(act):
                for n, (g, j, t, rows) in enumerate(tiles):
                    act.wait_ge(done, n + 1)
                    if n >= 4:
                        act.wait_ge(stored[n % 4], 16 * (n // 4))
                    nc.scalar.activation(halves(o[0:rows, n % 4, :]), acc[0:rows, n % 4, :, 0:HN], ACT.Copy).then_inc(evac, 1)
                    act.wait_ge(evac, n + 1)
                    act.dma_start(a["PT"][t * P:t * P + rows, :], o[0:rows, n % 4, :]).then_inc(stored[n % 4], 16)
                for s in range(4):
                    act.wait_ge(stored[s], 16 * len(range(s, len(tiles), 4)))


def token_major(nc, a, m):
    fgroups = [(i, min(4, len(TM_TILES) - i)) for i in range(0, len(TM_TILES), 4)]
    work = [(t, i, n) for t in range(5) for i, n in fgroups]
    with ExitStack() as ctx:
        sem, sb, ps = (f(nc, ctx, "tok") for f in (sem_maker, sb_maker, ps_maker))
        ft = sb("ft", [P, len(TM_TILES), NT])
        pt = sb("pt", [P, 14, NS + 1])
        gt = sb("gt", [24, NT])
        tok = sb("tok", [P, 5, TM_W])
        pbs = sb("pbs", [NS + 1, SHIFT_W])
        gate = sb("gate", [P, 5, 24])
        tp = ps("tp", [P, 4, 512])
        pp = ps("pp", [P, 4, 512])
        loaded, turned, kept, pturned, pkept, sig = (
            sem(s) for s in ("loaded", "turned", "kept", "pturned", "pkept", "sig"))
        out = m["shift_rows_out"]
        rows = lambda t: P if t < 4 else NS
        with nc.Block() as block:

            @block.sync
            def _(sp):
                for i, t in enumerate(TM_TILES):
                    sp.dma_start(ft[:, i, :], a["PT"][t * P:(t + 1) * P, :]).then_inc(loaded, 16)
                t = TILE0["pb"] * P
                sp.dma_start(pt[:, :, :], a["PT"][t:t + SHIFT_W, SEQ - 1:NT].rearrange("(n p) t -> p n t", p=P)).then_inc(loaded, 16)
                t = TILE0["ga"] * P
                sp.dma_start(gt[:, :], a["PT"][t:t + 24, :]).then_inc(loaded, 16)

            @block.tensor
            def _(pe):
                pe.wait_ge(loaded, 16 * (len(TM_TILES) + 2))
                for t in range(5):
                    i = pe.transpose(pp[0:rows(t), 0, t * 32:t * 32 + 24], gt[:, t * P:t * P + rows(t)], m["ident"][0:24, 0:24])
                i.then_inc(pturned, 1)
                for n in range(14):
                    if n % 4 == 0 and n == 12:
                        pe.wait_ge(pkept, 1)
                    i = pe.transpose(pp[0:NS + 1, (n // 4 + 1) % 4, (n % 4) * P:(n % 4 + 1) * P], pt[:, n, :], m["ident"][:, :])
                    if n % 4 == 3 or n == 13:
                        i.then_inc(pturned, 1)
                for w, (t, i0, n) in enumerate(work):
                    if w >= 4:
                        pe.wait_ge(kept, w - 3)
                    for j in range(n):
                        i = pe.transpose(tp[0:rows(t), w % 4, j * P:(j + 1) * P], ft[:, i0 + j, t * P:t * P + rows(t)], m["ident"][:, :])
                    i.then_inc(turned, 1)

            @block.vector
            def _(dve):
                dve.wait_ge(pturned, 1)
                dve.tensor_copy(gate[:, 0:4, :], pp[:, 0, 0:P].rearrange("p (t c) -> p t c", t=4)[:, :, 0:24])
                dve.tensor_copy(gate[0:NS, 4, :], pp[0:NS, 0, P:P + 24]).then_inc(pkept, 1)
                for g in range(4):
                    n = min(512, SHIFT_W - g * 512)
                    dve.wait_ge(pturned, g + 2)
                    dve.tensor_copy(pbs[:, g * 512:g * 512 + n], pp[0:NS + 1, (g + 1) % 4, 0:n]).then_inc(pkept, 1)
                for w, (t, i0, n) in enumerate(work):
                    dve.wait_ge(turned, w + 1)
                    dve.tensor_copy(tok[0:rows(t), t, i0 * P:(i0 + n) * P], tp[0:rows(t), w % 4, 0:n * P]).then_inc(kept, 1)

            @block.scalar
            def _(act):
                act.wait_ge(pkept, 1)
                nc.scalar.activation(m["gateP"][:, :, :], gate[:, 0:4, :], ACT.Sigmoid).then_inc(sig, 1)
                nc.scalar.activation(gate[0:NS, 4, :], gate[0:NS, 4, :], ACT.Sigmoid).then_inc(sig, 1)
                act.wait_ge(sig, 2)
                act.dma_start(a["GA"][SEQ:NT, :], gate[0:NS, 4, :]).then_inc(out, 16)
                act.wait_ge(pkept, 5)
                act.dma_start(a["PBS"], pbs[:, :]).then_inc(out, 16)
                act.dma_start(a["o_shift_p"][0, 0], pbs[0:1, :]).then_inc(out, 16)
                for b in range(DB):
                    r = 1 + b * DT + DT - 1
                    act.dma_start(a["o_shift_s"][0, b], pbs[r:r + 1, :]).then_inc(out, 16)
                n_out = 3 + DB
                act.wait_ge(kept, len(work))
                for t in range(5):
                    act.dma_start(a["TM"][t * P:t * P + rows(t), :], tok[0:rows(t), t, :]).then_inc(out, 16)
                n_out += 5
                act.wait_ge(out, 16 * n_out)


def new_cache_rows(sp, a, out):
    n = 0
    TM = a["TM"]
    for name, col in (("cmp", 0), ("slc", 256), ("win", 512)):
        sp.dma_start(a[f"o_{name}_p"][0, 0].rearrange("v g t d -> t (v g) d"),
                     TM[0:SEQ, col:col + 256].rearrange("t (c d) -> t c d", d=HD)).then_inc(out, 16)
        n += 1
    for g, (win, _) in enumerate(DIL):
        for v in range(2):
            col = TM_COL["kc" if v == 0 else "vc"] + g * 256
            sp.dma_start(a[f"o_dil{g}_p"][0, 0, v].rearrange("h t d -> t h d"),
                         TM[SEQ - min(win, SEQ):SEQ, col:col + 256].rearrange("t (c d) -> t c d", d=HD)).then_inc(out, 16)
            n += 1
    for b in range(DB):
        rows = TM[SEQ + b * DT:SEQ + (b + 1) * DT]
        for name, col in (("cmp", 0), ("slc", 256), ("win", 512)):
            o = a[f"o_{name}_s"][0, b]
            w = o.shape[2]
            sp.dma_start(o.rearrange("v g t d -> t (v g) d")[w - DT:w],
                         rows[:, col:col + 256].rearrange("t (c d) -> t c d", d=HD)).then_inc(out, 16)
            n += 1
        for g, (win, _) in enumerate(DIL):
            for v in range(2):
                col = TM_COL["kc" if v == 0 else "vc"] + g * 256
                sp.dma_start(a[f"o_dil{g}_s"][0, b, v].rearrange("h t d -> t h d")[win - DT:win],
                             rows[:, col:col + 256].rearrange("t (c d) -> t c d", d=HD)).then_inc(out, 16)
                n += 1
    return n


NEW_ROW_STORES = 3 + 6 + 9 * DB


def shift_caches(sp, a, copied):
    n = 0
    for name, w, heads, cut in (("win", 512, 4, 4), ("dil0", 128, 8, 1), ("dil1", 512, 8, 4), ("dil2", 2048, 8, 28)):
        src = a["cache_nsa_win" if name == "win" else f"cache_{name}"][0].rearrange("b v h t d -> (b v h) (t d)")
        dst = a[f"o_{name}_s"][0].rearrange("b v h t d -> (b v h) (t d)")
        src, dst = src[:, DT * HD:], dst[:, 0:(w - DT) * HD]
        sp.dma_start(dst.rearrange("r (c n) -> r c n", c=cut), src.rearrange("r (c n) -> r c n", c=cut)).then_inc(copied, 16)
        n += 1
    return n


def head_sums(pe, out, ones, x, ready=None):
    for h in range(2):
        i = pe.matmul(out[:, h, 0:HN], ones, x[:, h * HN:(h + 1) * HN], start=True, stop=True)
    return i


def halves(ap):
    return ap.rearrange("p (h c) -> p h c", h=2)


CH = 64
NCH = SEQ // CH
HALF_LIFE = math.exp(-0.5)


def rwkv(nc, a, m):
    with ExitStack() as ctx:
        sem, sb, ps = (f(nc, ctx, "rw") for f in (sem_maker, sb_maker, ps_maker))
        pb = sb("pb", [P, 14, NT])
        xm = sb("xm", [P, 14, NT])
        cum = sb("cum", [P, 4, SEQ])
        masks = sb("masks", [P, 9, P])
        gam = sb("gam", [P, 4, NCH])
        kk, kp, bb = pb[:, 0:4], pb[:, 4:8], pb[:, 8:12]
        r, k, v = xm[:, 0:4], xm[:, 4:8], xm[:, 8:12]
        gate, bonus = m["hT"][:, 0:4], m["hT"][:, 4:8]
        rwkv_elementwise(nc, a, m, pb, xm, cum, masks, gam, kk, kp, bb, r, k, v, gate, bonus)
        rwkv_chunks(nc, a, m, pb, xm, kk, kp, bb, r, k, v, cum, masks, gam)
        rwkv_norm(nc, a, m, gate, bonus)


def rwkv_elementwise(nc, a, m, pb, xm, cum, masks, gam, kk, kp, bb, r, k, v, gate, bonus):
    prm = m["prm"]
    with ExitStack() as ctx:
        sem, sb, ps = (f(nc, ctx, "rwe") for f in (sem_maker, sb_maker, ps_maker))
        ld = sb("ld", [P, 4, NT])
        av = sb("av", [P, 4, NT])
        tmp = sb("tmp", [P, 4, NT])
        shs = sb("shs", [DB, SHIFT_W])
        shT = sb("shT", [P, 14, DB])
        w2 = sb("w2", [P, 512])
        g2 = sb("g2", [P, 512])
        omka = sb("omka", [P, 4])
        dq = sb("dq", [NS, 6, 512])
        acc = ps("acc", [P, 4, 2, 512])
        loaded, sht, ch, ach, z_in, z, zout, sqr, kkn, kkn2, bin_, bsum, exps, dqt, dqc, stored, cums, cumd, vdone, xmd = (sem(s) for s in (
            "loaded", "sht", "ch", "ach", "z_in", "z", "zout", "sqr", "kkn", "kkn2", "bin", "bsum", "exps", "dqt", "dqc", "stored", "cums", "cumd", "vdone", "xmd"))
        with nc.Block() as block:

            @block.sync
            def _(sp):
                t = TILE0["pb"] * P
                sp.dma_start(pb[:, :, :], a["PT"][t:t + SHIFT_W, :].rearrange("(n p) t -> p n t", p=P)).then_inc(loaded, 16)
                sp.dma_start(shs[:, :], a["state_rwkv_shift"][0].rearrange("b o w -> (b o) w")).then_inc(loaded, 16)
                sp.dma_start(w2[0:64, :], a["rw_w2"][0]).then_inc(loaded, 16)
                sp.dma_start(w2[64:128, :], a["rw_a2"][0]).then_inc(loaded, 16)
                sp.dma_start(g2[:, :], a["rw_g2"][0]).then_inc(loaded, 16)
                sp.dma_start(masks[:, :, :], a["c_masks"].rearrange("l p q -> p l q")).then_inc(loaded, 16)
                sp.wait_ge(dqc, 6)
                sp.dma_start(a["DQ"], dq[:, :, :]).then_inc(stored, 16)
                sp.wait_ge(stored, 16)

            @block.tensor
            def _(pe):
                pe.wait_ge(loaded, 96)
                for n in range(14):
                    i = pe.transpose(acc[:, 3, 1, n * DB:(n + 1) * DB], shs[:, n * P:(n + 1) * P], m["ident"][0:DB, 0:DB])
                i.then_inc(sht, 1)
                pe.wait_ge(z_in, 2)
                for n in range(12):
                    which, t = n // 4, n % 4
                    lhs = (w2[0:64], w2[64:128], g2)[which][:, t * P:(t + 1) * P]
                    rhs = (xm[0:64, 12], xm[64:128, 12], xm[:, 13])[which]
                    if n >= 4:
                        pe.wait_ge(zout, n - 3)
                    for h in range(2):
                        i = pe.matmul(acc[:, n % 4, h, 0:HN], lhs, rhs[:, h * HN:(h + 1) * HN], start=True, stop=True)
                    i.then_inc(z, 1)
                pe.wait_ge(zout, 12)
                for t in range(4):
                    pe.wait_ge(kkn, t + 1)
                    head_sums(pe, acc[:, t], m["headones"][:, :], tmp[:, t]).then_inc(sqr, 1)
                for t in range(4):
                    pe.wait_ge(bin_, t + 1)
                    head_sums(pe, acc[:, t], m["headones"][:, :], tmp[:, t]).then_inc(bsum, 1)
                pe.wait_ge(vdone, 1)
                for q, src in enumerate((r, ld, kp, kk, bb, v)):
                    if q >= 2:
                        pe.wait_ge(dqc, q - 1)
                    for t in range(4):
                        i = pe.transpose(acc[0:NS, q % 2, 0, t * P:(t + 1) * P], src[:, t, SEQ:NT], m["ident"][:, :])
                    i.then_inc(dqt, 1)

            @block.scalar
            def _(act):
                act.wait_ge(xmd, 1)
                nc.scalar.activation(xm[0:64, 12, :], xm[0:64, 12, :], ACT.Tanh).then_inc(z_in, 1)
                nc.scalar.activation(xm[:, 13, :], xm[:, 13, :], ACT.Sigmoid).then_inc(z_in, 1)
                for n in range(12):
                    which, t = n // 4, n % 4
                    act.wait_ge(z, n + 1)
                    src = acc[:, n % 4, :, 0:HN]
                    if which == 0:
                        i = nc.scalar.activation(halves(ld[:, t]), src, ACT.Sigmoid, bias=prm[:, PROW["rw_w0"] + t:PROW["rw_w0"] + t + 1])
                    elif which == 1:
                        i = nc.scalar.activation(halves(av[:, t]), src, ACT.Sigmoid, bias=prm[:, PROW["rw_a0"] + t:PROW["rw_a0"] + t + 1])
                    else:
                        i = nc.scalar.activation(halves(gate[:, t]), src, ACT.Copy)
                    i.then_inc(zout, 1)
                for t in range(4):
                    act.wait_ge(sqr, t + 1)
                    nc.scalar.activation(halves(tmp[:, t]), acc[:, t, :, 0:HN], ACT.Sqrt).then_inc(kkn2, 1)
                act.wait_ge(cumd, 1)
                nc.scalar.activation(av[:, :, 0:SEQ], cum[:, :, :], ACT.Exp).then_inc(exps, 1)
                nc.scalar.activation(gam[:, :, :], cum[:, :, CH - 1:SEQ:CH], ACT.Exp).then_inc(exps, 1)
                nc.scalar.activation(tmp[:, :, 0:SEQ], tmp[:, :, 0:SEQ], ACT.Exp).then_inc(exps, 1)
                act.wait_ge(exps, 3)
                nc.scalar.activation(cum[:, :, :], cum[:, :, :], ACT.Exp, scale=-1.0).then_inc(exps, 1)
                nc.scalar.activation(ld[:, :, SEQ:NT], ld[:, :, SEQ:NT], ACT.Exp).then_inc(exps, 1)

            @block.vector
            def _(dve):
                c = Chain(dve, ch)
                dve.wait_ge(loaded, 96)
                dve.wait_ge(sht, 1)
                c(dve.tensor_copy(shT[:, :, :], acc[:, 3, 1, 0:14 * DB].rearrange("p (n b) -> p n b", b=DB)))
                c(dve.tensor_scalar(omka[:, :], prm[:, PROW["rw_ka"]:PROW["rw_ka"] + 4], -1.0, 1.0, ALU.mult, ALU.add))
                pbs = pb[:, :, SEQ:NT].rearrange("p n (b t) -> p n b t", t=DT)
                xms = xm[:, :, SEQ:NT].rearrange("p n (b t) -> p n b t", t=DT)
                c(dve.tensor_tensor(xm[:, :, 1:SEQ], pb[:, :, 0:SEQ - 1], pb[:, :, 1:SEQ], ALU.subtract))
                c(dve.tensor_scalar(xm[:, :, 0:1], pb[:, :, 0:1], -1.0, None, ALU.mult))
                c(dve.tensor_tensor(xms[:, :, :, 1:DT], pbs[:, :, :, 0:DT - 1], pbs[:, :, :, 1:DT], ALU.subtract))
                c(dve.tensor_tensor(xms[:, :, :, 0], shT[:, :, :], pbs[:, :, :, 0], ALU.subtract))
                for n in range(14):
                    i = dve.scalar_tensor_tensor(xm[:, n], xm[:, n], prm[:, PROW["rw_mu"] + n:PROW["rw_mu"] + n + 1],
                                                 pb[:, n], ALU.mult, ALU.add)
                    c(i)
                c(dve.memset(gam[:, 0, 0:1], 0.0))
                dve.tensor_copy(omka[:, :], omka[:, :]).then_inc(xmd, 1)
                for t in range(4):
                    c(dve.tensor_scalar(kk[:, t], k[:, t], prm[:, PROW["rw_kk"] + t:PROW["rw_kk"] + t + 1], None, ALU.mult))
                    dve.tensor_tensor(tmp[:, t], kk[:, t], kk[:, t], ALU.mult).then_inc(kkn, 1)
                dve.wait_ge(kkn2, 4)
                c(dve.tensor_scalar(tmp[:, :, :], tmp[:, :, :], 1e-12, None, ALU.max))
                c(dve.reciprocal(tmp[:, :, :], tmp[:, :, :]))
                c(dve.tensor_tensor(kk, kk, tmp[:, :, :], ALU.mult))
                dve.wait_ge(zout, 12)
                for t in range(4):
                    c(dve.tensor_scalar(kp[:, t], av[:, t], prm[:, PROW["rw_ka"] + t:PROW["rw_ka"] + t + 1], omka[:, t:t + 1], ALU.mult, ALU.add))
                c(dve.tensor_tensor(kp, kp, k, ALU.mult))
                c(dve.tensor_tensor(bb, kk, av[:, :, :], ALU.mult))
                for t in range(4):
                    dve.scalar_tensor_tensor(tmp[:, t], r[:, t], prm[:, PROW["rw_rk"] + t:PROW["rw_rk"] + t + 1], kp[:, t],
                                             ALU.mult, ALU.mult).then_inc(bin_, 1)
                for t in range(4):
                    dve.wait_ge(bsum, t + 1)
                    c(dve.tensor_tensor(halves(bonus[:, t]), acc[:, t, :, 0:HN], halves(v[:, t]), ALU.mult))
                c(dve.tensor_scalar(ld[:, :, :], ld[:, :, :], -HALF_LIFE, None, ALU.mult))
                for t in range(4):
                    c(dve.tensor_tensor_scan(cum[:, t, :], m["reset"][:, :], ld[:, t, 0:SEQ], 0.0, ALU.mult, ALU.add))
                c(dve.tensor_tensor(tmp[:, :, 0:SEQ], cum[:, :, :], ld[:, :, 0:SEQ], ALU.subtract))
                dve.tensor_copy(omka[:, :], omka[:, :]).then_inc(cumd, 1)
                dve.wait_ge(exps, 5)
                c(dve.tensor_tensor(r[:, :, 0:SEQ], r[:, :, 0:SEQ], av[:, :, 0:SEQ], ALU.mult))
                c(dve.tensor_tensor(kk[:, :, 0:SEQ], kk[:, :, 0:SEQ], tmp[:, :, 0:SEQ], ALU.mult))
                c(dve.tensor_tensor(bb[:, :, 0:SEQ], bb[:, :, 0:SEQ], cum[:, :, :], ALU.mult))
                c(dve.tensor_tensor(kp[:, :, 0:SEQ], kp[:, :, 0:SEQ], cum[:, :, :], ALU.mult))
                dve.tensor_copy(omka[:, :], omka[:, :]).then_inc(vdone, 1)
                for q in range(6):
                    dve.wait_ge(dqt, q + 1)
                    dve.tensor_copy(dq[:, q, :], acc[0:NS, q % 2, 0, :]).then_inc(dqc, 1)


class SampleRecurrence:
    HR = HD // 2
    HH = HR // 2

    def __init__(self, nc, a, m, pb, xm, sem, sb):
        self.a, self.out = a, m["sample_state_out"]
        flat = lambda x: x.rearrange("p n t -> p (n t)")
        self.S = flat(m["oaT"][:, :, :])[:, 0:self.HR * HD].rearrange("p (i j) -> p i j", j=HD)
        self.tmp = flat(pb[:, 12:14, :])[:, 0:self.HH * HD].rearrange("p (i j) -> p i j", j=HD)
        q012 = flat(xm[:, 12:14, :])[:, 0:3 * 5 * HD].rearrange("p (t q d) -> p t q d", t=3, q=5)
        self.q = [q012[:, t] for t in range(3)]
        self.q.append(m["ocT"][:, 0, 0:5 * HD].rearrange("p (q d) -> p q d", q=5))
        self.ot = m["ocT"][0:NS, 1, 0:512]
        self.vs = sb("vs", [P, DT, self.HR])
        self.sa = sb("sa", [P, self.HR])
        self.o = sb("o", [P, DT, self.HR])
        self.loaded, self.ch, self.done, self.back = (sem(s) for s in ("sloaded", "sch", "sdone", "sback"))
        self.n_loads = 0

    def load(self, sp):
        st, HR = self.a["state_rwkv"][0].rearrange("b h i j -> (b h) i j"), self.HR
        for ih in range(2):
            sp.dma_start(self.S[ih * 64:ih * 64 + 64], st[:, ih * HR:(ih + 1) * HR, :]).then_inc(self.loaded, 16)
            for b in range(DB):
                p0 = ih * 64 + b * 8
                rows = self.a["DQ"][b * DT:(b + 1) * DT]
                for t in range(DT):
                    sp.dma_start(self.q[t][p0:p0 + 8], rows[t, 0:5].rearrange("q (h d) -> h q d", h=8)).then_inc(self.loaded, 16)
                sp.dma_start(self.vs[p0:p0 + 8], rows[:, 5, :].rearrange("t (h d) -> h t d", h=8)[:, :, ih * HR:(ih + 1) * HR]).then_inc(self.loaded, 16)
        self.n_loads = 2 + 2 * DB * (DT + 1)

    def step(self, pool, c, t):
        B = [P, self.HH, HD]
        over_i = lambda x: x.unsqueeze(1).to_broadcast(B)
        over_j = lambda x: x.unsqueeze(2).to_broadcast(B)
        if t == 0:
            pool.wait_ge(self.loaded, 16 * (2 + 2 * DB * (DT + 1)))
        r, d, k, kk, b = (self.q[t][:, j, :] for j in range(5))
        tmp = self.tmp
        for i in range(2):
            half = slice(i * self.HH, (i + 1) * self.HH)
            S, sa, v, o = self.S[:, half, :], self.sa[:, half], self.vs[:, t, half], self.o[:, t, half]
            c(pool.tensor_tensor(tmp, S, over_i(kk), ALU.mult))
            row_sum(pool, c, sa, tmp)
            c(pool.tensor_tensor(S, S, over_i(d), ALU.mult))
            c(pool.tensor_tensor(tmp, over_j(sa), over_i(b), ALU.mult))
            c(pool.tensor_tensor(S, S, tmp, ALU.subtract))
            c(pool.tensor_tensor(tmp, over_j(v), over_i(k), ALU.mult))
            c(pool.tensor_tensor(S, S, tmp, ALU.add))
            c(pool.tensor_tensor(tmp, S, over_i(r), ALU.mult))
            row_sum(pool, c, o, tmp)
        if t == DT - 1:
            pool.sem_inc(self.done, 1)

    def store(self, sp):
        sp.wait_ge(self.done, 1)
        so, HR = self.a["o_rwkv_s"][0].rearrange("b h i j -> (b h) i j"), self.HR
        for ih in range(2):
            sp.dma_start(so[:, ih * HR:(ih + 1) * HR, :], self.S[ih * 64:ih * 64 + 64]).then_inc(self.out, 16)
            for b in range(DB):
                p0 = ih * 64 + b * 8
                sp.dma_start(self.a["OD"][b * DT:(b + 1) * DT].rearrange("t (h d) -> h t d", h=8)[:, :, ih * HR:(ih + 1) * HR],
                             self.o[p0:p0 + 8]).then_inc(self.out, 16)
        sp.wait_ge(self.out, 16 * 18)
        sp.dma_start(self.ot, self.a["OD"]).then_inc(self.back, 16)


def row_sum(pool, c, out, x):
    n = x.shape[-1] // 2
    while n > 1:
        c(pool.tensor_tensor(x[:, :, 0:n], x[:, :, 0:n], x[:, :, n:2 * n], ALU.add))
        n //= 2
    c(pool.tensor_tensor(out, x[:, :, 0], x[:, :, 1], ALU.add))


def rwkv_chunks(nc, a, m, pb, xm, kk, kp, bb, r, k, v, cum, masks, gam):
    NL = 6
    STRICT, INCL, LOW0 = 6, 7, 8
    with ExitStack() as ctx:
        sem, sb, ps = (f(nc, ctx, "rwc") for f in (sem_maker, sb_maker, ps_maker))
        bt, kt = cum, k[:, :, 0:SEQ]
        vt = sb("vt", [P, 4, 512])
        lt = sb("lt", [P, 8, P])
        ltm = sb("ltm", [P, 8, P])
        T = sb("T", [P, 8, P])
        X = sb("X", [P, 8, P])
        TT = sb("TT", [P, 2, 8, P])
        ak = sb("ak", [P, 2, 8, P])
        arb = sb("arb", [P, 2, 8, P])
        ark = sb("ark", [P, 2, 8, P])
        S = sb("S", [P, 4, HD])
        X1 = sb("X1", [P, 512])
        akv = sb("akv", [P, 2, 512])
        U = sb("U", [P, 512])
        so = sb("so", [HD, 8, HD])
        pp = ps("pp", [P, 2, 2, 512])
        pX = ps("pX", [P, 2, 512])
        pU, pO = ps("pU", [P, 512]), ps("pO", [P, 512])
        pS = pX[:, 0, 256:512]
        pOs = pX[:, 1, 256:512]
        pA = pp[:, 0, 0]
        ch, turned, tkept, prod, pkept, lvx, xk, lvy, lvk, masked, x1, x1k, u, uk, od, ok, sd, sk, fin, fink, s0, akd, akk, osp, oadd = (
            sem(s) for s in ("ch", "turned", "tkept", "prod", "pkept", "lvx", "xk", "lvy", "lvk", "masked", "x1", "x1k",
                             "u", "uk", "od", "ok", "sd", "sk", "fin", "fink", "s0", "akd", "akk", "osp", "oadd"))
        out = m["prompt_state_out"]
        sample = SampleRecurrence(nc, a, m, pb, xm, sem, sb)
        at = lambda h: (slice((h % 2) * 64, (h % 2) * 64 + 64), h // 2)
        pos = lambda h: (h % 2) * 4 + h // 2
        slot = lambda s: pp[:, s].rearrange("p a (h c) -> p (a h) c", h=4)
        NP = 5
        with nc.Block() as block:

            @block.sync
            def _(sp):
                sample.load(sp)
                new_cache_rows(sp, a, m["token_rows_out"])
                shift_caches(sp, a, m["copied"])
                sample.store(sp)

            @block.tensor
            def _(pe):
                for n, src in enumerate((bb, kp, v)):
                    for t in range(4):
                        w = n * 4 + t
                        if w >= 4:
                            pe.wait_ge(tkept, w - 3)
                        bank = pp[:, w % 4 // 2, w % 2]
                        for f in range(4):
                            i = pe.transpose(bank[:, f * P:(f + 1) * P], src[:, f, t * P:(t + 1) * P], m["ident"][:, :])
                        i.then_inc(turned, 1)
                pe.wait_ge(tkept, 12)
                for t in range(5):
                    if t < 4:
                        cols = slice(t * P, (t + 1) * P)
                        for n, (lhs, rhs) in enumerate(((bb, kk), (kk, bb), (kp, kk), (bb, r), (kp, r))):
                            w = t * NP + n
                            if n >= 2:
                                pe.wait_ge(pkept, w - 1)
                            elif t:
                                pe.wait_ge(lvk, (NL - 1) * t)
                            for h in range(8):
                                p, f = at(h)
                                i = pe.matmul(slot(n % 2)[:, pos(h), :], lhs[p, f, cols], rhs[p, f, cols], start=True, stop=True)
                            i.then_inc(prod, 1)
                        pe.wait_ge(pkept, (t + 1) * NP)
                        for h in range(8):
                            i = pe.matmul(pA[:, pos(h) * HD:(pos(h) + 1) * HD], ak[:, t % 2, pos(h), :], vt[:, t, h * HD:(h + 1) * HD], start=True, stop=True)
                        i.then_inc(akd, 1)
                        pe.wait_ge(akk, t + 1)
                        for l in range(1, NL):
                            lv = t * (NL - 1) + l
                            pe.wait_ge(masked, lv)
                            pe.wait_ge(lvk, lv - 1) if lv > 1 else None
                            for h in range(8):
                                i = pe.matmul(slot(0)[:, h, :], ltm[:, h, :], T[:, h, :], start=True, stop=True)
                            i.then_inc(lvx, 1)
                            pe.wait_ge(xk, lv)
                            for h in range(8):
                                pe.matmul(slot(0)[:, h, :], TT[:, t % 2, h, :], X[:, h, :], start=True, stop=True)
                                i = pe.matmul(slot(1)[:, h, :], X[:, h, :], TT[:, t % 2, h, :], start=True, stop=True)
                            i.then_inc(lvy, 1)
                    if t == 0:
                        pe.wait_ge(s0, 1)
                        continue
                    s = t - 1
                    pe.wait_ge(lvk, (NL - 1) * t)
                    for c in (2 * s, 2 * s + 1):
                        cb = slice((c % 2) * 64, (c % 2) * 64 + 64)
                        tc = slice(c * CH, (c + 1) * CH)
                        hc = lambda h: slice(h * HD, (h + 1) * HD)
                        pc = lambda h: slice(pos(h) * HD, (pos(h) + 1) * HD)
                        if c:
                            pe.wait_ge(sk, c)
                            pe.wait_ge(ok, c)
                        for h in range(8):
                            p, f = at(h)
                            i = pe.matmul(pX[cb, h % 2, f * HD:(f + 1) * HD], kk[p, f, tc], S[p, f, :], start=True, stop=True)
                        i.then_inc(x1, 1)
                        pe.wait_ge(x1k, c + 1)
                        for h in range(8):
                            p, f = at(h)
                            i = pe.matmul(pOs[p, f * CH:(f + 1) * CH], S[p, f, :], r[p, f, tc], start=True, stop=True)
                        i.then_inc(osp, 1)
                        for h in range(8):
                            i = pe.matmul(pU[cb, pc(h)], TT[cb, s % 2, pos(h), cb], X1[cb, pc(h)], start=True, stop=True)
                        i.then_inc(u, 1)
                        pe.wait_ge(uk, c + 1)
                        for h in range(8):
                            p, f = at(h)
                            o = pS[p, f * HD:(f + 1) * HD]
                            pe.matmul(o, bt[cb, s, hc(h)], U[cb, pc(h)], start=True, stop=False)
                            i = pe.matmul(o, kt[cb, s, hc(h)], vt[cb, s, hc(h)], start=False, stop=True)
                        i.then_inc(sd, 1)
                        if c:
                            pe.wait_ge(oadd, c)
                        for h in range(8):
                            p, f = at(h)
                            o = pO[p, f * CH:(f + 1) * CH]
                            pe.matmul(o, U[cb, pc(h)], arb[cb, s % 2, pos(h), cb], start=True, stop=False)
                            i = pe.matmul(o, vt[cb, s, hc(h)], ark[cb, s % 2, pos(h), cb], start=False, stop=True)
                        i.then_inc(od, 1)
                pe.wait_ge(sk, NCH)
                for f in range(4):
                    i = pe.transpose(pA[0:HD, f * P:(f + 1) * P], S[:, f, :], m["ident"][:, :])
                i.then_inc(fin, 1)
                pe.wait_ge(sample.back, 16)
                for t in range(4):
                    i = pe.transpose(pp[:, 1, 0, t * NS:(t + 1) * NS], sample.ot[:, t * P:(t + 1) * P], m["ident"][0:NS, 0:NS])
                i.then_inc(fin, 1)

            @block.gpsimd
            def _(pool):
                c = Chain(pool, sample.ch)
                pool.memset(S[:, :, :], 0.0).then_inc(s0, 1)
                for t in range(DT):
                    sample.step(pool, c, t)

            @block.vector
            def _(dve):
                c_ = Chain(dve, ch)
                for n, dst in enumerate((bt, kt, vt)):
                    for t in range(4):
                        w = n * 4 + t
                        dve.wait_ge(turned, w + 1)
                        dve.tensor_copy(dst[:, t, :], pp[:, w % 4 // 2, w % 2]).then_inc(tkept, 1)
                mask = lambda n: masks[:, n:n + 1, :].to_broadcast([P, 8, P])
                eye = m["ident"][:, :].unsqueeze(1).to_broadcast([P, 8, P])
                for t in range(5):
                    if t < 4:
                        for n in range(NP):
                            w = t * NP + n
                            dve.wait_ge(prod, w + 1)
                            p = slot(n % 2)
                            if n == 0:
                                if t:
                                    dve.wait_ge(masked, t * (NL - 1))
                                c_(dve.tensor_copy(lt[:, :, :], p))
                                c_(dve.tensor_tensor(X[:, :, :], lt[:, :, :], mask(0), ALU.mult))
                                dve.tensor_tensor(ltm[:, :, :], lt[:, :, :], mask(1), ALU.mult).then_inc(masked, 1)
                                dve.tensor_tensor(TT[:, t % 2], eye, X[:, :, :], ALU.subtract).then_inc(pkept, 1)
                            elif n == 1:
                                dve.wait_ge(pkept, w)
                                c_(dve.tensor_tensor(X[:, :, :], p, mask(LOW0), ALU.mult))
                                dve.tensor_tensor(T[:, :, :], eye, X[:, :, :], ALU.subtract).then_inc(pkept, 1)
                            else:
                                dst = (ak, arb, ark)[n - 2]
                                dve.tensor_tensor(dst[:, t % 2], p, mask(STRICT if n == 2 else INCL), ALU.mult).then_inc(pkept, 1)
                        dve.wait_ge(akd, t + 1)
                        dve.tensor_copy(akv[:, t % 2], pA).then_inc(akk, 1)
                        for l in range(1, NL):
                            lv = t * (NL - 1) + l
                            dve.wait_ge(lvx, lv)
                            dve.tensor_copy(X[:, :, :], slot(0)).then_inc(xk, 1)
                            if l + 1 < NL:
                                dve.tensor_tensor(ltm[:, :, :], lt[:, :, :], mask(l + 1), ALU.mult).then_inc(masked, 1)
                            dve.wait_ge(lvy, lv)
                            c_(dve.tensor_tensor(T[:, :, :], T[:, :, :], slot(0), ALU.subtract))
                            dve.tensor_tensor(TT[:, t % 2], TT[:, t % 2], slot(1), ALU.subtract).then_inc(lvk, 1)
                    if t == 0:
                        dve.wait_ge(s0, 1)
                        continue
                    s = t - 1
                    for c in (2 * s, 2 * s + 1):
                        cb = slice((c % 2) * 64, (c % 2) * 64 + 64)
                        dve.wait_ge(x1, c + 1)
                        hp = lambda x: x.rearrange("p (a c) -> p a c", a=2)
                        dve.tensor_tensor(hp(X1[cb, :]), pX[cb, :, 0:256], hp(akv[cb, s % 2, :]), ALU.add).then_inc(x1k, 1)
                        dve.wait_ge(u, c + 1)
                        if c >= 1:
                            dve.wait_ge(od, c)
                        dve.tensor_scalar(U[cb, :], pU[cb, :], -1.0, None, ALU.mult).then_inc(uk, 1)
                        dve.wait_ge(sd, c + 1)
                        dve.wait_ge(od, c + 1)
                        c_(dve.tensor_tensor(S[:, :, :], S[:, :, :], pS.rearrange("p (f c) -> p f c", f=4), ALU.add))
                        dve.tensor_tensor(S[:, :, :], S[:, :, :], gam[:, :, c:c + 1].to_broadcast([P, 4, HD]), ALU.mult).then_inc(sk, 1)
                        dve.wait_ge(ok, c + 1)
                        oc = m["obT"][:, :, c * CH:(c + 1) * CH]
                        dve.tensor_tensor(oc, oc, pO[:, 0:256].rearrange("p (f c) -> p f c", f=4), ALU.add).then_inc(oadd, 1)
                dve.wait_ge(fin, 1)
                dve.tensor_copy(so[:, :, :], pA[0:HD, :].rearrange("p (h j) -> p h j", h=8)).then_inc(fink, 1)
                dve.wait_ge(fin, 2)
                dve.tensor_copy(m["obT"][:, :, SEQ:NT], pp[:, 1, 0, 0:4 * NS].rearrange("p (t c) -> p t c", t=4))

            @block.scalar
            def _(act):
                for c in range(NCH):
                    act.wait_ge(osp, c + 1)
                    nc.scalar.activation(m["obT"][:, :, c * CH:(c + 1) * CH], pOs.rearrange("p (f c) -> p f c", f=4), ACT.Copy).then_inc(ok, 1)
                act.wait_ge(fink, 1)
                act.dma_start(a["o_rwkv_p"][0, 0].rearrange("h i j -> i h j"), so[:, :, :]).then_inc(out, 16)
                act.wait_ge(out, 16)


def rwkv_norm(nc, a, m, gate, bonus):
    o, prm = m["obT"], m["prm"]
    with ExitStack() as ctx:
        sem, sb, ps = (f(nc, ctx, "rwn") for f in (sem_maker, sb_maker, ps_maker))
        sq = sb("sq", [P, 4, NT])
        eps = sb("eps", [P, 1])
        acc = ps("acc", [P, 4, 2, 512])
        ch, mean, cen, var, std = (sem(s) for s in ("ch", "mean", "cen", "var", "std"))
        with nc.Block() as block:

            @block.tensor
            def _(pe):
                for t in range(4):
                    head_sums(pe, acc[:, t], m["headones"][:, :], o[:, t]).then_inc(mean, 1)
                for t in range(4):
                    pe.wait_ge(cen, t + 1)
                    head_sums(pe, acc[:, t], m["headones"][:, :], sq[:, t]).then_inc(var, 1)

            @block.scalar
            def _(act):
                for t in range(4):
                    act.wait_ge(var, t + 1)
                    nc.scalar.activation(halves(sq[:, t]), acc[:, t, :, 0:HN], ACT.Sqrt, bias=eps[:, :], scale=1.0 / HD).then_inc(std, 1)

            @block.vector
            def _(dve):
                c = Chain(dve, ch)
                c(dve.memset(eps[:, :], GN_EPS))
                for t in range(4):
                    dve.wait_ge(mean, t + 1)
                    c(dve.scalar_tensor_tensor(halves(o[:, t]), acc[:, t, :, 0:HN], -1.0 / HD, halves(o[:, t]), ALU.mult, ALU.add))
                    dve.tensor_tensor(sq[:, t], o[:, t], o[:, t], ALU.mult).then_inc(cen, 1)
                for t in range(4):
                    dve.wait_ge(std, t + 1)
                    c(dve.reciprocal(sq[:, t], sq[:, t]))
                    c(dve.tensor_tensor(o[:, t], o[:, t], sq[:, t], ALU.mult))
                    c(dve.tensor_scalar(o[:, t], o[:, t], prm[:, PROW["rw_gn_g"] + t:PROW["rw_gn_g"] + t + 1],
                                        prm[:, PROW["rw_gn_b"] + t:PROW["rw_gn_b"] + t + 1], ALU.mult, ALU.add))
                    c(dve.tensor_tensor(o[:, t], o[:, t], bonus[:, t], ALU.add))
                    c(dve.tensor_tensor(o[:, t], o[:, t], gate[:, t], ALU.mult))


def compress(nc, a, m):
    NSEQ = DB + 1
    work = [(s, c) for s in range(NSEQ) for c in range(4)]
    nhalf = lambda s: 2 if s < DB else 1
    rows = lambda s: P if s < DB else SEQ // 16
    nwin = lambda s: NC_S if s < DB else NC_P
    tmark, n = [], 0
    for s, c in work:
        tmark.append(n)
        n += 2 * nhalf(s)
    with ExitStack() as ctx:
        sem, sb, ps = (f(nc, ctx, "cmp") for f in (sem_maker, sb_maker, ps_maker))
        w1h, w1l = sb("w1h", [P, 2, 16, P], F32R), sb("w1l", [P, 2, 16, P], F32R)
        w2 = sb("w2", [P, 2, HD])
        per = sb("per", [32, P])
        peT = sb("peT", [P, 32])
        hc = sb("hc", [P, 2])
        R = [[sb("R0", [P, 4, 1024]), sb("R1", [P, 4, 1024])],
             [sb("R2", [P, 4, 1024]), m["hT"][:, :, :].rearrange("p k t -> p (k t)")[:, 0:4096].rearrange("p (c n) -> p c n", c=4)]]
        RTh, RTl = sb("RTh", [P, 2, 8, 257], F32R), sb("RTl", [P, 2, 8, 257], F32R)
        zero = sb("zero", [P, 16])
        w1 = R[1][0][:, :, :].rearrange("p c n -> p (c n)").rearrange("p (v c h) -> p v c h", v=2, c=16)
        hid = sb("hid", [P, 2, 256])
        pt = sb("pt", [P, 2 * DB], I32)
        lane = sb("lane", [P, 1], I32)
        pT = ps("pT", [P, 4, 512])
        pH = ps("pH", [P, 2, 512])
        pK = ps("pK", [P, 2, 512])
        wfree = sem("wfree")
        loaded, idx, ix, pet, pek, hcd, hck, turned, tkept, hd, act_, od, ok = (
            sem(s) for s in ("loaded", "idx", "ix", "pet", "pek", "hcd", "hck", "turned", "tkept", "hd", "act", "od", "ok"))
        got, got_p = [sem(f"got{i}") for i in range(2)], sem("gotp")
        with nc.Block() as block:

            @block.sync
            def _(sp):
                sp.dma_start(pt[:, :], a["page_lanes"]).then_inc(loaded, 16)
                sp.dma_start(lane[:, :], a["c_lane"]).then_inc(loaded, 16)
                sp.dma_start(w1, a["phi_w1"][0].rearrange("v l d h -> v (l d) h").rearrange("v (c p) h -> p v c h", p=P)).then_inc(loaded, 16)
                sp.dma_start(w2[:, :, :], a["phi_w2"][0].rearrange("v h d -> h v d")).then_inc(loaded, 16)
                sp.dma_start(per[:, :], a["phi_pe"][0].rearrange("v l d -> (v l d)").rearrange("(c p) -> c p", p=P)).then_inc(loaded, 16)
                sp.wait_ge(tkept, tmark[4 * (DB - 1)])
                sp.wait_ge(m["token_rows_out"], 16 * NEW_ROW_STORES)
                sp.dma_start(R[DB % 2][0][0:32, :, :],
                             a["o_cmp_p"][0, 0].rearrange("v g (c l) d -> c (v g) (l d)", l=16)).then_inc(got_p, 16)

            @block.gpsimd
            def _(pool):
                pool.wait_ge(idx, 5)
                src = a["cache_nsa_cmp"][0].rearrange("n v g (c l) d -> (n v g c) (l d)", l=16)
                for s in range(DB):
                    if s >= 2:
                        pool.wait_ge(tkept, tmark[4 * (s - 1)])
                    elif s == 1:
                        pool.wait_ge(wfree, 3)
                    for h in range(2):
                        for c in range(4):
                            pool.indirect_dma_start(
                                out=R[s % 2][h][:, c, :], out_offset=None, in_=src,
                                in_offset=bass.IndirectOffsetOnAxis(ap=m["idx"][:, c, 2 * s + h:2 * s + h + 1], axis=0),
                            ).then_inc(got[s % 2], 16)

            @block.tensor
            def _(pe):
                pe.wait_ge(loaded, 80)
                pe.transpose(pK[:, 0, 0:32], per[:, :], m["ident"][0:32, 0:32]).then_inc(pet, 1)
                pe.wait_ge(pek, 1)
                for v in range(2):
                    for c in range(16):
                        i = pe.matmul(pH[:, 0, v:v + 1], w1[:, v, c, :], peT[:, v * 16 + c:v * 16 + c + 1], start=(c == 0), stop=(c == 15))
                i.then_inc(hcd, 1)
                pe.wait_ge(hck, 1)

                def turn(w):
                    s, c = work[w]
                    if c == 0:
                        if s < DB:
                            pe.wait_ge(got[s % 2], 128 * (s // 2 + 1))
                        else:
                            pe.wait_ge(got_p, 16)
                    k = tmark[w]
                    for h in range(nhalf(s)):
                        for kq in range(2):
                            if k >= 4:
                                pe.wait_ge(tkept, k - 3)
                            for j in range(4):
                                kc = kq * 4 + j
                                i = pe.transpose(pT[:, k % 4, j * P:j * P + rows(s)], R[s % 2][h][0:rows(s), c, kc * P:(kc + 1) * P],
                                                 m["ident"][0:rows(s), 0:rows(s)])
                            i.then_inc(turned, 1)
                            k += 1

                def hidden(w):
                    s, c = work[w]
                    pe.wait_ge(tkept, tmark[w] + 2 * nhalf(s))
                    if w >= 2:
                        pe.wait_ge(act_, w - 1)
                    nw = nwin(s) + 1
                    if w == 0:
                        pe.wait_ge(wfree, 3)
                    for q in range(16):
                        lo, hi = w1l[:, c // 2, q, :], w1h[:, c // 2, q, :]
                        x = slice(q // 8, q // 8 + nw)
                        xh, xl = RTh[:, w % 2, q % 8, x], RTl[:, w % 2, q % 8, x]
                        for n, (l, r) in enumerate(((hi, xh), (hi, xl), (lo, xh))):
                            i = pe.matmul(pH[:, w % 2, 0:nw], l, r, start=(q == 0 and n == 0), stop=(q == 15 and n == 2))
                    i.then_inc(hd, 1)

                def project(w):
                    s, c = work[w]
                    v, g = c // 2, c % 2
                    pe.wait_ge(act_, w + 1)
                    if w >= 2:
                        pe.wait_ge(ok, w - 1)
                    nw = nwin(s)
                    if v == 0:
                        i = pe.matmul(pK[g * HD:(g + 1) * HD, w % 2, 0:nw], w2[:, 0, :], hid[:, w % 2, 0:nw], start=True, stop=True)
                    else:
                        for h in range(nhalf(s)):
                            n = min(P, nw - h * P)
                            i = pe.matmul(pK[0:n, w % 2, h * HD:(h + 1) * HD], hid[:, w % 2, h * P:h * P + n], w2[:, 1, :], start=True, stop=True)
                    i.then_inc(od, 1)

                turn(0)
                for w in range(len(work)):
                    if w + 1 < len(work):
                        turn(w + 1)
                    hidden(w)
                    if w:
                        project(w - 1)
                project(len(work) - 1)

            @block.scalar
            def _(act):
                act.wait_ge(hck, 1)
                for w, (s, c) in enumerate(work):
                    act.wait_ge(hd, w + 1)
                    if w >= 2:
                        act.wait_ge(od, w - 1)
                    nc.scalar.activation(hid[:, w % 2, 0:nwin(s)], pH[:, w % 2, 0:nwin(s)], ACT.Gelu_apprx_tanh,
                                         bias=hc[:, c // 2:c // 2 + 1]).then_inc(act_, 1)

            @block.vector
            def _(dve):
                ch = Chain(dve, ix)
                dve.wait_ge(loaded, 80)
                ch(dve.tensor_scalar(pt[:, :], pt[:, :], 32.0, None, ALU.mult))
                ch(dve.tensor_tensor(pt[:, :], pt[:, :], lane[:, 0:1].to_broadcast([P, 2 * DB]), ALU.add))
                for c in range(4):
                    dve.tensor_scalar(m["idx"][:, c, :], pt[:, :], float(8 * c), None, ALU.add).then_inc(idx, 1)
                dve.wait_ge(idx, 4)
                dve.sem_inc(idx, 1)
                dve.wait_ge(pet, 1)
                dve.tensor_copy(peT[:, :], pK[:, 0, 0:32]).then_inc(pek, 1)
                ch(split_high(dve, w1h[:, :, :, :], w1))
                split_low(dve, w1l[:, :, :, :], w1, w1h[:, :, :, :]).then_inc(wfree, 1)
                ch(dve.memset(zero[:, :], 0.0))
                for x in (RTh, RTl):
                    ch(dve.tensor_copy(x[:, :, :, 256], zero[:, :].rearrange("p (s k) -> p s k", s=2)))
                dve.sem_inc(wfree, 1)
                dve.wait_ge(hcd, 1)
                dve.tensor_copy(hc[:, :], pH[:, 0, 0:2]).then_inc(hck, 1)
                dve.wait_ge(hck, 1)
                dve.sem_inc(wfree, 1)

                def keep(w):
                    s, c = work[w]
                    if w >= 2:
                        dve.wait_ge(hd, w - 1)
                    k = tmark[w]
                    for h in range(nhalf(s)):
                        for kq in range(2):
                            dve.wait_ge(turned, k + 1)
                            at = (slice(None), w % 2, slice(kq * 4, kq * 4 + 4), slice(h * P, h * P + rows(s)))
                            x = pT[:, k % 4, :].rearrange("p (j c) -> p j c", j=4)[:, :, 0:rows(s)]
                            ch(split_high(dve, RTh[at], x))
                            split_low(dve, RTl[at], x, RTh[at]).then_inc(tkept, 1)
                            k += 1

                def result(w):
                    s, c = work[w]
                    v, g = c // 2, c % 2
                    dve.wait_ge(od, w + 1)
                    nw = nwin(s)
                    if v == 0:
                        gp = slice(g * HD, (g + 1) * HD)
                        dve.tensor_copy(m["kcT"][gp, s, 0:nw], pK[gp, w % 2, 0:nw]).then_inc(ok, 1)
                    else:
                        for h in range(nhalf(s)):
                            n = min(P, nw - h * P)
                            i = dve.tensor_copy(m["vc"][0:n, s, h, g * HD:(g + 1) * HD], pK[0:n, w % 2, h * HD:(h + 1) * HD])
                        i.then_inc(ok, 1)

                keep(0)
                for w in range(len(work)):
                    if w + 1 < len(work):
                        keep(w + 1)
                    if w:
                        result(w - 1)
                result(len(work) - 1)


def layer_norm_t(nc, a, m, tag, xin, out_tokens=None, gain="ln1"):
    prm = m["prm"]
    with ExitStack() as ctx:
        sem, sb, ps = (f(nc, ctx, tag) for f in (sem_maker, sb_maker, ps_maker))
        ones = sb("ones", [P, P])
        eps = sb("eps", [P, 1])
        mu = sb("mu", [P, NT])
        sq = sb("sq", [P, 2, NT])
        acc = ps("acc", [P, 2, 2, 512])
        y = sb("y", [P, 2, 512])
        pT = ps("pT", [P, 2, 512])
        ch, o1, summed, cen, var, std, ready, turned, kept = (sem(s) for s in (
            "ch", "o1", "summed", "cen", "var", "std", "ready", "turned", "kept"))
        stored = [m["y_out0"], m["y_out1"]]
        work = [(t, h) for t in range(5) for h in range(2)] if out_tokens else []
        rows = lambda t: P if t < 4 else NS
        with nc.Block() as block:

            @block.tensor
            def _(pe):
                pe.wait_ge(o1, 1)
                for k in range(KD):
                    for h in range(2):
                        i = pe.matmul(acc[:, 0, h, 0:HN], ones[:, :], xin[:, k, h * HN:(h + 1) * HN], start=(k == 0), stop=(k == KD - 1))
                i.then_inc(summed, 1)
                for k in range(KD):
                    pe.wait_ge(cen, k + 1)
                    for h in range(2):
                        i = pe.matmul(acc[:, 1, h, 0:HN], ones[:, :], sq[:, k % 2, h * HN:(h + 1) * HN], start=(k == 0), stop=(k == KD - 1))
                    i.then_inc(var, 1)
                for w, (t, h) in enumerate(work):
                    if w == 0:
                        pe.wait_ge(ready, KD)
                    if w >= 2:
                        pe.wait_ge(kept, w - 1)
                    for j in range(4):
                        i = pe.transpose(pT[0:rows(t), w % 2, j * P:(j + 1) * P], xin[:, 4 * h + j, t * P:t * P + rows(t)], m["ident"][:, :])
                    i.then_inc(turned, 1)

            @block.scalar
            def _(act):
                act.wait_ge(var, KD)
                nc.scalar.activation(halves(sq[:, 0]), acc[:, 1, :, 0:HN], ACT.Sqrt, bias=eps[:, :], scale=1.0 / D).then_inc(std, 1)
                if work:
                    for w, (t, h) in enumerate(work):
                        act.wait_ge(kept, w + 1)
                        if t < 4:
                            dst = a[out_tokens[0]][0, t * P:(t + 1) * P, h * 512:(h + 1) * 512]
                        else:
                            dst = a[out_tokens[1]].rearrange("b t d -> (b t) d")[:, h * 512:(h + 1) * 512]
                        act.dma_start(dst, y[0:rows(t), w % 2, :]).then_inc(stored[w % 2], 16)
                    for s in range(2):
                        act.wait_ge(stored[s], 16 * (len(work) // 2))

            @block.vector
            def _(dve):
                c = Chain(dve, ch)
                c(dve.memset(eps[:, :], LN_EPS))
                dve.memset(ones[:, :], 1.0).then_inc(o1, 1)
                dve.wait_ge(summed, 1)
                c(dve.tensor_scalar(halves(mu[:, :]), acc[:, 0, :, 0:HN], -1.0 / D, None, ALU.mult))
                for k in range(KD):
                    c(dve.tensor_tensor(xin[:, k], xin[:, k], mu[:, :], ALU.add))
                    if k >= 2:
                        dve.wait_ge(var, k - 1)
                    dve.tensor_tensor(sq[:, k % 2], xin[:, k], xin[:, k], ALU.mult).then_inc(cen, 1)
                dve.wait_ge(std, 1)
                c(dve.reciprocal(mu[:, :], sq[:, 0]))
                for k in range(KD):
                    c(dve.tensor_tensor(xin[:, k], xin[:, k], mu[:, :], ALU.mult))
                    g, b = PROW[gain + "_g"] + k, PROW[gain + "_b"] + k
                    dve.tensor_scalar(xin[:, k], xin[:, k], prm[:, g:g + 1], prm[:, b:b + 1], ALU.mult, ALU.add).then_inc(ready, 1)
                for w, (t, h) in enumerate(work):
                    dve.wait_ge(turned, w + 1)
                    if w >= 2:
                        dve.wait_ge(stored[w % 2], 16 * (w // 2))
                    dve.tensor_copy(y[0:rows(t), w % 2, :], pT[0:rows(t), w % 2, :]).then_inc(kept, 1)


def gated_residual(dve, c, x, n, acc, modT, gate, tmp):
    g = gate + n
    flat = tmp
    c(dve.tensor_copy(halves(flat), acc))
    c(dve.tensor_scalar(flat[:, 0:SEQ], flat[:, 0:SEQ], modT[:, g, 0:1], None, ALU.mult))
    s = flat[:, SEQ:NT].rearrange("p (b t) -> p b t", t=DT)
    c(dve.tensor_tensor(s, s, modT[:, g, 1:9].unsqueeze(2).to_broadcast([P, DB, DT]), ALU.mult))
    c(dve.scalar_tensor_tensor(x[:, n], x[:, n], ALPHA, flat, ALU.mult, ALU.add))


def merge(nc, a, m):
    BR = (("w_br_a", "oaT", 4), ("w_br_b", "obT", 4), ("w_br_c", "ocT", 2))
    with ExitStack() as ctx:
        sem, sb, ps = (f(nc, ctx, "mrg") for f in (sem_maker, sb_maker, ps_maker))
        wb = sb("wb", [P, 10, D])
        wo = sb("wo", [P, KD, D])
        gt = sb("gt", [P, 6, NT])
        t1 = sb("t1", [P, NT])
        t2 = sb("t2", [P, NT])
        acc = ps("acc", [P, 4, 2, 512])
        mT = m["hT"]
        loaded, wol, sig, done, used, ch, out, oused = (sem(s) for s in ("loaded", "wol", "sig", "done", "used", "ch", "out", "oused"))
        gl = [sem(f"g{i}") for i in range(2)]
        with nc.Block() as block:

            @block.sync
            def _(sp):
                at = 0
                for name, _, n in BR:
                    sp.dma_start(wb[:, at:at + n, :], a[name][0].rearrange("(k p) n -> p k n", p=P)).then_inc(loaded, 16)
                    at += n
                for n in range(KD):
                    if n >= 2:
                        sp.wait_ge(used, 3 * (n - 1))
                    for b in range(3):
                        t = TILE0["gm"] + b * KD + n
                        sp.dma_start(gt[:, 3 * (n % 2) + b, :], a["PT"][t * P:(t + 1) * P, :]).then_inc(gl[n % 2], 16)
                    if n == 1:
                        sp.dma_start(wo[:, :, :], a["w_o"][0].rearrange("(k p) n -> p k n", p=P)).then_inc(wol, 16)

            @block.scalar
            def _(act):
                for n in range(KD):
                    act.wait_ge(gl[n % 2], 48 * (n // 2 + 1))
                    nc.scalar.activation(gt[:, 3 * (n % 2):3 * (n % 2) + 3, :], gt[:, 3 * (n % 2):3 * (n % 2) + 3, :], ACT.Sigmoid).then_inc(sig, 1)

            @block.tensor
            def _(pe):
                pe.wait_ge(loaded, 48)
                for n in range(KD):
                    at = 0
                    for b, (_, src, nk) in enumerate(BR):
                        w = 3 * n + b
                        if w >= 4:
                            pe.wait_ge(used, w - 3)
                        for k in range(nk):
                            for h in range(2):
                                i = pe.matmul(acc[:, w % 4, h, 0:HN], wb[:, at + k, n * P:(n + 1) * P],
                                              m[src][:, k, h * HN:(h + 1) * HN], start=(k == 0), stop=(k == nk - 1))
                        i.then_inc(done, 1)
                        at += nk
                pe.wait_ge(wol, 16)
                pe.wait_ge(used, 3 * KD)
                for n in range(KD):
                    if n >= 4:
                        pe.wait_ge(oused, n - 3)
                    for k in range(KD):
                        for h in range(2):
                            i = pe.matmul(acc[:, n % 4, h, 0:HN], wo[:, k, n * P:(n + 1) * P], mT[:, k, h * HN:(h + 1) * HN],
                                          start=(k == 0), stop=(k == KD - 1))
                    i.then_inc(out, 1)

            @block.vector
            def _(dve):
                c = Chain(dve, ch)
                for n in range(KD):
                    dve.wait_ge(sig, n + 1)
                    g = lambda b: halves(gt[:, 3 * (n % 2) + b])
                    ac = lambda w: acc[:, w % 4, :, 0:HN]
                    w = 3 * n
                    dve.wait_ge(done, w + 1)
                    c(dve.tensor_tensor(halves(t1[:, :]), ac(w), g(0), ALU.mult))
                    dve.sem_inc(used, 1)
                    dve.wait_ge(done, w + 2)
                    c(dve.tensor_tensor(halves(t2[:, :]), ac(w + 1), g(1), ALU.mult))
                    dve.sem_inc(used, 1)
                    c(dve.tensor_tensor(t1[:, :], t1[:, :], t2[:, :], ALU.add))
                    dve.wait_ge(done, w + 3)
                    c(dve.tensor_tensor(halves(t2[:, :]), ac(w + 2), g(2), ALU.mult))
                    dve.tensor_tensor(mT[:, n], t1[:, :], t2[:, :], ALU.add).then_inc(used, 1)
                    dve.wait_ge(used, 3 * n + 3)
                for n in range(KD):
                    dve.wait_ge(out, n + 1)
                    gated_residual(dve, c, m["xT"], n, acc[:, n % 4, :, 0:HN], m["modT"], 2 * KD, t1[:, :])
                    dve.sem_inc(oused, 1)
    layer_norm_t(nc, a, m, "ln1", m["xT"])


def feed_forward(nc, a, m):
    NF = FF // P
    PIECES = [(t, u, 0, KD) for t in range(NF) for u in range(2)]
    PIECES += [(n, 2, k0, min(KD, NF - k0)) for n in range(KD) for k0 in range(0, NF, KD)]
    PER_N = -(-NF // KD)
    N1 = 2 * NF
    with ExitStack() as ctx:
        sem, sb, ps = (f(nc, ctx, "ffn") for f in (sem_maker, sb_maker, ps_maker))
        fh, fl = sb("fh", [P, NF, NT], F32R), sb("fl", [P, NF, NT], F32R)
        w = sb("w", [P, 3, KD, P])
        wh, wl = sb("wh", [P, 3, KD, P], F32R), sb("wl", [P, 3, KD, P], F32R)
        sil = sb("sil", [P, 2, NT])
        tmp = sb("tmp", [P, NT])
        acc = ps("acc", [P, 4, 2, 512])
        hh, hl = sb("hh", [P, KD, NT], F32R), sb("hl", [P, KD, NT], F32R)
        loaded = [sem(f"w{i}") for i in range(3)]
        hsplit, wsplit, done, sd, used, used2, ch = (sem(s) for s in ("hsplit", "wsplit", "done", "sd", "used", "used2", "ch"))
        w1r = a["w_ffn1"][0].rearrange("(k p) n -> p k n", p=P)
        w2r = a["w_ffn2"][0].rearrange("(k p) n -> p k n", p=P)
        with nc.Block() as block:

            @block.sync
            def _(sp):
                for i, (t, u, k0, nk) in enumerate(PIECES):
                    if i >= 3:
                        sp.wait_ge(wsplit, i - 2)
                    src = w2r[:, k0:k0 + nk, t * P:(t + 1) * P] if u == 2 else w1r[:, :, u * FF + t * P:u * FF + (t + 1) * P]
                    sp.dma_start(w[:, i % 3, 0:nk, :], src).then_inc(loaded[i % 3], 16)

            @block.tensor
            def _(pe):
                for i, (t, u, k0, nk) in enumerate(PIECES):
                    pe.wait_ge(wsplit, i + 1)
                    if i < N1:
                        if i >= 4:
                            pe.wait_ge(used, (i - 4) // 2 + 1)
                    elif i == N1:
                        pe.wait_ge(used, NF)
                    elif k0 == 0 and t >= 4:
                        pe.wait_ge(used2, t - 3)
                    slot = t % 4 if u == 2 else i % 4
                    for k in range(nk):
                        if i == 0:
                            pe.wait_ge(hsplit, k + 1)
                        x = (fh[:, k0 + k], fl[:, k0 + k]) if u == 2 else (hh[:, k], hl[:, k])
                        n = split_product(pe, acc[:, slot], (wh[:, i % 3, k], wl[:, i % 3, k]), x,
                                          k0 + k == 0, k0 + k == (NF if u == 2 else KD) - 1)
                    n.then_inc(done, 1)

            @block.scalar
            def _(act):
                for t in range(NF):
                    act.wait_ge(done, 2 * t + 1)
                    if t >= 2:
                        act.wait_ge(used, t - 1)
                    nc.scalar.activation(halves(sil[:, t % 2]), acc[:, 2 * t % 4, :, 0:HN], ACT.Silu).then_inc(sd, 1)

            @block.vector
            def _(dve):
                c = Chain(dve, ch)
                for k in range(KD):
                    scale, shift = 4 * KD + k, 3 * KD + k
                    c(dve.tensor_scalar(tmp[:, 0:SEQ], m["xT"][:, k, 0:SEQ], m["modT"][:, scale, 0:1], m["modT"][:, shift, 0:1],
                                        ALU.mult, ALU.add))
                    by_seq = lambda x: x[:, SEQ:NT].rearrange("p (b t) -> p b t", t=DT)
                    of_seq = lambda t: m["modT"][:, t, 1:9].unsqueeze(2).to_broadcast([P, DB, DT])
                    c(dve.tensor_tensor(by_seq(tmp), by_seq(m["xT"][:, k]), of_seq(scale), ALU.mult))
                    c(dve.tensor_tensor(by_seq(tmp), by_seq(tmp), of_seq(shift), ALU.add))
                    c(split_high(dve, hh[:, k], tmp[:, :]))
                    c(split_low(dve, hl[:, k], tmp[:, :], hh[:, k]))
                    dve.sem_inc(hsplit, 1)

                def split(i):
                    nk = PIECES[i][3]
                    dve.wait_ge(loaded[i % 3], 16 * (i // 3 + 1))
                    if i >= 3:
                        dve.wait_ge(done, i - 2)
                    c(split_high(dve, wh[:, i % 3, 0:nk], w[:, i % 3, 0:nk]))
                    split_low(dve, wl[:, i % 3, 0:nk], w[:, i % 3, 0:nk], wh[:, i % 3, 0:nk]).then_inc(wsplit, 1)

                split(0)
                split(1)
                for t in range(NF):
                    if t + 1 < NF:
                        split(2 * t + 2)
                        split(2 * t + 3)
                    dve.wait_ge(sd, t + 1)
                    dve.wait_ge(done, 2 * t + 2)
                    c(dve.tensor_tensor(halves(tmp[:, :]), acc[:, (2 * t + 1) % 4, :, 0:HN], halves(sil[:, t % 2]), ALU.mult))
                    c(split_high(dve, fh[:, t], tmp[:, :]))
                    c(split_low(dve, fl[:, t], tmp[:, :], fh[:, t]))
                    dve.sem_inc(used, 1)
                for n in range(-1, KD):
                    for i in range(N1 + PER_N * (n + 1), min(len(PIECES), N1 + PER_N * (n + 2))):
                        split(i)
                    if n < 0:
                        continue
                    dve.wait_ge(done, N1 + PER_N * (n + 1))
                    gated_residual(dve, c, m["xT"], n, acc[:, n % 4, :, 0:HN], m["modT"], 5 * KD, tmp[:, :])
                    dve.sem_inc(used2, 1)
    layer_norm_t(nc, a, m, "ln2", m["xT"], out_tokens=("o_y_p", "o_y_s"), gain="ln2")


def prompt_attention(nc, a, m):
    SA = slopes(GRP * HPG)
    SC = slopes(12)
    units = [(qt, "A", h) for qt in range(4) for h in range(8)] + [(qt, "C", h) for qt in range(4) for h in range(4)]
    NU = len(units)
    with ExitStack() as ctx:
        sem, sb, ps = (f(nc, ctx, "pat") for f in (sem_maker, sb_maker, ps_maker))
        qA = sb("qA", [P, HPG, SEQ])
        kA = sb("kA", [P, 2, SEQ])
        vA = sb("vA", [P, 2, 4, P])
        qC = sb("qC", [P, 6, SEQ])
        kC = sb("kC", [P, 6, SEQ])
        vC = sb("vC", [P, 4, 768])
        dist = sb("dist", [P, 4, SEQ])
        distc = sb("distc", [P, 4, 32])
        s = sb("s", [P, 3, 3, SEQ])
        pT = sb("pT", [P, 2, 3, SEQ])
        st = sb("st", [P, 4, 4, 4])
        tot = sb("tot", [P, 4, 2])
        pS = ps("pS", [P, 3, 512])
        pX = ps("pX", [P, 3, 512])
        pO = ps("pO", [P, 2, 512])
        loaded, qs, sc, sx, ex, wt, sd, tr, tk, pv, oe, ch = (
            sem(n) for n in ("loaded", "qs", "sc", "sx", "ex", "wt", "sd", "tr", "tk", "pv", "oe", "ch"))

        def branch(u, b):
            qt, kind, h = units[u]
            qc = slice(qt * P, (qt + 1) * P)
            if kind == "A":
                g, n = h // HPG, h % HPG
                r = slice(g * HD, (g + 1) * HD)
                if b == 0:
                    return qA[r, n, qc], m["kcT"][r, DB, 0:NC_P], 0, NC_P, [m["vc"][0:NC_P, DB, 0, r]], SA[h], distc[:, qt, 0:NC_P]
                return (qA[r, n, qc], kA[r, b - 1, 0:(qt + 1) * P], 0, (qt + 1) * P,
                        [vA[:, b - 1, k, r] for k in range(qt + 1)], SA[h], dist[:, 0, (3 - qt) * P:SEQ])
            r = slice((h % 2) * HD, (h % 2) * HD + HD)
            t = 2 * b + h // 2
            k0 = max(0, qt - 1) if b == 0 else 0
            c0 = (4 * b + h) * HD
            return (qC[r, t, qc], kC[r, t, k0 * P:(qt + 1) * P], k0 * P, (qt + 1 - k0) * P,
                    [vC[:, k, c0:c0 + HD] for k in range(k0, qt + 1)], SC[4 * b + h],
                    dist[:, 1 + b, (3 - qt + k0) * P:SEQ])

        with nc.Block() as block:

            @block.sync
            def _(sp):
                t = TILE0["qa"] * P
                for g in range(GRP):
                    sp.dma_start(qA[g * HD:(g + 1) * HD, :, :],
                                 a["PT"][t + g * 256:t + (g + 1) * 256, 0:SEQ].rearrange("(n d) t -> d n t", d=HD)).then_inc(loaded, 16)
                for i, (name, col) in enumerate((("kvs", "slc"), ("kvw", "win"))):
                    t = TILE0[name] * P
                    sp.dma_start(kA[:, i, :], a["PT"][t:t + P, 0:SEQ]).then_inc(loaded, 16)
                    c = TM_COL[col] + P
                    sp.dma_start(vA[:, i, :, :], a["TM"][0:SEQ, c:c + P].rearrange("(k p) c -> p k c", p=P)).then_inc(loaded, 16)
                for buf, name in ((qC, "qc"), (kC, "kc")):
                    t = TILE0[name] * P
                    sp.dma_start(buf[:, :, :], a["PT"][t:t + 768, 0:SEQ].rearrange("(n p) t -> p n t", p=P)).then_inc(loaded, 16)
                c = TM_COL["vc"]
                sp.dma_start(vC[:, :, :], a["TM"][0:SEQ, c:c + 768].rearrange("(k p) c -> p k c", p=P)).then_inc(loaded, 16)
                sp.dma_start(dist[:, :, :], a["c_dist"].rearrange("n p k -> p n k")).then_inc(loaded, 16)
                sp.dma_start(distc[:, :, :], a["c_distc"].rearrange("n p k -> p n k")).then_inc(loaded, 16)
            NLOAD = 16 * 11

            @block.tensor
            def _(pe):
                pe.wait_ge(qs, 2)

                def scores(u):
                    if u:
                        pe.wait_ge(sx, u)
                    for b in range(3):
                        q, k, _, n, _, _, _ = branch(u, b)
                        i = pe.matmul(pS[:, b, 0:n], q, k, start=True, stop=True)
                    i.then_inc(sc, 1)

                def turn(u):
                    for b in range(3):
                        w = 3 * u + b
                        pe.wait_ge(sd, w + 1)
                        if w >= 3:
                            pe.wait_ge(tk, w - 2)
                        n = branch(u, b)[3]
                        for k in range(-(-n // P)):
                            c = min(P, n - k * P)
                            i = pe.transpose(pX[0:c, w % 3, k * P:(k + 1) * P], s[:, u % 3, b, k * P:k * P + c], m["ident"][:, :])
                        i.then_inc(tr, 1)

                def values(u):
                    qt, kind, h = units[u]
                    o = pO[(h % 2) * HD:(h % 2) * HD + HD, u % 2, 0:P]
                    if u >= 2:
                        pe.wait_ge(oe, u - 1)
                    for b in (1, 2, 0):
                        if b == 1:
                            pe.wait_ge(tk, 3 * u + 3)
                        vs = branch(u, b)[4]
                        for k, v in enumerate(vs):
                            i = pe.matmul(o, v, pT[0:v.shape[0], u % 2, b, k * P:(k + 1) * P],
                                          start=(b == 1 and k == 0), stop=(b == 0 and k == len(vs) - 1))
                    i.then_inc(pv, 1)

                for i in range(NU + 3):
                    if i < NU:
                        scores(i)
                    if 2 <= i < NU + 2:
                        turn(i - 2)
                    if i >= 3:
                        values(i - 3)

            @block.scalar
            def _(act):
                act.wait_ge(loaded, NLOAD)
                nc.scalar.activation(qA[:, :, :], qA[:, :, :], ACT.Copy, scale=HD ** -0.5).then_inc(qs, 1)
                nc.scalar.activation(qC[:, :, :], qC[:, :, :], ACT.Copy, scale=HD ** -0.5).then_inc(qs, 1)
                for i in range(NU + 2):
                    if i < NU:
                        act.wait_ge(sx, i + 1)
                        for b in range(3):
                            n = branch(i, b)[3]
                            nc.scalar.activation(s[:, i % 3, b, 0:n], s[:, i % 3, b, 0:n], ACT.Exp, bias=st[:, i % 4, 0, b:b + 1],
                                                 accum_out=st[:, i % 4, 1, b:b + 1]).then_inc(ex, 1)
                        if units[i][1] == "C":
                            nc.scalar.activation(st[:, i % 4, 3, 0:3], st[:, i % 4, 0, 0:3], ACT.Exp, scale=-1.0,
                                                 bias=tot[:, i % 4, 0:1]).then_inc(ex, 1)
                        else:
                            act.wait_ge(ex, 4 * i + 3)
                            act.sem_inc(ex, 1)
                    if i >= 2:
                        u = i - 2
                        if u >= 2:
                            act.wait_ge(pv, u - 1)
                        for b in range(3):
                            n = branch(u, b)[3]
                            r = min(n, P)
                            c = -(-n // P) * P
                            act.wait_ge(tr, 3 * u + b + 1)
                            nc.scalar.activation(pT[0:r, u % 2, b, 0:c], pX[0:r, b, 0:c], ACT.Copy).then_inc(tk, 1)

            @block.gpsimd
            def _(pool):
                for u in range(NU):
                    pool.wait_ge(wt, u + 1)
                    for b in range(3):
                        n = branch(u, b)[3]
                        pool.tensor_scalar(s[:, u % 3, b, 0:n], s[:, u % 3, b, 0:n], st[:, u % 4, 2, b:b + 1], None, ALU.mult).then_inc(sd, 1)

            @block.vector
            def _(dve):
                c = Chain(dve, ch)

                def softmax_in(u):
                    dve.wait_ge(sc, u + 1)
                    if u >= 3:
                        dve.wait_ge(tr, 3 * (u - 2))
                    for b in range(3):
                        _, _, _, n, _, slope, dm = branch(u, b)
                        c(dve.scalar_tensor_tensor(s[:, u % 3, b, 0:n], dm, -slope, pS[:, b, 0:n], ALU.mult, ALU.add))
                        c(dve.tensor_reduce(st[:, u % 4, 0, b:b + 1], s[:, u % 3, b, 0:n], AX, ALU.max, negate=True))
                    if units[u][1] == "A":
                        dve.tensor_scalar(st[:, u % 4, 0, 0:1], st[:, u % 4, 0, 0:1], 1e20, None, ALU.min).then_inc(sx, 1)
                    else:
                        dve.tensor_reduce(tot[:, u % 4, 0:1], st[:, u % 4, 0, 0:3], AX, ALU.min).then_inc(sx, 1)

                def weights(u):
                    qt, kind, h = units[u]
                    dve.wait_ge(ex, 4 * u + 4)
                    den, w, e = (st[:, u % 4, j, 0:3] for j in (1, 2, 3))
                    if kind == "A":
                        g = m["gateP"][:, qt, 3 * h:3 * h + 3]
                        c(dve.tensor_scalar(den, den, 1e-30, None, ALU.max))
                        c(dve.reciprocal(den, den))
                        dve.tensor_tensor(w, den, g, ALU.mult).then_inc(wt, 1)
                    else:
                        c(dve.tensor_tensor(den, den, e, ALU.mult))
                        c(dve.tensor_reduce(tot[:, u % 4, 1:2], den, AX, ALU.add))
                        c(dve.reciprocal(tot[:, u % 4, 1:2], tot[:, u % 4, 1:2]))
                        dve.tensor_scalar(w, e, tot[:, u % 4, 1:2], None, ALU.mult).then_inc(wt, 1)

                def output(u):
                    qt, kind, h = units[u]
                    r = slice((h % 2) * HD, (h % 2) * HD + HD)
                    dve.wait_ge(pv, u + 1)
                    dve.tensor_copy(m["oaT" if kind == "A" else "ocT"][r, h // 2, qt * P:(qt + 1) * P], pO[r, u % 2, 0:P]).then_inc(oe, 1)

                for i in range(NU + 4):
                    if i < NU:
                        softmax_in(i)
                    if 1 <= i <= NU:
                        weights(i - 1)
                    if i >= 4:
                        output(i - 4)


def sample_nsa(nc, a, m):
    with ExitStack() as ctx:
        sb = sb_maker(nc, ctx, "sna")
        m = dict(m)
        m["QD"] = sb("QD", [P, DB, 32])
        m["gd"] = sb("gd", [P, 2, 3])
        m["osum"] = sb("osum", [P, 2, P])
        m["selb"] = sb("selb", [P, 2, NBLK])
        m["slope"] = sb("slope", [P, 1])
        sample_compressed(nc, a, m)
        sample_window(nc, a, m)
        sample_selected(nc, a, m)


def sample_compressed(nc, a, m):
    QD, gd, osum, selb = m["QD"], m["gd"], m["osum"], m["selb"]
    with ExitStack() as ctx:
        sem, sb, ps = (f(nc, ctx, "sco") for f in (sem_maker, sb_maker, ps_maker))
        qd = sb("qd", [P, HPG, NS])
        bias = sb("bias", [P, NC_S])
        ovl = sb("ovl", [P, 2, NBLK])
        same = sb("same", [P, P])
        forced = sb("forced", [P, NBLK])
        tri = sb("tri", [P, NBLK, NBLK])
        s = sb("s", [P, 2, NC_S])
        st = sb("st", [P, 2, 2])
        pT = sb("pT", [P, 2, 2, P])
        imp = sb("imp", [P, 2, NBLK])
        score = sb("score", [P, 2, NBLK])
        cmpb = sb("cmpb", [P, NBLK, NBLK])
        rank = sb("rank", [P, 2, NBLK])
        pS = ps("pS", [P, 2, 512])
        pX = ps("pX", [P, 2, 512])
        pI = ps("pI", [P, 2, 512])
        pO = ps("pO", [P, 2, 512])
        loaded, qz, qdd, sc, sx, ex, pn, tr, tk, im, ik, gs, od, ch = (sem(n) for n in (
            "loaded", "qz", "qdd", "sc", "sx", "ex", "pn", "tr", "tk", "im", "ik", "gs", "od", "ch"))
        with nc.Block() as block:

            @block.sync
            def _(sp):
                n = 0
                t = TILE0["qa"] * P
                for g in range(GRP):
                    sp.dma_start(qd[g * HD:(g + 1) * HD, :, :],
                                 a["PT"][t + g * 256:t + (g + 1) * 256, SEQ:NT].rearrange("(n d) t -> d n t", d=HD)).then_inc(loaded, 16)
                    n += 1
                for b in range(DB):
                    for g in range(GRP):
                        p0 = 32 * (b % 4) + 16 * g
                        for q in range(DT):
                            sp.dma_start(gd[p0 + 4 * q:p0 + 4 * q + 4, b // 4, :],
                                         a["GA"][SEQ + b * DT + q, 12 * g:12 * g + 12].rearrange("(n r) -> n r", r=3)).then_inc(loaded, 16)
                            n += 1
                for buf, name in ((bias[:, :], "c_cbias"), (same[:, :], "c_same"), (forced[:, :], "c_forced"),
                                  (m["slope"][:, :], "c_slope")):
                    sp.dma_start(buf, a[name]).then_inc(loaded, 16)
                    n += 1
                sp.dma_start(ovl[:, :, :], a["c_ovl"].rearrange("(h p) j -> p h j", p=P)).then_inc(loaded, 16)
                sp.dma_start(tri[:, :, :], a["c_tri"].partition_broadcast(P)).then_inc(loaded, 16)
            NLOAD = 16 * (2 + 64 + 4 + 2)

            @block.gpsimd
            def _(pool):
                pool.memset(QD[:, :, :], 0.0).then_inc(qz, 1)

            @block.tensor
            def _(pe):
                pe.wait_ge(qdd, 2)
                for b in range(DB):
                    i = pe.matmul(pS[32 * (b % 4):32 * (b % 4) + 32, b // 4, 0:NC_S], QD[:, b, :], m["kcT"][:, b, 0:NC_S], start=True, stop=True)
                    if b % 4 == 3:
                        i.then_inc(sc, 1)
                for g in range(2):
                    pe.wait_ge(pn, g + 1)
                    for h in range(2):
                        n = min(P, NC_S - h * P)
                        i = pe.transpose(pX[0:n, g, h * P:(h + 1) * P], s[:, g, h * P:h * P + n], m["ident"][:, :])
                    i.then_inc(tr, 1)
                for g in range(2):
                    pe.wait_ge(tk, g + 1)
                    for h in range(2):
                        n = min(P, NC_S - h * P)
                        i = pe.matmul(pI[:, g, 0:NBLK], pT[0:n, g, h, :], ovl[0:n, h, :], start=(h == 0), stop=(h == 1))
                    i.then_inc(im, 1)
                for g in range(2):
                    pe.wait_ge(ik, g + 1)
                    pe.matmul(pI[:, g, 128:128 + NBLK], same[:, :], imp[:, g, :], start=True, stop=True).then_inc(gs, 1)
                for g in range(2):
                    for b in range(4):
                        for h in range(2):
                            n = min(P, NC_S - h * P)
                            i = pe.matmul(pO[32 * b:32 * b + 32, g, 0:P], pT[0:n, g, h, 32 * b:32 * b + 32], m["vc"][0:n, 4 * g + b, h, :],
                                          start=(h == 0), stop=(h == 1))
                    i.then_inc(od, 1)

            @block.scalar
            def _(act):
                for g in range(2):
                    act.wait_ge(sx, g + 1)
                    nc.scalar.activation(s[:, g, :], s[:, g, :], ACT.Exp, bias=st[:, g, 0:1], accum_out=st[:, g, 1:2]).then_inc(ex, 1)

            @block.vector
            def _(dve):
                c = Chain(dve, ch)
                dve.wait_ge(loaded, NLOAD)
                dve.wait_ge(qz, 1)
                for g in range(GRP):
                    gp = slice(g * HD, (g + 1) * HD)
                    dve.tensor_scalar(QD[gp, :, 16 * g:16 * g + 16].rearrange("p b (q n) -> p b q n", q=DT),
                                      qd[gp].rearrange("p n (b q) -> p b q n", q=DT), HD ** -0.5, None, ALU.mult).then_inc(qdd, 1)
                for g in range(2):
                    dve.wait_ge(sc, g + 1)
                    c(dve.tensor_tensor(s[:, g, :], pS[:, g, 0:NC_S], bias[:, :], ALU.add))
                    dve.tensor_reduce(st[:, g, 0:1], s[:, g, :], AX, ALU.max, negate=True).then_inc(sx, 1)
                for g in range(2):
                    dve.wait_ge(ex, g + 1)
                    c(dve.reciprocal(st[:, g, 1:2], st[:, g, 1:2]))
                    dve.tensor_scalar(s[:, g, :], s[:, g, :], st[:, g, 1:2], None, ALU.mult).then_inc(pn, 1)
                for g in range(2):
                    dve.wait_ge(tr, g + 1)
                    c(dve.tensor_copy(pT[:, g, 0, :], pX[:, g, 0:P]))
                    n = NC_S - P
                    dve.tensor_copy(pT[0:n, g, 1, :], pX[0:n, g, P:2 * P]).then_inc(tk, 1)
                for g in range(2):
                    dve.wait_ge(im, g + 1)
                    dve.tensor_copy(imp[:, g, :], pI[:, g, 0:NBLK]).then_inc(ik, 1)
                B = [P, NBLK, NBLK]
                for g in range(2):
                    dve.wait_ge(gs, g + 1)
                    c(dve.tensor_tensor(score[:, g, :], pI[:, g, 128:128 + NBLK], forced[:, :], ALU.add))
                    si = score[:, g, :].unsqueeze(1).to_broadcast(B)
                    sj = score[:, g, :].unsqueeze(2).to_broadcast(B)
                    c(dve.tensor_tensor(cmpb[:, :, :], si, sj, ALU.is_equal))
                    c(dve.tensor_tensor(cmpb[:, :, :], cmpb[:, :, :], tri[:, :, :], ALU.mult))
                    c(dve.tensor_reduce(rank[:, g, :], cmpb[:, :, :], AX, ALU.add))
                    c(dve.tensor_tensor(cmpb[:, :, :], si, sj, ALU.is_gt))
                    c(dve.tensor_reduce(selb[:, g, :], cmpb[:, :, :], AX, ALU.add))
                    c(dve.tensor_tensor(rank[:, g, :], rank[:, g, :], selb[:, g, :], ALU.add))
                    c(dve.tensor_scalar(selb[:, g, :], rank[:, g, :], TOPN - 0.5, -BIG, ALU.is_gt, ALU.mult))
                    dve.wait_ge(od, g + 1)
                    c(dve.tensor_scalar(osum[:, g, :], pO[:, g, 0:P], gd[:, g, 0:1], None, ALU.mult))


def sample_window(nc, a, m):
    QD, gd, osum = m["QD"], m["gd"], m["osum"]
    W = 512
    with ExitStack() as ctx:
        sem, sb, ps = (f(nc, ctx, "swi") for f in (sem_maker, sb_maker, ps_maker))
        K = sb("K", [P, DB, 4, P])
        V = sb("V", [P, DB, 4, P])
        KN = sb("KN", [P, NS])
        VN = sb("VN", [DT, DB, P])
        KT = sb("KT", [P, 2, 512])
        s = sb("s", [P, 2, W + DT])
        bias = sb("bias", [P, W + DT])
        pT = sb("pT", [P, 2, 5, P])
        st = sb("st", [P, 2, 3])
        pK = ps("pK", [P, 2, 512])
        pS = ps("pS", [P, 2, 512])
        pN = ps("pN", [P, 512])
        pX = ps("pX", [P, 2, 512])
        pO = ps("pO", [P, 512])
        loaded, kt, kk, sc, scn, sx, ex, tr, tk, od, ch, ok = (sem(n) for n in (
            "loaded", "kt", "kk", "sc", "scn", "sx", "ex", "tr", "tk", "od", "ch", "ok"))
        with nc.Block() as block:

            @block.sync
            def _(sp):
                for b in range(DB):
                    for v, buf in ((0, K), (1, V)):
                        for g in range(GRP):
                            sp.dma_start(buf[:, b, :, g * HD:(g + 1) * HD], a["cache_nsa_win"][0, b, v, g].rearrange("(p l) d -> p l d", l=4)).then_inc(loaded, 16)
                t = TILE0["kvw"] * P
                sp.dma_start(KN[:, :], a["PT"][t:t + P, SEQ:NT]).then_inc(loaded, 16)
                c = TM_COL["win"] + P
                sp.dma_start(VN[:, :, :], a["TM"][SEQ:NT, c:c + P].rearrange("(b q) c -> q b c", q=DT)).then_inc(loaded, 16)
                sp.dma_start(bias[:, :], a["c_wbias"]).then_inc(loaded, 16)
            NLOAD = 16 * (4 * DB + 3)

            @block.tensor
            def _(pe):
                pe.wait_ge(loaded, NLOAD)

                def score(b):
                    pe.wait_ge(kk, b + 1)
                    if b >= 2:
                        pe.wait_ge(sx, b - 1)
                    pe.matmul(pS[32 * (b % 4):32 * (b % 4) + 32, b % 2, :], QD[:, b, :], KT[:, b % 2, :], start=True, stop=True).then_inc(sc, 1)

                for b in range(DB):
                    if b >= 2:
                        pe.wait_ge(kk, b - 1)
                    for l in range(4):
                        i = pe.transpose(pK[:, b % 2, l * P:(l + 1) * P], K[:, b, l, :], m["ident"][:, :])
                    i.then_inc(kt, 1)
                    if b:
                        score(b - 1)
                score(DB - 1)
                for b in range(DB):
                    i = pe.matmul(pN[32 * (b % 4):32 * (b % 4) + 32, 8 * (b // 4):8 * (b // 4) + DT], QD[:, b, :], KN[:, b * DT:(b + 1) * DT], start=True, stop=True)
                i.then_inc(scn, 1)
                for g in range(2):
                    pe.wait_ge(ex, g + 1)
                    if g:
                        pe.wait_ge(tk, 2)
                    for l in range(4):
                        i = pe.transpose(pX[:, 0, l * P:(l + 1) * P], s[:, g, l * P:(l + 1) * P], m["ident"][:, :])
                    i = pe.transpose(pX[0:DT, 1, 0:P], s[:, g, W:W + DT], m["ident"][:, :])
                    i.then_inc(tr, 1)
                    pe.wait_ge(tk, 2 * g + 2)
                    if g:
                        pe.wait_ge(ok, 1)
                    for b in range(4):
                        o = pO[32 * b:32 * b + 32, 0:P]
                        rows = slice(32 * b, 32 * b + 32)
                        for l in range(4):
                            pe.matmul(o, pT[:, g, l, rows], V[:, 4 * g + b, l, :], start=(l == 0), stop=False)
                        i = pe.matmul(o, pT[0:DT, g, 4, rows], VN[:, 4 * g + b, :], start=False, stop=True)
                    i.then_inc(od, 1)

            @block.scalar
            def _(act):
                for g in range(2):
                    act.wait_ge(sx, DB + g + 1)
                    nc.scalar.activation(s[:, g, :], s[:, g, :], ACT.Exp, bias=st[:, g, 0:1], accum_out=st[:, g, 1:2]).then_inc(ex, 1)

            @block.vector
            def _(dve):
                c = Chain(dve, ch)

                def score(b):
                    r = slice(32 * (b % 4), 32 * (b % 4) + 32)
                    dve.wait_ge(sc, b + 1)
                    dve.tensor_tensor(s[r, b // 4, 0:W], pS[r, b % 2, :], bias[r, 0:W], ALU.add).then_inc(sx, 1)

                dve.wait_ge(loaded, NLOAD)
                for b in range(DB):
                    dve.wait_ge(kt, b + 1)
                    if b >= 2:
                        dve.wait_ge(sc, b - 1)
                    dve.tensor_copy(KT[:, b % 2, :], pK[:, b % 2, :]).then_inc(kk, 1)
                    if b:
                        score(b - 1)
                score(DB - 1)
                dve.wait_ge(scn, 1)
                dve.wait_ge(sx, DB)
                for g in range(2):
                    c(dve.tensor_tensor(s[:, g, W:W + DT], pN[:, 8 * g:8 * g + DT], bias[:, W:W + DT], ALU.add))
                    dve.tensor_reduce(st[:, g, 0:1], s[:, g, :], AX, ALU.max, negate=True).then_inc(sx, 1)
                for g in range(2):
                    dve.wait_ge(tr, g + 1)
                    dve.tensor_copy(pT[:, g, 0:4, :], pX[:, 0, :].rearrange("p (l r) -> p l r", l=4)).then_inc(tk, 1)
                    dve.tensor_copy(pT[0:DT, g, 4, :], pX[0:DT, 1, 0:P]).then_inc(tk, 1)
                    c(dve.reciprocal(st[:, g, 1:2], st[:, g, 1:2]))
                    c(dve.tensor_tensor(st[:, g, 2:3], st[:, g, 1:2], gd[:, g, 2:3], ALU.mult))
                    dve.wait_ge(od, g + 1)
                    c(dve.scalar_tensor_tensor(osum[:, g, :], pO[:, 0:P], st[:, g, 2:3], osum[:, g, :], ALU.mult, ALU.add))
                    dve.sem_inc(ok, 1)


def sample_selected(nc, a, m):
    QD, gd, osum, selb, idx = m["QD"], m["gd"], m["osum"], m["selb"], m["idx"]
    NKS = 2
    with ExitStack() as ctx:
        sem, sb, ps = (f(nc, ctx, "ssl") for f in (sem_maker, sb_maker, ps_maker))
        K = sb("K", [P, NKS, 2, 1024])
        KR = sb("KR", [P, 2, 16, P])
        V = sb("V", [P, 4, 2, 2, 1024])
        KN = sb("KN", [P, NS])
        VN = sb("VN", [DT, DB, P])
        KT = sb("KT", [P, 2, 512])
        s = sb("s", [P, PAST + DT])
        nbias = sb("nbias", [P, DT])
        pn = sb("pn", [DT, P])
        pT = KT
        st = sb("st", [P, 2, 3])
        rel = m["hT"][:, :, :].rearrange("p k t -> p (k t)")[:, 0:PAST]
        pK = ps("pK", [P, 2, 512])
        pS = ps("pS", [P, 2, 512])
        pN = ps("pN", [P, 512])
        pO = ps("pO", [P, 512])
        pF = ps("pF", [P, 2, 512])
        loaded, kt, kk, sc, sx, scn, snk, mx, ex, tr, tk, od, ok, ch, ft, kr = (sem(n) for n in (
            "loaded", "kt", "kk", "sc", "sx", "scn", "snk", "mx", "ex", "tr", "tk", "od", "ok", "ch", "ft", "kr"))
        kg = [sem(f"kg{i}") for i in range(NKS)]
        vg = [sem(f"vg{i}") for i in range(4)]
        NU = 64
        with nc.Block() as block:

            @block.sync
            def _(sp):
                t = TILE0["kvs"] * P
                sp.dma_start(KN[:, :], a["PT"][t:t + P, SEQ:NT]).then_inc(loaded, 16)
                c = TM_COL["slc"] + P
                sp.dma_start(VN[:, :, :], a["TM"][SEQ:NT, c:c + P].rearrange("(b q) c -> q b c", q=DT)).then_inc(loaded, 16)
                sp.dma_start(rel, a["c_rel"].partition_broadcast(P)).then_inc(loaded, 16)
                sp.dma_start(nbias[:, :], a["c_nbias"]).then_inc(loaded, 16)

            @block.gpsimd
            def _(pool):
                src = a["cache_nsa_slc"][0].rearrange("n v g (c l) d -> (n v g c) (l d)", l=16)

                def gather(dst, c, h, done):
                    pool.indirect_dma_start(out=dst, out_offset=None, in_=src,
                                            in_offset=bass.IndirectOffsetOnAxis(ap=idx[:, c, h:h + 1], axis=0)).then_inc(done, 16)

                for b in range(DB):
                    for h in range(2):
                        u = 2 * b + h
                        if u >= NKS:
                            pool.wait_ge(kr, u - NKS + 1)
                        for g in range(GRP):
                            gather(K[:, u % NKS, g, :], g, u, kg[u % NKS])
                    if b == 4:
                        pool.wait_ge(od, 1)
                    for h in range(2):
                        for g in range(GRP):
                            gather(V[:, b % 4, h, g, :], 2 + g, 2 * b + h, vg[b % 4])

            @block.tensor
            def _(pe):
                pe.wait_ge(loaded, 64)

                def turn(w):
                    u, lq = w // 4, w % 4
                    if lq == 0:
                        pe.wait_ge(kr, u + 1)
                    k = w + (w // 32) * 8
                    if k >= 2:
                        pe.wait_ge(kk, k - 1)
                    for j in range(4):
                        l = 4 * lq + j
                        i = pe.transpose(pK[:, k % 2, j * P:(j + 1) * P], KR[:, u % 2, l, :], m["ident"][:, :])
                    i.then_inc(kt, 1)

                def score(w):
                    b = w // 8
                    k = w + (w // 32) * 8
                    pe.wait_ge(kk, k + 1)
                    if w >= 2:
                        pe.wait_ge(sx, w - 1)
                    pe.matmul(pS[32 * (b % 4):32 * (b % 4) + 32, w % 2, :], QD[:, b, :], KT[:, k % 2, :], start=True, stop=True).then_inc(sc, 1)

                for g in range(2):
                    if g:
                        pe.wait_ge(snk, 1)
                    for b in range(4 * g, 4 * g + 4):
                        i = pe.matmul(pN[32 * (b % 4):32 * (b % 4) + 32, 0:DT], QD[:, b, :], KN[:, b * DT:(b + 1) * DT], start=True, stop=True)
                    i.then_inc(scn, 1)
                    turn(32 * g)
                    for w in range(32 * g, 32 * g + 32):
                        if w + 1 < 32 * g + 32:
                            turn(w + 1)
                        score(w)
                    pe.wait_ge(ex, g + 1)
                    pe.transpose(pN[0:DT, 128:256], s[:, PAST:PAST + DT], m["ident"][:, :]).then_inc(tr, 1)
                    for b in range(4):
                        pe.wait_ge(vg[b], 64 * (g + 1))
                    if g:
                        pe.wait_ge(ok, 1)

                    def turn_p(t):
                        k = 40 * g + 32 + t
                        pe.wait_ge(kk, k - 1)
                        for j in range(4):
                            n = 4 * t + j
                            i = pe.transpose(pK[:, k % 2, j * P:(j + 1) * P], s[:, n * P:(n + 1) * P], m["ident"][:, :])
                        i.then_inc(tr, 1)

                    def values(t):
                        k = 40 * g + 32 + t
                        pe.wait_ge(kk, k + 1)
                        for b in range(4):
                            for j in range(4):
                                n = 4 * t + j
                                h, l = n // 16, n % 16
                                
                                i = pe.matmul(pO[32 * b:32 * b + 32, 0:P], pT[:, k % 2, j * P + 32 * b:j * P + 32 * b + 32],
                                              V[:, b, h, :, l * HD:(l + 1) * HD], start=(n == 0), stop=False)
                        i.then_inc(tk, 1)

                    turn_p(0)
                    for t in range(8):
                        if t + 1 < 8:
                            turn_p(t + 1)
                        values(t)
                    pe.wait_ge(snk, g + 1)
                    for b in range(4):
                        i = pe.matmul(pO[32 * b:32 * b + 32, 0:P], pn[0:DT, 32 * b:32 * b + 32], VN[:, 4 * g + b, :], start=False, stop=True)
                    i.then_inc(od, 1)
                pe.wait_ge(ok, 2)
                for g in range(2):
                    i = pe.transpose(pF[:, g, 0:P], osum[:, g, :], m["ident"][:, :])
                i.then_inc(ft, 1)

            @block.scalar
            def _(act):
                for g in range(2):
                    for u in range(8 * g, 8 * g + 8):
                        act.wait_ge(kg[u % NKS], 32 * (u // NKS + 1))
                        if u >= 2:
                            act.wait_ge(kt, 4 * (u - 1))
                        nc.scalar.activation(KR[:, u % 2].rearrange("p l (g d) -> p g l d", g=GRP),
                                             K[:, u % NKS].rearrange("p g (l d) -> p g l d", l=16), ACT.Copy).then_inc(kr, 1)
                    act.wait_ge(mx, g + 1)
                    nc.scalar.activation(s[:, :], s[:, :], ACT.Exp, bias=st[:, g, 0:1], accum_out=st[:, g, 1:2]).then_inc(ex, 1)

            @block.vector
            def _(dve):
                c = Chain(dve, ch)
                dve.wait_ge(loaded, 64)

                def keep(k, last_read):
                    last_read()
                    dve.tensor_copy(KT[:, k % 2, :], pK[:, k % 2, :]).then_inc(kk, 1)

                def score(w):
                    b = w // 8
                    r = slice(32 * (b % 4), 32 * (b % 4) + 32)
                    dve.wait_ge(sc, w + 1)
                    if w % 8 == 0 and w >= 32:
                        dve.wait_ge(tr, 9 * (w // 32))
                    dve.scalar_tensor_tensor(s[r, (w % 8) * 512:(w % 8 + 1) * 512], rel[r, (w % 8) * 512:(w % 8 + 1) * 512],
                                             m["slope"][r, :], pS[r, w % 2, :], ALU.mult, ALU.add).then_inc(sx, 1)

                for g in range(2):
                    for w in range(32 * g, 32 * g + 32):
                        dve.wait_ge(kt, w + 1)
                        k = w + 8 * g

                        def free():
                            if w - 32 * g >= 2:
                                dve.wait_ge(sc, w - 1)
                            elif g:
                                dve.wait_ge(tk, 7 + (w - 32 * g))
                        keep(k, free)
                        if w > 32 * g:
                            score(w - 1)
                    score(32 * g + 31)
                    dve.wait_ge(scn, g + 1)
                    dve.wait_ge(sx, 32 * g + 32)
                    c(dve.tensor_tensor(s[:, PAST:PAST + DT], pN[:, 0:DT], nbias[:, :], ALU.add))
                    c(dve.tensor_scalar(s[:, PAST:PAST + DT], s[:, PAST:PAST + DT], selb[:, g, NBLK - 1:NBLK], None, ALU.add))
                    for h in range(2):
                        v = s[:, h * 2048:(h + 1) * 2048].rearrange("p (l j i) -> p l j i", l=16, i=4)
                        sel = selb[:, g, 32 * h:32 * h + 32].unsqueeze(1).unsqueeze(3).to_broadcast([P, 16, 32, 4])
                        c(dve.tensor_tensor(v, v, sel, ALU.add))
                    dve.tensor_reduce(st[:, g, 0:1], s[:, :], AX, ALU.max, negate=True).then_inc(mx, 1)
                    dve.wait_ge(tr, 9 * g + 1)
                    if g:
                        dve.wait_ge(od, g)
                    dve.tensor_copy(pn[:, :], pN[0:DT, 128:256]).then_inc(snk, 1)
                    for t in range(8):
                        dve.wait_ge(tr, 9 * g + 2 + t)

                        def free():
                            if t >= 2:
                                dve.wait_ge(tk, 8 * g + t - 1)
                            else:
                                dve.wait_ge(sc, 32 * g + 31 + t)
                        keep(40 * g + 32 + t, free)
                    c(dve.reciprocal(st[:, g, 1:2], st[:, g, 1:2]))
                    c(dve.tensor_tensor(st[:, g, 2:3], st[:, g, 1:2], gd[:, g, 1:2], ALU.mult))
                    dve.wait_ge(od, g + 1)
                    dve.scalar_tensor_tensor(osum[:, g, :], pO[:, 0:P], st[:, g, 2:3], osum[:, g, :], ALU.mult, ALU.add).then_inc(ok, 1)
                dve.wait_ge(ft, 1)
                for f in range(2):
                    for g in range(GRP):
                        for n in range(HPG):
                            r = slice((n % 2) * HD, (n % 2) * HD + HD)
                            src = pF[g * HD:(g + 1) * HD, f, 0:P].rearrange("p (b g q n) -> p g n b q", b=4, g=2, q=DT)[:, g, n]
                            dst = m["oaT"][r, 2 * g + n // 2, SEQ + 16 * f:SEQ + 16 * f + 16].rearrange("p (b q) -> p b q", q=DT)
                            dve.tensor_copy(dst, src)


SOFTMAX_AFTER = [(2, 3), (5, 3), (9, 3)]


def sample_dilated(nc, a, m):
    NK = 129
    NW = 2
    loads = [("w_in", c, t) for c, _, t in GROUPS if t >= TILE0["gm"]]
    loads += [("w_ada", t * P, t) for t in range(2 * KD, MODT, 4)]
    n_gate = sum(l[0] == "w_in" for l in loads)
    with ExitStack() as ctx:
        sem, sb, ps = (f(nc, ctx, "sdi") for f in (sem_maker, sb_maker, ps_maker))
        kv = [sb(f"kv{i}", [P, NK, HD]) for i in range(3)]
        qf = sb("qf", [P, 6, NS])
        qt = sb("qt", [NS, 768])
        q = sb("q", [P, 3, HD])
        bias = sb("bias", [P, 3, NK])
        s = sb("s", [P, 3, NK])
        st = sb("st", [P, 4, 3])
        tot = sb("tot", [P, 2])
        o = sb("o", [P, 3, HD])
        oo = sb("oo", [P, HD])
        pq = ps("pq", [P, 2, 512])
        pf = ps("pf", [P, 512])
        fl, qtr, qk, qst, loaded, sx, ex, ch, fin, ft = (sem(n) for n in (
            "fl", "qtr", "qk", "qst", "loaded", "sx", "ex", "ch", "fin", "ft"))
        kvl = [sem(f"kvl{n}") for n in range(6)]
        kvused = sem("kvused")
        w = sb("w", [P, NW, KD, 512])
        go = sb("go", [P, 2, NT])
        acc = ps("acc", [P, 2, 2, 512])
        wl = [sem(f"w{i}") for i in range(NW)]
        gdone, gevac, mdone, mevac = (sem(n) for n in ("gdone", "gevac", "mdone", "mevac"))
        gst = [sem(f"gst{i}") for i in range(2)]

        NROW = [32, 20, 20]

        def rows(sp, g, v, buf, done):
            cache, (win, dil) = a[f"cache_dil{g}"][0], DIL[g]
            c = TM_COL["kc" if v == 0 else "vc"] + 256 * g
            new = a["TM"][SEQ:NT, c:c + 256].rearrange("(b i) (h d) -> h b i d", i=DT, h=4)
            for h in range(4):
                if g > 0:
                    own = a["TM"][SEQ:NT, c + h * HD:c + (h + 1) * HD]
                    sp.dma_start(buf[NS * h:NS * (h + 1), NK - 1, :], own).then_inc(done, 16)
                for t in range(DT):
                    dst = buf[NS * h + t:NS * (h + 1):DT]
                    if g == 0:
                        sp.dma_start(dst[:, 0:win - t, :], cache[:, v, h, t:win, :]).then_inc(done, 16)
                        sp.dma_start(dst[:, win - t:NK, :], new[h, :, 0:t + 1, :]).then_inc(done, 16)
                    else:
                        src = cache[:, v, h].rearrange("b (i r) d -> b r i d", r=dil)[:, t]
                        sp.dma_start(dst[:, 0:NK - 1, :], src).then_inc(done, 16)

        with nc.Block() as block:

            @block.sync
            def _(sp):
                t = TILE0["qc"] * P
                sp.dma_start(qf[:, :, :], a["PT"][t:t + 768, SEQ:NT].rearrange("(n p) t -> p n t", p=P)).then_inc(fl, 16)
                sp.dma_start(bias[:, :, :], a["c_dbias"]).then_inc(loaded, 16)
                rows(sp, 0, 0, kv[0], kvl[0])
                sp.wait_ge(qk, 2)
                sp.dma_start(a["QC"], qt[:, :]).then_inc(qst, 16)
                sp.wait_ge(qst, 16)
                for h in range(4):
                    sp.dma_start(q[NS * h:NS * (h + 1), :, :],
                                 a["QC"].rearrange("q (g h d) -> q g h d", g=3, h=4)[:, :, h, :]).then_inc(loaded, 16)
                for n in (2, 4):
                    if n >= 3:
                        sp.wait_ge(kvused, n - 2)
                    rows(sp, n // 2, 0, kv[n % 3], kvl[n])

            @block.gpsimd
            def _(pool):
                for n in (1, 3, 5):
                    if n >= 3:
                        pool.wait_ge(kvused, n - 2)
                    rows(pool, n // 2, 1, kv[n % 3], kvl[n])

            @block.scalar
            def _(act):
                def load(l):
                    src, col, _ = loads[l]
                    act.dma_start(w[:, l % NW, :, :], a[src][0].rearrange("(k p) n -> p k n", p=P)[:, :, col:col + 512]).then_inc(wl[l % NW], 16)

                def softmax(g):
                    act.wait_ge(sx, g + 1)
                    nc.scalar.activation(s[:, g, :], s[:, g, :], ACT.Exp, bias=st[:, 0, g:g + 1], accum_out=st[:, 1, g:g + 1]).then_inc(ex, 1)

                for l in range(NW):
                    load(l)
                at = SOFTMAX_AFTER
                for l, (src, _, t0) in enumerate(loads):
                    for j in range(4):
                        if src == "w_in":
                            n = 4 * l + j
                            act.wait_ge(gdone, n + 1)
                            if n >= 2:
                                act.wait_ge(gst[n % 2], 16 * (n // 2))
                            nc.scalar.activation(halves(go[:, n % 2]), acc[:, n % 2, :, 0:HN], ACT.Copy).then_inc(gevac, 1)
                            act.wait_ge(gevac, n + 1)
                            t = t0 + j
                            act.dma_start(a["PT"][t * P:(t + 1) * P, :], go[:, n % 2]).then_inc(gst[n % 2], 16)
                        if (l, j) in at:
                            softmax(at.index((l, j)))
                    if src == "w_ada":
                        n = l - n_gate
                        act.wait_ge(mdone, n + 1)
                        nc.scalar.activation(m["modT"][:, t0:t0 + 4, :], acc[:, n % 2, 0, 0:36].rearrange("p (j c) -> p j c", j=4), ACT.Copy).then_inc(mevac, 1)
                    if l + NW < len(loads):
                        load(l + NW)
                act.wait_ge(sx, 4)
                nc.scalar.activation(st[:, 3, :], st[:, 0, :], ACT.Exp, scale=-1.0, bias=tot[:, 0:1]).then_inc(ex, 1)
                for i in range(2):
                    act.wait_ge(gst[i], 16 * (4 * n_gate // 2))

            @block.tensor
            def _(pe):
                pe.wait_ge(fl, 16)
                for n in range(6):
                    i = pe.transpose(pq[0:NS, n // 4, (n % 4) * P:(n % 4 + 1) * P], qf[:, n, :], m["ident"][:, :])
                i.then_inc(qtr, 1)
                for l, (src, _, _) in enumerate(loads):
                    pe.wait_ge(wl[l % NW], 16 * (l // NW + 1))
                    for j in range(4):
                        if src == "w_in":
                            n = 4 * l + j
                            if n >= 2:
                                pe.wait_ge(gevac, n - 1)
                            for k in range(KD):
                                for h in range(2):
                                    i = pe.matmul(acc[:, n % 2, h, 0:HN], w[:, l % NW, k, j * P:(j + 1) * P],
                                                  m["hT"][:, k, h * HN:(h + 1) * HN], start=(k == 0), stop=(k == KD - 1))
                            i.then_inc(gdone, 1)
                        else:
                            n = l - n_gate
                            if j == 0 and n < 2:
                                pe.wait_ge(gevac, 4 * n_gate)
                            elif j == 0:
                                pe.wait_ge(mevac, n - 1)
                            for k in range(KD):
                                i = pe.matmul(acc[:, n % 2, 0, j * 9:j * 9 + 9], w[:, l % NW, k, j * P:(j + 1) * P],
                                              m["cT"][:, k, :], start=(k == 0), stop=(k == KD - 1))
                    if src == "w_ada":
                        i.then_inc(mdone, 1)
                pe.wait_ge(fin, 1)
                pe.transpose(pf[0:HD, 0:P], oo[:, :], m["ident"][:, :]).then_inc(ft, 1)

            @block.vector
            def _(dve):
                c = Chain(dve, ch)
                dve.wait_ge(qtr, 1)
                dve.tensor_scalar(qt[:, 0:512], pq[0:NS, 0, :], HD ** -0.5, None, ALU.mult).then_inc(qk, 1)
                dve.tensor_scalar(qt[:, 512:768], pq[0:NS, 1, 0:256], HD ** -0.5, None, ALU.mult).then_inc(qk, 1)
                dve.wait_ge(loaded, 16 * 5)
                for g in range(3):
                    K, V = kv[2 * g % 3], kv[(2 * g + 1) % 3]
                    dve.wait_ge(kvl[2 * g], 16 * NROW[g])
                    c(dve.tensor_tensor(K[:, :, :], K[:, :, :], q[:, g, :].unsqueeze(1).to_broadcast([P, NK, HD]), ALU.mult))
                    c(dve.tensor_reduce(s[:, g, :], K[:, :, :], AX, ALU.add))
                    dve.sem_inc(kvused, 1)
                    c(dve.tensor_tensor(s[:, g, :], s[:, g, :], bias[:, g, :], ALU.add))
                    dve.tensor_reduce(st[:, 0, g:g + 1], s[:, g, :], AX, ALU.max, negate=True).then_inc(sx, 1)
                    dve.wait_ge(ex, g + 1)
                    dve.wait_ge(kvl[2 * g + 1], 16 * NROW[g])
                    t3 = V[:, :, :].rearrange("p n d -> p d n")
                    c(dve.tensor_tensor(t3, t3, s[:, g, :].unsqueeze(1).to_broadcast([P, HD, NK]), ALU.mult))
                    c(dve.tensor_reduce(o[:, g, :], t3, AX, ALU.add))
                    dve.sem_inc(kvused, 1)
                dve.tensor_reduce(tot[:, 0:1], st[:, 0, :], AX, ALU.min).then_inc(sx, 1)
                dve.wait_ge(ex, 4)
                c(dve.tensor_tensor(st[:, 1, :], st[:, 1, :], st[:, 3, :], ALU.mult))
                c(dve.tensor_reduce(tot[:, 1:2], st[:, 1, :], AX, ALU.add))
                c(dve.reciprocal(tot[:, 1:2], tot[:, 1:2]))
                c(dve.tensor_scalar(st[:, 2, :], st[:, 3, :], tot[:, 1:2], None, ALU.mult))
                c(dve.tensor_scalar(oo[:, :], o[:, 0, :], st[:, 2, 0:1], None, ALU.mult))
                c(dve.scalar_tensor_tensor(oo[:, :], o[:, 1, :], st[:, 2, 1:2], oo[:, :], ALU.mult, ALU.add))
                dve.scalar_tensor_tensor(oo[:, :], o[:, 2, :], st[:, 2, 2:3], oo[:, :], ALU.mult, ALU.add).then_inc(fin, 1)
                dve.wait_ge(ft, 1)
                for h in range(4):
                    r = slice((h % 2) * HD, (h % 2) * HD + HD)
                    dve.tensor_copy(m["ocT"][r, h // 2, SEQ:NT], pf[0:HD, NS * h:NS * (h + 1)])
                dve.wait_ge(mevac, len(loads) - n_gate)
                mod = m["modT"][:, 2 * KD:MODT, :]
                c(dve.tensor_tensor(mod, mod, m["prm"][:, PROW["b_ada"] + 2 * KD:PROW["b_ada"] + MODT]
                                    .unsqueeze(2).to_broadcast([P, MODT - 2 * KD, 1 + DB]), ALU.add))
                c(dve.tensor_scalar(m["modT"][:, 4 * KD:5 * KD, :], m["modT"][:, 4 * KD:5 * KD, :], 1.0, None, ALU.add))


def build(nc, a):
    with ExitStack() as ctx:
        def sb(name, shape, dt=F32):
            return ctx.enter_context(nc.sbuf_tensor(name, shape, dt))

        m = {
            "ident": sb("ident", [P, P]), "headones": sb("headones", [P, P]),
            "reset": sb("reset", [P, SEQ]), "prm": sb("prm", [P, NPROW]), "gateP": sb("gateP", [P, 4, 24]),

            "cT": sb("cT", [P, KD, 1 + DB]),
            "xT": sb("xT", [P, KD, NT]), "modT": sb("modT", [P, MODT, 1 + DB]),
        }
        for name in ("copied", "shift_rows_out", "token_rows_out", "sample_state_out", "prompt_state_out", "y_out0", "y_out1"):
            m[name] = ctx.enter_context(nc.semaphore(name))
        with ExitStack() as mixer:
            for name, chunks in (("hT", KD), ("oaT", 4), ("obT", 4), ("ocT", 2)):
                m[name] = mixer.enter_context(nc.sbuf_tensor(name, [P, chunks, NT], F32))
            for phase in BEFORE_NSA:
                phase(nc, a, m)
            with ExitStack() as nsa:
                m["kcT"] = nsa.enter_context(nc.sbuf_tensor("kcT", [P, DB + 1, 256], F32))
                m["vc"] = nsa.enter_context(nc.sbuf_tensor("vc", [P, DB + 1, 2, P], F32))
                m["idx"] = nsa.enter_context(nc.sbuf_tensor("idx", [P, 4, 2 * DB], I32))
                for phase in NSA:
                    phase(nc, a, m)
            merge(nc, a, m)
        feed_forward(nc, a, m)
        finish(nc, m)


def finish(nc, m):
    with nc.Block() as block:

        @block.sync
        def _(sp):
            sp.wait_ge(m["copied"], 16 * 4)


BEFORE_NSA = [conditioning, in_projection, token_major, sample_dilated, rwkv]
NSA = [compress, prompt_attention, sample_nsa]


def constants():
    c = {}
    c["ident"] = np.eye(P, dtype=np.float32)
    c["headones"] = np.kron(np.eye(2), np.ones((HD, HD))).astype(np.float32)
    c["reset"] = np.tile((np.arange(SEQ) % CH != 0).astype(np.float32), (P, 1))
    s, t = np.arange(P)[:, None], np.arange(P)[None, :]
    mk = [((s // (2 * n) == t // (2 * n)) & (s // n % 2 == 0) & (t // n % 2 == 1)) for n in (1, 2, 4, 8, 16, 32)]
    mk += [(s // CH == t // CH) & (s < t), (s // CH == t // CH) & (s <= t), mk[0].T]
    c["masks"] = np.stack(mk).astype(np.float32)
    c["lane"] = (np.arange(P, dtype=np.int32) % 8).reshape(P, 1)
    rel = np.arange(P)[:, None] - np.arange(SEQ)[None, :] + SEQ - P
    ok = [rel >= 0] + [(rel >= 0) & (rel <= w) & (rel % d == 0) for w, d in DIL]
    c["dist"] = np.stack([np.where(o, rel, BIG) for o in ok]).astype(np.float32)
    rel = np.arange(SEQ).reshape(4, P, 1) - (16 * np.arange(32) + 31)
    c["distc"] = np.where(rel >= 0, rel, BIG).astype(np.float32)
    r = np.arange(P)
    q, slope = r // 4 % 4, np.array(slopes(8))[r // 16 % 2 * 4 + r % 4]
    c["slope"] = slope.reshape(P, 1).astype(np.float32)
    c["cbias"] = (-slope[:, None] * (PAST + q[:, None] - 16 * np.arange(NC_S) - 31)).astype(np.float32)
    c["same"] = (r[:, None] // 4 == r[None, :] // 4).astype(np.float32)
    w, j = np.arange(2 * P)[:, None] * 16, np.arange(NBLK)[None, :] * 64
    c["ovl"] = ((w < j + 64) & (w + 31 >= j)).astype(np.float32)
    c["forced"] = np.tile(1e4 * np.isin(np.arange(NBLK), (0, NBLK - 2, NBLK - 1)), (P, 1)).astype(np.float32)
    c["tri"] = np.tril(np.ones((NBLK, NBLK)), -1).astype(np.float32)
    x = np.concatenate([(4 * np.arange(P)[None, :] + np.arange(4)[:, None]).ravel(), 512 + np.arange(DT)])
    rel = 512 + q[:, None] - x[None, :]
    c["wbias"] = np.where((rel >= 0) & (rel <= 512), -slope[:, None] * rel, -BIG).astype(np.float32)
    tok = 2048 * np.arange(2)[:, None, None] + 16 * np.arange(P)[None, None, :] + np.arange(16)[None, :, None]
    c["rel"] = (tok.ravel() - PAST).astype(np.float32)
    d = q[:, None] - np.arange(DT)
    c["nbias"] = np.where(d >= 0, slope[:, None] * np.arange(DT), -BIG).astype(np.float32)
    h = r // NS
    c["dbias"] = np.stack([-np.array(slopes(12))[4 * g + h][:, None] * d * (128 - np.arange(129))
                           for g, (_, d) in enumerate(DIL)], 1).astype(np.float32)
    return c


_INS = ["x_prompt", "x_sample", "cache_nsa_cmp", "cache_nsa_slc", "cache_nsa_win", "state_rwkv",
        "state_rwkv_shift", "cache_dil0", "cache_dil1", "cache_dil2", "page_table", "c_prompt", "c_sample",
        "w_ada", "b_ada", "w_in", "phi_w1", "phi_pe", "phi_w2", "rw_mu", "rw_w0", "rw_w2", "rw_a0", "rw_a2",
        "rw_g2", "rw_kk", "rw_ka", "rw_rk", "rw_gn_g", "rw_gn_b", "w_br_a", "w_br_b", "w_br_c", "w_o",
        "ln1_g", "ln1_b", "ln2_g", "ln2_b", "w_ffn1", "w_ffn2"]
_OUTS = [((1, 512, 1024), "y_p"), ((8, 4, 1024), "y_s"),
         ((1, 1, 2, 2, 512, 64), "cmp_p"), ((1, 8, 2, 2, 4, 64), "cmp_s"),
         ((1, 1, 2, 2, 512, 64), "slc_p"), ((1, 8, 2, 2, 4, 64), "slc_s"),
         ((1, 1, 2, 2, 512, 64), "win_p"), ((1, 8, 2, 2, 512, 64), "win_s"),
         ((1, 1, 8, 64, 64), "rwkv_p"), ((1, 8, 8, 64, 64), "rwkv_s"),
         ((1, 1, 1, 1792), "shift_p"), ((1, 8, 1, 1792), "shift_s"),
         ((1, 1, 2, 4, 128, 64), "dil0_p"), ((1, 8, 2, 4, 128, 64), "dil0_s"),
         ((1, 1, 2, 4, 512, 64), "dil1_p"), ((1, 8, 2, 4, 512, 64), "dil1_s"),
         ((1, 1, 2, 4, 512, 64), "dil2_p"), ((1, 8, 2, 4, 2048, 64), "dil2_s")]
_SCRATCH = [("PT", (NTILE * P, NT)), ("TM", (NT, TM_W)), ("GA", (NT, 24)), ("PBS", (33, SHIFT_W)),
            ("DQ", (NS, 6, 512)), ("OD", (NS, 512)), ("QC", (NS, 768))]


def kernel(**inputs):
    import concourse.bacc as _bacc
    from concourse.bass_utils import run_bass_kernel_spmd as _run

    nc = _bacc.Bacc("TRN2", target_bir_lowering=False, num_devices=1)
    arrays, args = {}, {}
    named = {n: np.ascontiguousarray(inputs[n]) for n in _INS}
    named["page_lanes"] = np.ascontiguousarray(np.repeat(named.pop("page_table").reshape(2 * DB, NPAGE // 2).T, 8, axis=0))
    named.update({f"c_{n}": v for n, v in constants().items()})
    for name, v in named.items():
        arrays[f"in_{name}_dram"] = v
        args[name] = nc.dram_tensor(f"in_{name}_dram", v.shape, mybir.dt.from_np(v.dtype), kind="ExternalInput").ap()
    for i, (shape, name) in enumerate(_OUTS):
        args["o_" + name] = nc.dram_tensor(f"out_{i}_dram", shape, F32, kind="ExternalOutput").ap()
    for name, shape in _SCRATCH:
        args[name] = nc.dram_tensor(name, shape, F32).ap()
    build(nc, args)
    r = _run(nc, [arrays], core_ids=[0])
    return tuple(r.results[0][f"out_{i}_dram"] for i in range(len(_OUTS)))
```
